# Optimizing a Trainium2 kernel written in Bass

```python
import jax, jax.numpy as jnp
from jax import lax
import numpy as np

D_MODEL = 1024
BATCH = 1
SEQ = 512
DEPTH = 1

CONV_W = D_MODEL // 2
N_HEADS = 8
HEAD_DIM = (D_MODEL - CONV_W) // N_HEADS
ATTN_W = N_HEADS * HEAD_DIM
IN_COLS = 3 * CONV_W + 3 * ATTN_W
CONV_K = 3
D_FF = 2816
PLE_DIM = 256
DILATED_PAIRS = ((128, 1), (512, 4), (2048, 16))
BLOCK = 128
EPS = 1e-6


def rmsnorm(a, g):
    af = a.astype(jnp.float32)
    af = af * lax.rsqrt(jnp.mean(af * af, axis=-1, keepdims=True) + EPS)
    return (af * g.astype(jnp.float32)).astype(a.dtype)

def causal_dwconv3(u, w, b):
    up = jnp.pad(u, ((0, 0), (CONV_K - 1, 0), (0, 0)))
    t = u.shape[1]
    return up[:, 0:t] * w[0] + up[:, 1:t + 1] * w[1] + up[:, 2:t + 2] * w[2] + b

def alibi_slopes(n):
    return jnp.exp2(-8.0 * jnp.arange(1, n + 1, dtype=jnp.float32) / n)

def dilated_branch(q, k, v, slopes, window, dilation):
    b, t, h, hd = q.shape
    steps = window // dilation
    L = t // dilation
    nb = -(-L // BLOCK)
    lp = nb * BLOCK

    def to_blocks(a):
        a = a.reshape(b, L, dilation, h, hd).transpose(0, 2, 3, 1, 4)
        a = jnp.pad(a, ((0, 0), (0, 0), (0, 0), (0, lp - L), (0, 0)))
        return a.reshape(b, dilation, h, nb, BLOCK, hd)

    def with_prev(a):
        prev = jnp.pad(a[:, :, :, :-1], ((0, 0), (0, 0), (0, 0), (1, 0), (0, 0), (0, 0)))
        return jnp.concatenate([prev, a], axis=4)

    qb = to_blocks(q)
    kk = with_prev(to_blocks(k))
    vv = with_prev(to_blocks(v))

    s = jnp.einsum('brhnqd,brhnkd->brhnqk', qb, kk) * (hd ** -0.5)
    qi = jnp.arange(BLOCK)[:, None] + BLOCK
    kj = jnp.arange(2 * BLOCK)[None, :]
    step = qi - kj
    band = (step >= 0) & (step <= steps)
    first = (jnp.arange(nb)[:, None, None] == 0) & (kj < BLOCK)[None]
    mask = band[None] & ~first
    dist = (step * dilation).astype(jnp.float32)
    bias = -slopes[:, None, None] * dist[None]
    s = jnp.where(mask, s + bias[:, None], -jnp.inf)
    m = jnp.max(s, axis=-1, keepdims=True)
    e = jnp.exp(s - m)
    den = jnp.sum(e, axis=-1, keepdims=True)
    o = jnp.einsum('brhnqk,brhnkd->brhnqd', e, vv) / den
    lse = (m + jnp.log(den))[..., 0]

    o = o.reshape(b, dilation, h, lp, hd)[:, :, :, :L]
    o = o.transpose(0, 3, 1, 2, 4).reshape(b, t, h, hd)
    lse = lse.reshape(b, dilation, h, lp)[:, :, :, :L]
    lse = lse.transpose(0, 3, 1, 2).reshape(b, t, h)
    return o, lse

def dilated_attention(q, k, v):
    slopes = alibi_slopes(q.shape[2])
    outs, lses = [], []
    for window, dilation in DILATED_PAIRS:
        o, lse = dilated_branch(q, k, v, slopes, window, dilation)
        outs.append(o)
        lses.append(lse)
    wts = jax.nn.softmax(jnp.stack(lses, axis=0), axis=0)
    o = jnp.sum(wts[..., None] * jnp.stack(outs, axis=0), axis=0)
    return o

def first_inputs(seed: int = 0) -> dict:
    key = jax.random.key(seed)
    ks = jax.random.split(key, 24)
    f32 = jnp.float32

    def nrm(k, shape, fan):
        return jax.random.normal(k, shape, f32) * (fan ** -0.5)

    def gain(k, shape):
        return 1.0 + 0.05 * jax.random.normal(k, shape, f32)

    def bias(k, shape):
        return 0.01 * jax.random.normal(k, shape, f32)

    return {
        'x': jax.random.normal(ks[0], (BATCH, SEQ, D_MODEL), f32),
        'p': jax.random.normal(ks[1], (DEPTH, BATCH, SEQ, PLE_DIM), f32),
        'g_mix': gain(ks[2], (DEPTH, D_MODEL)),
        'w_in': nrm(ks[3], (DEPTH, D_MODEL, IN_COLS), D_MODEL),
        'conv_w': nrm(ks[4], (DEPTH, CONV_K, CONV_W), CONV_K),
        'conv_b': bias(ks[5], (DEPTH, CONV_W)),
        'q_norm_g': gain(ks[6], (DEPTH, HEAD_DIM)),
        'k_norm_g': gain(ks[7], (DEPTH, HEAD_DIM)),
        'g_out_conv': gain(ks[8], (DEPTH, CONV_W)),
        'g_out_attn': gain(ks[9], (DEPTH, ATTN_W)),
        'w_out': nrm(ks[10], (DEPTH, CONV_W + ATTN_W, D_MODEL), CONV_W + ATTN_W),
        'g_ffn': gain(ks[11], (DEPTH, D_MODEL)),
        'w_gate': nrm(ks[12], (DEPTH, D_MODEL, D_FF), D_MODEL),
        'w_up': nrm(ks[13], (DEPTH, D_MODEL, D_FF), D_MODEL),
        'ffn_conv_w': nrm(ks[14], (DEPTH, CONV_K, D_FF), CONV_K),
        'ffn_conv_b': bias(ks[15], (DEPTH, D_FF)),
        'w_down': nrm(ks[16], (DEPTH, D_FF, D_MODEL), D_FF),
        'g_ple': gain(ks[17], (DEPTH, D_MODEL)),
        'w_ple_gate': nrm(ks[18], (DEPTH, D_MODEL, D_MODEL), D_MODEL),
        'w_ple_proj': nrm(ks[19], (DEPTH, PLE_DIM, D_MODEL), PLE_DIM),
    }

def first_block(x, p, g_mix, w_in, conv_w, conv_b, q_norm_g, k_norm_g, g_out_conv,
              g_out_attn, w_out, g_ffn, w_gate, w_up, ffn_conv_w, ffn_conv_b, w_down,
              g_ple, w_ple_gate, w_ple_proj):
    b, t, _ = x.shape
    for i in range(DEPTH):
        h = rmsnorm(x, g_mix[i])
        z = h @ w_in[i]
        zb, zc, zx, zq, zk, zv = jnp.split(
            z, np.cumsum([CONV_W, CONV_W, CONV_W, ATTN_W, ATTN_W]), axis=-1)
        y_c = zb * causal_dwconv3(zc * zx, conv_w[i], conv_b[i])
        q = rmsnorm(zq.reshape(b, t, N_HEADS, HEAD_DIM), q_norm_g[i]).astype(jnp.float32)
        k = rmsnorm(zk.reshape(b, t, N_HEADS, HEAD_DIM), k_norm_g[i]).astype(jnp.float32)
        v = zv.reshape(b, t, N_HEADS, HEAD_DIM).astype(jnp.float32)
        y_a = dilated_attention(q, k, v).reshape(b, t, ATTN_W).astype(x.dtype)
        y = jnp.concatenate([rmsnorm(y_c, g_out_conv[i]), rmsnorm(y_a, g_out_attn[i])], axis=-1)
        x = x + y @ w_out[i]
        h = rmsnorm(x, g_ffn[i])
        gate = causal_dwconv3(h @ w_gate[i], ffn_conv_w[i], ffn_conv_b[i])
        x = x + (jax.nn.silu(gate) * (h @ w_up[i])) @ w_down[i]
        ple_gate = jax.nn.sigmoid(rmsnorm(x, g_ple[i]) @ w_ple_gate[i])
        x = x + ple_gate * (p[i].astype(x.dtype) @ w_ple_proj[i])
    return x


MIX_WIDTH = D_MODEL
A_HEADS = 4
A_DV = MIX_WIDTH // 2 // A_HEADS
A_DK = A_DV // 2
B_HEADS = 4
B_DV = MIX_WIDTH // 2 // B_HEADS
B_DK = B_DV // 2
A_QK = A_HEADS * A_DK
A_V = A_HEADS * A_DV
B_QK = B_HEADS * B_DK
B_V = B_HEADS * B_DV
GLA_RANK = 16
GLA_GATE_TEMP = 16.0
CONV_W_2 = 3
CHUNK = 64
IN_WIDTHS = (2 * A_QK, A_V, A_V, 4 * A_HEADS, B_QK, B_QK, B_V, B_V, 2 * GLA_RANK)
IN_COLS_2 = 2 * A_QK + A_V + A_V + 4 * A_HEADS + B_QK + B_QK + B_V + B_V + 2 * GLA_RANK


def rms_norm(x, g):
    xf = x.astype(jnp.float32)
    y = xf * lax.rsqrt(jnp.mean(xf * xf, axis=-1, keepdims=True) + EPS)
    return (y * g.astype(jnp.float32)).astype(x.dtype)

def head_rms_norm(y, g):
    y = y * lax.rsqrt(jnp.mean(y * y, axis=-1, keepdims=True) + EPS)
    return y * g.astype(jnp.float32)

def dwconv3(x, w, b):
    xp = jnp.pad(x, ((0, 0), (1, 1), (0, 0)))
    return xp[:, :-2] * w[0] + xp[:, 1:-1] * w[1] + xp[:, 2:] * w[2] + b

def flip(t):
    return t[:, ::-1]

def to_chunks(t):
    b, s, h = t.shape[:3]
    t = t.reshape((b, s // CHUNK, CHUNK, h) + t.shape[3:])
    return jnp.moveaxis(t, (1, 3), (0, 2))

def from_chunks(y):
    y = jnp.moveaxis(y, (0, 2), (1, 3))
    b, nc, l, h, d = y.shape
    return y.reshape(b, nc * l, h, d)

def mlstm_chunkwise(q, k, v, i_pre, log_f):
    bsz, _, h, dk = q.shape
    dv = v.shape[-1]
    causal = jnp.tril(jnp.ones((CHUNK, CHUNK), dtype=bool))

    def step(carry, inp):
        c_st, n_st, m_st = carry
        q_, k_, v_, i_, f_ = inp
        b = jnp.cumsum(f_, axis=-1)
        d_intra = jnp.where(causal, b[..., :, None] - b[..., None, :] + i_[..., None, :], -jnp.inf)
        m_inter = b + m_st[..., None]
        m_t = jnp.maximum(m_inter, jnp.max(d_intra, axis=-1))
        s = jnp.einsum('bhtd,bhsd->bhts', q_, k_) * jnp.exp(d_intra - m_t[..., None])
        inter = jnp.exp(m_inter - m_t)
        num = jnp.einsum('bhts,bhse->bhte', s, v_) + inter[..., None] * jnp.einsum('bhtd,bhde->bhte', q_, c_st)
        den = jnp.sum(s, axis=-1) + inter * jnp.einsum('bhtd,bhd->bht', q_, n_st)
        h_out = num / jnp.maximum(jnp.abs(den), jnp.exp(-m_t))[..., None]
        b_last = b[..., -1]
        g = b_last[..., None] - b + i_
        m_new = jnp.maximum(b_last + m_st, jnp.max(g, axis=-1))
        decay = jnp.exp(b_last + m_st - m_new)
        wk = jnp.exp(g - m_new[..., None])[..., None] * k_
        c_new = decay[..., None, None] * c_st + jnp.einsum('bhsd,bhse->bhde', wk, v_)
        n_new = decay[..., None] * n_st + jnp.sum(wk, axis=-2)
        return (c_new, n_new, m_new), h_out

    init = (jnp.zeros((bsz, h, dk, dv), jnp.float32),
            jnp.zeros((bsz, h, dk), jnp.float32),
            jnp.zeros((bsz, h), jnp.float32))
    _, hs = lax.scan(step, init, (to_chunks(q), to_chunks(k), to_chunks(v),
                                  to_chunks(i_pre), to_chunks(log_f)))
    return from_chunks(hs)

def gla_chunkwise(q, k, v, log_a):
    bsz, _, h, dk = q.shape
    dv = v.shape[-1]
    causal = jnp.tril(jnp.ones((CHUNK, CHUNK), dtype=bool))[..., None]

    def step(s_st, inp):
        q_, k_, v_, a_ = inp
        b = jnp.cumsum(a_, axis=-2)
        diff = b[..., :, None, :] - b[..., None, :, :]
        decay = jnp.exp(jnp.where(causal, diff, -jnp.inf))
        s = jnp.einsum('bhtd,bhsd,bhtsd->bhts', q_, k_, decay)
        o = jnp.einsum('bhts,bhse->bhte', s, v_) + jnp.einsum('bhtd,bhde->bhte', q_ * jnp.exp(b), s_st)
        b_last = b[..., -1:, :]
        k_dec = k_ * jnp.exp(b_last - b)
        s_new = jnp.exp(b_last[..., 0, :])[..., None] * s_st + jnp.einsum('bhsd,bhse->bhde', k_dec, v_)
        return s_new, o

    init = jnp.zeros((bsz, h, dk, dv), jnp.float32)
    _, os_ = lax.scan(step, init, (to_chunks(q), to_chunks(k), to_chunks(v), to_chunks(log_a)))
    return from_chunks(os_)

def hybrid_mixer(hn, w_in, mlstm_gate_b, mlstm_conv_w, mlstm_conv_b, mlstm_norm,
                 gla_w2, gla_b, gla_norm, w_out):
    bsz, s, _ = hn.shape
    proj = jnp.matmul(hn, w_in).astype(jnp.float32)
    idx = np.cumsum(np.array(IN_WIDTHS))[:-1].tolist()
    a_qk, a_v, a_o, a_gates, b_q, b_k, b_v, b_r, b_lr = jnp.split(proj, idx, axis=-1)

    qk = jax.nn.silu(dwconv3(a_qk, mlstm_conv_w.astype(jnp.float32), mlstm_conv_b.astype(jnp.float32)))
    q_a = qk[..., :A_QK].reshape(bsz, s, A_HEADS, A_DK)
    k_a = qk[..., A_QK:].reshape(bsz, s, A_HEADS, A_DK) * (A_DK ** -0.5)
    v_a = a_v.reshape(bsz, s, A_HEADS, A_DV)
    gates = a_gates + mlstm_gate_b.astype(jnp.float32)
    i_fw, f_fw, i_bw, f_bw = jnp.split(gates, 4, axis=-1)
    h_fw = mlstm_chunkwise(q_a, k_a, v_a, i_fw, jax.nn.log_sigmoid(f_fw))
    h_bw = flip(mlstm_chunkwise(flip(q_a), flip(k_a), flip(v_a), flip(i_bw), flip(jax.nn.log_sigmoid(f_bw))))
    y_a = jax.nn.sigmoid(a_o) * head_rms_norm(h_fw + h_bw, mlstm_norm).reshape(bsz, s, A_V)

    q_b = b_q.reshape(bsz, s, B_HEADS, B_DK) * (B_DK ** -0.5)
    k_b = b_k.reshape(bsz, s, B_HEADS, B_DK)
    v_b = b_v.reshape(bsz, s, B_HEADS, B_DV)
    lr_fw, lr_bw = jnp.split(b_lr, 2, axis=-1)
    w2 = gla_w2.astype(jnp.float32)
    gb = gla_b.astype(jnp.float32)
    la_fw = (jax.nn.log_sigmoid(lr_fw @ w2[0] + gb[0]) / GLA_GATE_TEMP).reshape(bsz, s, B_HEADS, B_DK)
    la_bw = (jax.nn.log_sigmoid(lr_bw @ w2[1] + gb[1]) / GLA_GATE_TEMP).reshape(bsz, s, B_HEADS, B_DK)
    o_fw = gla_chunkwise(q_b, k_b, v_b, la_fw)
    o_bw = flip(gla_chunkwise(flip(q_b), flip(k_b), flip(v_b), flip(la_bw)))
    y_b = jax.nn.silu(b_r) * head_rms_norm(o_fw + o_bw, gla_norm).reshape(bsz, s, B_V)

    y = jnp.concatenate([y_a, y_b], axis=-1).astype(hn.dtype)
    return jnp.matmul(y, w_out)

def conv_ffn(hn, w_gate, w_up, conv_w, conv_b, w_down):
    g = dwconv3(jnp.matmul(hn, w_gate), conv_w, conv_b)
    u = jnp.matmul(hn, w_up)
    return jnp.matmul(jax.nn.gelu(g, approximate=True) * u, w_down)

def second_inputs(seed: int = 0) -> dict:
    key = jax.random.key(seed)
    ks = jax.random.split(key, 20)
    f32 = jnp.float32

    def nrm(k, shape, scale):
        return jax.random.normal(k, shape, f32) * scale

    def gain(k, shape):
        return 1.0 + 0.05 * jax.random.normal(k, shape, f32)

    f_base = jnp.linspace(3.0, 6.0, A_HEADS, dtype=f32)
    i_base = jnp.zeros((A_HEADS,), f32)
    gate_base = jnp.concatenate([i_base, f_base, i_base, f_base])
    return {
        "x": nrm(ks[0], (BATCH, SEQ, D_MODEL), 1.0),
        "norm_mix_pre": gain(ks[1], (DEPTH, D_MODEL)),
        "norm_mix_post": gain(ks[2], (DEPTH, D_MODEL)),
        "norm_ffn_pre": gain(ks[3], (DEPTH, D_MODEL)),
        "norm_ffn_post": gain(ks[4], (DEPTH, D_MODEL)),
        "w_in": nrm(ks[5], (DEPTH, D_MODEL, IN_COLS_2), D_MODEL ** -0.5),
        "mlstm_gate_b": gate_base + nrm(ks[6], (DEPTH, 4 * A_HEADS), 0.1),
        "mlstm_conv_w": nrm(ks[7], (DEPTH, CONV_W_2, 2 * A_QK), CONV_W_2 ** -0.5),
        "mlstm_conv_b": nrm(ks[8], (DEPTH, 2 * A_QK), 0.02),
        "mlstm_norm": gain(ks[9], (DEPTH, A_HEADS, A_DV)),
        "gla_w2": nrm(ks[10], (DEPTH, 2, GLA_RANK, B_QK), GLA_RANK ** -0.5),
        "gla_b": nrm(ks[11], (DEPTH, 2, B_QK), 0.02),
        "gla_norm": gain(ks[12], (DEPTH, B_HEADS, B_DV)),
        "w_out": nrm(ks[13], (DEPTH, MIX_WIDTH, D_MODEL), MIX_WIDTH ** -0.5),
        "ffn_w_gate": nrm(ks[14], (DEPTH, D_MODEL, D_FF), D_MODEL ** -0.5),
        "ffn_w_up": nrm(ks[15], (DEPTH, D_MODEL, D_FF), D_MODEL ** -0.5),
        "ffn_conv_w": nrm(ks[16], (DEPTH, CONV_W_2, D_FF), CONV_W_2 ** -0.5),
        "ffn_conv_b": nrm(ks[17], (DEPTH, D_FF), 0.02),
        "ffn_w_down": nrm(ks[18], (DEPTH, D_FF, D_MODEL), D_FF ** -0.5),
    }

def second_block(x, norm_mix_pre, norm_mix_post, norm_ffn_pre, norm_ffn_post, w_in,
              mlstm_gate_b, mlstm_conv_w, mlstm_conv_b, mlstm_norm, gla_w2, gla_b, gla_norm,
              w_out, ffn_w_gate, ffn_w_up, ffn_conv_w, ffn_conv_b, ffn_w_down):
    for l in range(DEPTH):
        hn = rms_norm(x, norm_mix_pre[l])
        mix = hybrid_mixer(hn, w_in[l], mlstm_gate_b[l], mlstm_conv_w[l], mlstm_conv_b[l], mlstm_norm[l],
                           gla_w2[l], gla_b[l], gla_norm[l], w_out[l])
        x = x + rms_norm(mix, norm_mix_post[l])
        hn = rms_norm(x, norm_ffn_pre[l])
        ff = conv_ffn(hn, ffn_w_gate[l], ffn_w_up[l], ffn_conv_w[l], ffn_conv_b[l], ffn_w_down[l])
        x = x + rms_norm(ff, norm_ffn_post[l])
    return x


def setup_inputs(seed=0):
    out = dict(first_inputs(seed))
    for name, value in second_inputs(seed + 1).items():
        if name != "x":
            out[name + "_2"] = value
    return out


def reference(
    x, p, g_mix, w_in, conv_w, conv_b, q_norm_g, k_norm_g, g_out_conv, g_out_attn, w_out, g_ffn,
    w_gate, w_up, ffn_conv_w, ffn_conv_b, w_down, g_ple, w_ple_gate, w_ple_proj, norm_mix_pre_2,
    norm_mix_post_2, norm_ffn_pre_2, norm_ffn_post_2, w_in_2, mlstm_gate_b_2, mlstm_conv_w_2,
    mlstm_conv_b_2, mlstm_norm_2, gla_w2_2, gla_b_2, gla_norm_2, w_out_2, ffn_w_gate_2,
    ffn_w_up_2, ffn_conv_w_2, ffn_conv_b_2, ffn_w_down_2,
):
    x = first_block(
        x, p, g_mix, w_in, conv_w, conv_b, q_norm_g, k_norm_g, g_out_conv, g_out_attn, w_out,
        g_ffn, w_gate, w_up, ffn_conv_w, ffn_conv_b, w_down, g_ple, w_ple_gate, w_ple_proj,
    )
    return second_block(
        x, norm_mix_pre_2, norm_mix_post_2, norm_ffn_pre_2, norm_ffn_post_2, w_in_2,
        mlstm_gate_b_2, mlstm_conv_w_2, mlstm_conv_b_2, mlstm_norm_2, gla_w2_2, gla_b_2,
        gla_norm_2, w_out_2, ffn_w_gate_2, ffn_w_up_2, ffn_conv_w_2, ffn_conv_b_2, ffn_w_down_2,
    )


_drawn_inputs = setup_inputs


def setup_inputs(seed=0):
    import zlib

    import numpy as np

    out = dict(_drawn_inputs(seed))
    spreads = {}
    factors = {'conv_b': 7.12,
     'ffn_conv_b': 8.0,
     'g_ple': 6.096,
     'mlstm_conv_b_2': 4.954,
     'mlstm_norm_2': 3.201,
     'gla_b_2': 34.865,
     'ffn_conv_b_2': 6.084,
     'gla_norm_2': 5.644}
    for name, (base, spread) in spreads.items():
        noise = np.random.default_rng([zlib.crc32(name.encode()), seed]).standard_normal(out[name].shape)
        drawn = base * np.exp(spread * noise) if base else spread * noise
        out[name] = __import__('jax').numpy.asarray(drawn.astype(out[name].dtype))
    for name, factor in factors.items():
        out[name] = (out[name] * factor).astype(out[name].dtype)
    return out
```

```python
from contextlib import ExitStack

import concourse.bass as bass
from concourse import mybir

F32 = mybir.dt.float32
F32R = mybir.dt.float32r
ALU = mybir.AluOpType
ACT = mybir.ActivationFunctionType

P = 128
T = 512
NT = T // P
D = 1024
DK = D // P
DFF = 2816
FC = DFF // P
CW = 512
CK = CW // P
H1 = 8
HD = 64
H2 = 4
DV = 128
UW = 8 * P
NS = 4
EPS = 1e-6
BIG = (256, 128)
SMALL = (64, 32, 16, 8, 4, 2, 1)

PCOLS = {}


def _param_columns():
    at = 0
    for name, n in (("eps", 4), ("g_mix", DK), ("g_ffn", DK), ("g_ple", DK), ("pre2", DK), ("post2", DK),
                    ("fpre2", DK), ("fpost2", DK), ("g_oc", CK), ("g_oa", CK), ("cw", 3 * CK), ("cb", CK),
                    ("qg", 1), ("kg", 1), ("mcw", 3 * 4), ("mcb", 4), ("mnorm", H2), ("gnorm", H2),
                    ("glab", H2), ("gib", 1), ("gfb", 1), ("fcw", 3 * FC), ("fcb", FC), ("fcw2", 3 * FC),
                    ("fcb2", FC)):
        PCOLS[name] = at
        at += n
    return at


NPRM = _param_columns()

class Stage:

    def __init__(self, sem, base):
        self.sem = sem
        self.base = base


UNITS = {}


def _unit_table():
    at = 0
    for name, n in (("qk", 8), ("v", 4), ("conv", 12), ("wo", 8), ("ffn", 2 * FC), ("down", 32),
                    ("pgate", 8), ("pproj", 2),
                    ("small", 1), ("bv", 4), ("kq0", 2), ("ao", 4), ("kq1", 2), ("aqk", 4), ("br", 4), ("av", 4),
                    ("wo2", 8), ("ffn2", 2 * FC), ("down2", 32)):
        UNITS[name] = (at, n)
        at += n
    return at


NU = _unit_table()
DOWN_TILES = (6, 6, 5, 5)


def tokens(j, n=1):
    return slice(j * P, (j + n) * P)


def build(nc, dram, out, stop=None):
    ctx = ExitStack()
    with ctx:
        base = [(nc.sbuf_base + 63) // 64 * 64]

        def put(name, shape, dt, at=None):
            size = 4
            for s in shape[1:]:
                size *= s
            if at is None:
                at = base[0]
                base[0] += (size + 31) // 32 * 32
            return nc.alloc_sbuf_tensor_at(name, shape, dt, offset=at)

        KB = 1024
        X = put("X", [P, DK, T], F32)
        S_at = base[0]
        SH = put("SH", [P, FC, T], F32R)
        SL = put("SL", [P, FC, T], F32R)
        A_at = base[0]
        AH = put("AH", [P, DK, T], F32R)
        AL = put("AL", [P, DK, T], F32R)
        RAW = put("RAW", [P, NS, UW], F32)
        WH = put("WH", [P, NS, UW], F32R)
        WL = put("WL", [P, NS, UW], F32R)
        TMP = put("TMP", [P, 4, T], F32)
        PAD = put("PAD", [P, 2, T + 2], F32)
        ACC = put("ACC", [P, T], F32)
        SQ = put("SQ", [P, 2, T], F32)
        RS = put("RS", [P, T], F32)
        PRM = put("PRM", [P, NPRM], F32)
        CST = put("CST", [P, 3, P], F32)
        COL = put("COL", [P, 256], F32)
        assert base[0] <= nc.sbuf_usable_end, (base[0], nc.sbuf_usable_end)
        IDENT, INVD, BONE = (CST[:, i, :] for i in range(3))

        YH = put("YH", [P, DK, T], F32R, S_at)
        YL = put("YL", [P, DK, T], F32R, S_at + 16 * KB)
        YC = put("YC", [P, CK, T], F32, S_at + 8 * KB)
        QT = put("QT", [P, CK, T], F32, S_at + 32 * KB)
        KT = put("KT", [P, CK, T], F32, S_at + 40 * KB)
        V = put("V", [P, NT, CW], F32, S_at + 48 * KB)
        BT = put("BT", [P, H1, T], F32, S_at + 56 * KB)
        YA = put("YA", [P, NT, CW], F32, S_at + 72 * KB)
        SC = put("SC", [P, 2, T], F32, S_at + 80 * KB)
        PT = put("PT", [P, 2, T], F32, S_at + 84 * KB)
        RC = COL[:, 252:256]
        MX, NM, DEN, RD = (COL[:, 32 * i:32 * i + 32] for i in range(1, 5))
        YS = COL[:, 160:164]

        SG = put("SG", [P, DK, T], F32, S_at + 32 * KB)
        PIN = put("PIN", [P, 2, T], F32, S_at + 48 * KB)
        PH = put("PH", [P, 2, T], F32R, S_at + 52 * KB)
        PL = put("PL", [P, 2, T], F32R, S_at + 56 * KB)

        GH = put("GH", [P, DK, T], F32R, S_at)
        GL = put("GL", [P, DK, T], F32R, S_at + 16 * KB)
        R = S_at + 32 * KB
        VB = put("VB", [P, NT, CW], F32, R)
        YB = put("YB", [P, NT, CW], F32, R + 8 * KB)
        AO = put("AO", [P, NT, CW], F32, R + 16 * KB)
        Q2 = put("Q2", [P, 2, T], F32, R + 24 * KB)
        K2 = put("K2", [P, 2, T], F32, R + 28 * KB)
        XG = put("XG", [P, 2, T], F32, R + 32 * KB)
        SA = put("SA", [P, 2, T], F32, R + 36 * KB)
        QB = put("QB", [P, 2, T], F32, R + 40 * KB)
        KB_ = put("KB", [P, 2, T], F32, R + 44 * KB)
        LM = put("LM", [P, 8 * P], F32, R + 48 * KB)
        AK = put("AK", [P, 2, T], F32, R + 52 * KB)
        QS = put("QS", [P, 7, T], F32, A_at)
        KS = put("KS", [P, 7, T], F32, A_at + 14 * KB)
        AQ = put("AQ", [P, 2, T], F32, A_at + 28 * KB)
        BR = put("BR", [P, NT, CW], F32, A_at)
        VA = put("VA", [P, NT, H2, DV + 1], F32, A_at + 8 * KB)
        YM = put("YM", [P, NT, CW], F32, R + 24 * KB)
        SEL = put("SEL", [P, 8 * P], F32, R + 48 * KB)
        NEG = put("NEG", [P, 2, P], F32, R + 32 * KB)
        WT = put("WT", [P, 2, 2, T], F32, R + 36 * KB)
        MIX = put("MIX", [P, DK, T], F32, S_at + 32 * KB)
        MIX2 = put("MIX2", [P, DK, T], F32, A_at)

        PS = ctx.enter_context(nc.psum_tensor("PS", [P, 8, T], F32))
        pb = [PS[:, i, :] for i in range(8)]

        def sem(name):
            return ctx.enter_context(nc.semaphore(name))

        def prm(name, i=0, rows=slice(0, P)):
            return PRM[rows, PCOLS[name] + i:PCOLS[name] + i + 1]

        def at(t, i, j=0, per=1):
            if isinstance(i, int):
                return t[:, per * i + j, :]
            return t[:, bass.ds(i * per + j, 1), :].rearrange("p o n -> p (o n)")

        def prm_at(name, off, i, per, j):
            c = PCOLS[name] + off + j
            if isinstance(i, int):
                return PRM[:, c + per * i:c + per * i + 1]
            return PRM[:, bass.ds(i * per + c, 1)]

        passed = {nc.scalar.engine: sem("s_act_passed"), nc.gpsimd.engine: sem("s_pool_passed")}

        def ge(eng, s, v, more=0):
            if isinstance(s, Stage):
                s, more = s.sem, more + s.base
            eng.wait_ge(s, v + more)

        def wait(eng, s, i, per, v):
            if not isinstance(i, int):
                ge(eng, s, i * per, v)
                if eng.engine in passed:
                    eng.sem_inc(passed[eng.engine], 1)
            elif per * i + v > 0:
                ge(eng, s, per * i + v)

        CG = COL[:, 0:128].rearrange("p (t g r) -> p t g r", t=NT, g=4)
        BSS, MSS, DN, NRM = COL[:, 128:144], COL[:, 144:160], COL[:, 164:172], COL[:, 172:204]

        MROWS = (PAD[0:8, 1, 0:T], SQ[0:8, 0, :])

        EPS_C, EPS64_C, ONE_C = prm("eps", 0), prm("eps", 1), prm("eps", 2)

        s_raw = [sem(f"s_raw{i}") for i in range(NS)]
        s_hi = sem("s_hi")
        s_split = sem("s_split")
        s_used = sem("s_used")
        s_xin = [sem(f"s_xin{i}") for i in range(4)]
        s_prm = sem("s_prm")
        s_bt = sem("s_bt")
        s_out = sem("s_out")
        s_pad = sem("s_pad")
        s_vc = sem("s_vc")
        s_ac = sem("s_ac")
        ALL = ("mix", "ffn", "ple", "mix2", "post", "ffn2", "fpost")
        SPLIT = tuple(n for n in ALL if n not in ("post", "fpost"))

        def stages(w, names, per):
            s = sem(f"s_{w}")
            return {n: Stage(s, per * i) for i, n in enumerate(names)}

        s_x = stages("x", ("ffn", "ple", "mix2", "ffn2", "fpost"), DK)
        s_gh, s_gl = stages("gh", SPLIT, DK), stages("gl", SPLIT, DK)
        s_sq, s_acc = stages("sq", ALL, DK), stages("acc", ALL, DK)
        s_ms, s_sd, s_rs = stages("ms", ALL, 1), stages("sd", ALL, 1), stages("rs", ALL, 1)
        s_z, s_zsq, s_hms, s_hsd, s_qk = (sem(f"s_{w}") for w in ("z", "zsq", "hms", "hsd", "qk"))
        s_v, s_rc, s_rcd = sem("s_v"), sem("s_rc"), sem("s_rcd")
        s_cuf, s_cx, s_c0, s_yc, s_ycsq, s_ycacc, s_ycms, s_ycsd, s_yn, s_yl = (
            sem(f"s_{w}") for w in ("cuf", "cx", "c0", "yc", "ycsq", "ycacc", "ycms", "ycsd", "yn", "yl"))
        s_s, s_sc, s_nm, s_e, s_pt, s_ptc, s_pv, s_ya, s_yss, s_yan, s_yt, s_yh = (
            sem(f"s_{w}") for w in ("s", "sc", "nm", "e", "pt", "ptc", "pv", "ya", "yss", "yan", "yt", "yh"))
        s_ynh = sem("s_ynh")
        FS = {"ffn": {}, "ffn2": {}}
        for w in ("pad", "t1", "ta", "t3", "act", "up", "h", "sh", "sl"):
            s_chunk = sem(f"s_ffn_{w}")
            FS["ffn"][w], FS["ffn2"][w] = Stage(s_chunk, 0), Stage(s_chunk, FC)
        s_pin, s_ph, s_pl, s_pgt, s_sg, s_pm, s_ppj = (
            sem(f"s_{w}") for w in ("pin", "ph", "pl", "pgt", "sg", "pm", "ppj"))
        s_mix, s_mix2, s_bcc = sem("s_mix"), sem("s_mix2"), sem("s_bcc")
        (s_sel, s_row, s_rw8, s_gabs, s_stk, s_stt, s_cols, s_dup, s_kqf, s_gpr, s_lax, s_la, s_xg, s_lm) = (
            sem(f"s_{w}") for w in ("sel", "row", "rw8", "gabs", "stk", "stt", "cols", "dup", "kqf", "gpr", "lax",
                                      "la", "xg", "lm"))
        s_vb, s_aof, s_dd, s_ee, s_lv, s_gs, s_gb, s_sad, s_sao, s_go, s_oc, s_ybq = (
            sem(f"s_{w}") for w in ("vb", "aof", "dd", "ee", "lv", "gs", "gb", "sad", "sao", "go", "oc", "ybq"))
        s_apad, s_a1, s_a3, s_aqk, s_br, s_va, s_zero = (
            sem(f"s_{w}") for w in ("apad", "a1", "a3", "aqk", "br", "va", "zero"))
        s_bc, s_ms2, s_ad, s_w, s_sw, s_mo, s_hb, s_hf, s_hst, s_gn, s_y2, s_y2t, s_y2h, s_y2l = (
            sem(f"s_{w}") for w in ("bc", "ms2", "ad", "w", "sw", "mo", "hb", "hf", "hst", "gn", "y2", "y2t",
                                      "y2h", "y2l"))

        block = ctx.enter_context(nc.Block())

        LIMIT = {"mixer1": UNITS["ffn"][0], "block1": UNITS["small"][0]}.get(stop, NU)

        def runs():
            u = 0
            while u < LIMIT:
                if u in (UNITS["down"][0], UNITS["down2"][0]):
                    yield u, 8, [t * P for t in DOWN_TILES]
                    u += 32
                    continue
                end = min(x for x in (UNITS["down"][0], UNITS["down2"][0], LIMIT) if x > u)
                if end - u >= NS:
                    n = (end - u) // NS
                    yield u, n, [UW] * NS
                    u += n * NS
                else:
                    yield u, 1, [UW] * (end - u)
                    u = end

        def each_unit(eng, step):
            for u0, iters, widths in runs():
                n = len(widths)
                first = 1 if u0 == 0 or iters == 1 else 0
                if first:
                    for j in range(n):
                        step(u0, 0, n, j, widths[j])
                    if u0 == 0 and eng.engine == nc.sync.engine:
                        eng.dma_start(BT[:], dram["bias"]).then_inc(s_bt, 16)
                if iters > first:
                    with eng.Fori(first, iters) as i:
                        for j in range(n):
                            step(u0, i, n, j, widths[j])

        @block.sync
        def _(sp):
            for k in range(0, DK, 2):
                sp.dma_start(X[:, k:k + 2, :], dram["x"][:, k:k + 2, :]).then_inc(s_xin[k // 2], 16)
                if k == 0:
                    sp.dma_start(PRM[:], dram["params"]).then_inc(s_prm, 16)
                    sp.dma_start(CST[:], dram["consts"]).then_inc(s_prm, 16)

            def load(u0, i, n, j, width):
                slot = (u0 + j) % NS
                wait(sp, s_split, i, n, u0 + j - NS + 1)
                if isinstance(i, int):
                    src = dram["w"][u0 + j + n * i, :, 0:width]
                else:
                    src = dram["w"][bass.ds(i * n + (u0 + j), 1), :, 0:width].rearrange("o p w -> p (o w)")
                sp.dma_start(RAW[:, slot, 0:width], src).then_inc(s_raw[slot], 16)

            each_unit(sp, load)
            last = {"mixer1": "ffn", "block1": "mix2"}.get(stop, "fpost")
            for k in range(DK):
                ge(sp, s_x[last], k + 1)
                sp.dma_start(out[:, k, :], X[:, k, :]).then_inc(s_out, 16)
            sp.wait_ge(s_out, 16 * DK)

        @block.gpsimd
        def _(pool):
            def split(u0, i, n, j, width):
                slot = (u0 + j) % NS
                wait(pool, s_used, i, n, u0 + j - NS + 1)
                wait(pool, s_raw[slot], i, 16 * n // NS, 16 * ((u0 + j) // NS + 1))
                nc.gpsimd.tensor_scalar(WH[:, slot, 0:width], RAW[:, slot, 0:width], 1.0, 1.0, ALU.mult, ALU.mult).then_inc(s_hi, 1)
                wait(pool, s_hi, i, n, u0 + j + 1)
                nc.gpsimd.tensor_tensor(WL[:, slot, 0:width], RAW[:, slot, 0:width],
                                        WH[:, slot, 0:width].bitcast(F32), ALU.subtract).then_inc(s_split, 1)

            each_unit(pool, split)

        @block.tensor
        def _(pe):
            def mm3(o, lh, ll, rh, rl, start, stop):
                nc.tensor.matmul(o, lh, rh, start=start, stop=False)
                nc.tensor.matmul(o, lh, rl, start=False, stop=False)
                return nc.tensor.matmul(o, ll, rh, start=False, stop=stop)

            def ready(u):
                pe.wait_ge(s_split, u + 1)

            def col_tiles(u, slots, tiles, o, hi, lo, each=None, start=True, stop=True):
                s = u % NS
                for n, k in zip(slots, tiles):
                    if each is not None:
                        ge(pe, each, k + 1)
                    c = tokens(n)
                    ins = mm3(o, WH[:, s, c], WL[:, s, c], hi[:, k, :], lo[:, k, :],
                              start and n == slots[0], stop and n == slots[-1])
                return ins

            def col_unit(u, o, hi, lo, each=None):
                return col_tiles(u, range(DK), range(DK), o, hi, lo, each)

            def row_unit(u, n, hi, lo, banks=4):
                s = u % NS
                for t in range(NT):
                    for kk in range(2):
                        k = 2 * n + kk
                        c = slice(kk * T, (kk + 1) * T)
                        ins = mm3(pb[banks + t], hi[:, k, tokens(t)], lo[:, k, tokens(t)], WH[:, s, c], WL[:, s, c],
                                  k == 0, k == DK - 1)
                return ins

            def statistic(n, with_columns=False):
                ge(pe, s_acc[n], DK)
                ins = nc.tensor.matmul(pb[6], INVD, ACC[:], start=True, stop=True)
                if with_columns:
                    for t in range(NT):
                        ins = nc.tensor.matmul(pb[7][:, t:t + 1], ACC[:, tokens(t)], INVD[:, 0:1],
                                               start=True, stop=True)
                ins.then_inc(s_ms[n].sem, 1)

            pe.wait_ge(s_prm, 32)
            u0 = UNITS["qk"][0]

            def head_sums(u):
                pe.wait_ge(s_zsq, u + 1)
                if u >= 2:
                    pe.wait_ge(s_hsd, u - 1)
                nc.tensor.matmul(pb[2 + u % 2], BONE, TMP[:, 2 + u % 2, :], start=True, stop=True
                                 ).then_inc(s_hms, 1)

            for u in range(8):
                ready(u0 + u)
                if u >= 2:
                    pe.wait_ge(s_z, u - 1)
                col_unit(u0 + u, pb[u % 2], AH, AL, s_gl["mix"] if u == 0 else None).then_inc(s_used, 1)
                if u == 0:
                    statistic("mix", True)
                if u >= 1:
                    head_sums(u - 1)

            for n in range(4):
                u = UNITS["v"][0] + n
                ready(u)
                if n == 0:
                    ge(pe, s_sd["mix"], 1)
                    pe.wait_ge(s_rcd, 1)
                row_unit(u, n, AH, AL).then_inc(s_used, 1)
                if n == 0:
                    head_sums(7)

            steps = NT * H1

            def score_step(n):
                i, h = NT - 1 - n // H1, n % H1
                w, hp, ht = (i + 1) * P, (h % 2) * HD, h // 2
                if n == 0:
                    pe.wait_ge(s_qk, 8)
                    pe.wait_ge(s_hsd, 8)
                if n >= 2:
                    pe.wait_ge(s_sc, n - 1)
                nc.tensor.matmul(pb[2 + n % 2][:, 0:w], QT[hp:hp + HD, ht, tokens(i)], KT[hp:hp + HD, ht, 0:w],
                                 start=True, stop=True).then_inc(s_s, 1)

            def turn_step(n):
                i = NT - 1 - n // H1
                pe.wait_ge(s_e, n + 1)
                if n == 0:
                    pe.wait_ge(s_v, NT)
                if n >= 2:
                    pe.wait_ge(s_ptc, n - 1)
                for j in range(i + 1):
                    ins = nc.tensor.transpose(pb[4 + n % 2][:, tokens(j)], SC[:, n % 2, tokens(j)], IDENT)
                ins.then_inc(s_pt, 1)

            def value_step(n):
                i, h = NT - 1 - n // H1, n % H1
                pe.wait_ge(s_ptc, n + 1)
                if n >= 2:
                    pe.wait_ge(s_ya, n - 1)
                for j in range(i + 1):
                    ins = nc.tensor.matmul(pb[6 + n % 2][:, 0:HD], PT[:, n % 2, tokens(j)],
                                           V[:, j, h * HD:(h + 1) * HD], start=(j == 0), stop=(j == i))
                ins.then_inc(s_pv, 1)

            for n in range(steps + 2):
                if n < steps:
                    score_step(n)
                    for t in range(3 * n, 3 * n + 3):
                        cu, k = divmod(t, DK)
                        u = UNITS["conv"][0] + cu
                        if k == 0:
                            ready(u)
                            if cu == 0:
                                pe.wait_ge(s_z, 8)
                            if cu >= 2:
                                pe.wait_ge(s_cuf, cu - 1)
                        ins = mm3(pb[cu % 2], WH[:, u % NS, tokens(k)], WL[:, u % NS, tokens(k)],
                                  AH[:, k, :], AL[:, k, :], k == 0, k == DK - 1)
                        if k == DK - 1:
                            ins.then_inc(s_used, 1)
                if 1 <= n <= steps:
                    turn_step(n - 1)
                if n >= 2:
                    value_step(n - 2)

            pe.wait_ge(s_ycacc, CK)
            pe.wait_ge(s_cuf, 12)
            nc.tensor.matmul(pb[0], INVD, ACC[:], start=True, stop=True).then_inc(s_ycms, 1)
            pe.wait_ge(s_ptc, steps)
            pe.wait_ge(s_ya, steps)
            for i in range(NT):
                pe.wait_ge(s_yan, i + 1)
                for b in range(CK):
                    ins = nc.tensor.transpose(pb[4 + b][:, tokens(i)], YA[:, i, tokens(b)], IDENT)
            ins.then_inc(s_yt, 1)

            def out_projection(name, each, free):
                for m in range(DK):
                    u = UNITS[name][0] + m
                    ready(u)
                    if m >= 2:
                        ge(pe, free, m - 1)
                    col_unit(u, pb[m % 2], YH, YL, each if m == 0 else None).then_inc(s_used, 1)

            pe.wait_ge(s_ycsd, 1)
            out_projection("wo", s_yl, s_x["ffn"])
            if stop == "mixer1":
                return

            def ffn(f, norm, down, free):
                S, u0 = FS[f], UNITS[f][0]
                statistic(norm)
                ge(pe, s_gl[norm], DK)

                def chunks(i):
                    for j in range(2):
                        for w, s in enumerate((S["pad"], S["up"])):
                            u = u0 + 2 * j + w
                            wait(pe, s_split, i, NS, u + 1)
                            wait(pe, s, i, 2, j - 1)
                            col_unit(u, pb[2 * j + w], AH, AL).then_inc(s_used, 1)

                chunks(0)
                with pe.Fori(1, FC // 2) as i:
                    chunks(i)

                u0 = UNITS[down][0]

                def down_pair(i):
                    for j in range(2):
                        k0 = 0
                        wait(pe, free, i, 2, j - 1)
                        for q, nt in enumerate(DOWN_TILES):
                            u = u0 + NS * j + q
                            wait(pe, s_split, i, 2 * NS, u + 1)
                            if q == 3 and isinstance(i, int) and j == 0:
                                ge(pe, S["sl"], FC)
                            ins = col_tiles(u, range(nt), range(k0, k0 + nt), pb[4 + j], SH, SL,
                                            start=(q == 0), stop=(q == 3))
                            ins.then_inc(s_used, 1)
                            k0 += nt

                ge(pe, S["sl"], FC - 1)
                down_pair(0)
                with pe.Fori(1, DK // 2) as i:
                    down_pair(i)

            ffn("ffn", "ffn", "down", s_x["ple"])

            statistic("ple")
            for m in range(DK):
                u = UNITS["pgate"][0] + m
                ready(u)
                if m >= 2:
                    pe.wait_ge(s_pgt, m - 1)
                col_unit(u, pb[m % 2], AH, AL, s_gl["ple"] if m == 0 else None).then_inc(s_used, 1)
            pe.wait_ge(s_pl, 2)
            for m in range(DK):
                u = UNITS["pproj"][0] + m // 4
                ready(u)
                if m >= 2:
                    pe.wait_ge(s_pm, m - 1)
                ins = col_tiles(u, range(2 * (m % 4), 2 * (m % 4) + 2), range(2), pb[2 + m % 2], PH, PL)
                if m % 4 == 3:
                    ins.then_inc(s_used, 1)
                else:
                    ins.then_inc(s_ppj, 1)
            if stop == "block1":
                return

            u = UNITS["small"][0]
            ready(u)
            pe.wait_ge(s_pgt, DK)
            col_unit(u, pb[0], GH, GL, s_gl["mix2"]).then_inc(s_used, 1)
            pe.wait_ge(s_pm, DK)
            statistic("mix2", True)
            for n in range(4):
                u = UNITS["bv"][0] + n
                ready(u)
                if n == 0:
                    ge(pe, s_sd["mix2"], 1)
                    pe.wait_ge(s_rcd, 2)
                row_unit(u, n, GH, GL).then_inc(s_used, 1)
            pe.wait_ge(s_stk, 1)
            for t in range(NT):
                ins = nc.tensor.transpose(pb[1][:, tokens(t)], TMP[:, 3, tokens(t)], IDENT)
            ins.then_inc(s_stt, 1)

            def key_query_units(pair, bank):
                for n in range(2):
                    u = UNITS[f"kq{pair}"][0] + n
                    ready(u)
                    col_unit(u, pb[bank + n], GH, GL).then_inc(s_used, 1)

            def decay_gates(pair, bank):
                for n in range(2):
                    h = 2 * pair + n
                    nc.tensor.matmul(pb[bank + n], SQ[64:96, 1, h * P:(h + 1) * P], SQ[64:96, 0, :],
                                     start=True, stop=True).then_inc(s_gpr, 1)

            pe.wait_ge(s_row, 1)
            pe.wait_ge(s_cols, 1)
            key_query_units(0, 0)
            pe.wait_ge(s_sel, 16)
            pe.wait_ge(s_vb, NT)
            decay_gates(0, 4)
            pe.wait_ge(s_lax, 2)
            for n in range(4):
                u = UNITS["ao"][0] + n
                ready(u)
                row_unit(u, n, GH, GL).then_inc(s_used, 1)

            def level_step(h, j):
                n = NT * h + j
                if j == 0:
                    pe.wait_ge(s_lv, 9 * (h + 1))
                    if h == 0:
                        pe.wait_ge(s_dup, 2)
                if n:
                    pe.wait_ge(s_sad, n)
                for l in range(8):
                    k, q = (KS[:, l, tokens(j)], QS[:, l, tokens(j)]) if l < 7 else \
                        (K2[:, h % 2, tokens(j)], Q2[:, h % 2, tokens(j)])
                    ins = nc.tensor.matmul(PS[:, 1 + l // 4, (l % 4) * P:(l % 4 + 1) * P], k, q,
                                           start=True, stop=True)
                ins.then_inc(s_gs, 1)
                if n:
                    pe.wait_ge(s_sao, n)
                for l, tiles in ((0, slice(2 * P, T) if j < 2 else slice(0, 2 * P)), (1, tokens(j ^ 1))):
                    ins = nc.tensor.matmul(pb[0][:, tiles], KB_[:, l, tokens(j)], QB[:, l, tiles],
                                           start=True, stop=True)
                ins.then_inc(s_gb, 1)

            def mix_step(h, j):
                n = NT * h + j
                pe.wait_ge(s_sad, n + 1)
                pe.wait_ge(s_sao, n + 1)
                if j == 0 and h:
                    pe.wait_ge(s_oc, h)
                for i in range(NT):
                    ins = nc.tensor.matmul(pb[3][:, tokens(i)], SA[:, j % 2, tokens(i)],
                                           VB[:, j, h * DV:(h + 1) * DV], start=(i == 0 and j == 0),
                                           stop=(i == NT - 1 and j == NT - 1), skip_group_check=True)
                ins.then_inc(s_go, 1)

            for h in range(H2):
                if h == 1:
                    pe.wait_ge(s_aof, NT)
                    key_query_units(1, 4)
                    decay_gates(1, 6)
                if h >= 2:
                    for m in range(2 * h - 4, 2 * h - 2):
                        u = UNITS["aqk"][0] + m
                        ready(u)
                        if m < 2:
                            pe.wait_ge(s_dup, 4)
                        else:
                            pe.wait_ge(s_apad, m - 1)
                        col_unit(u, pb[4 + m % 2], GH, GL).then_inc(s_used, 1)
                for j in range(NT + 1):
                    if j < NT:
                        level_step(h, j)
                    if j:
                        mix_step(h, j - 1)

            for name, done in (("br", None), ("av", s_br)):
                for n in range(4):
                    u = UNITS[name][0] + n
                    ready(u)
                    if n == 0:
                        pe.wait_ge(s_apad, 4)
                        pe.wait_ge(s_lax, 4)
                        if done is not None:
                            pe.wait_ge(done, NT)
                    row_unit(u, n, GH, GL).then_inc(s_used, 1)

            def state_bank(d, i):
                n = NT * d + i
                return PS[:, 4 + n // 3, (n % 3) * (DV + 1):(n % 3 + 1) * (DV + 1)]

            def lstm_scores(n):
                h, j = divmod(n, NT)
                hp, ht = (h % 2) * HD, h // 2
                if j == 0:
                    if h == 0:
                        pe.wait_ge(s_zero, 32)
                        pe.wait_ge(s_sad, 4 * NT)
                        pe.wait_ge(s_sao, 4 * NT)
                    else:
                        pe.wait_ge(s_bcc, 2 * h)
                    for d in range(2):
                        r = h + H2 * d
                        ins = nc.tensor.matmul(pb[d], SEL[0:8, r * P:(r + 1) * P], MROWS[d],
                                               start=True, stop=True)
                    ins.then_inc(s_bc, 1)
                if n == 0:
                    pe.wait_ge(s_aqk, 4)
                    pe.wait_ge(s_oc, H2)
                if n >= 2:
                    pe.wait_ge(s_sw, 2 * (n - 1))
                nc.tensor.matmul(pb[2 + n % 2], AK[hp:hp + HD, ht, tokens(j)], AQ[hp:hp + HD, ht, :],
                                 start=True, stop=True).then_inc(s_ms2, 1)

            def lstm_mix(n):
                h, j = divmod(n, NT)
                if n == 0:
                    pe.wait_ge(s_va, NT + 1)
                if j == 0 and h:
                    pe.wait_ge(s_hf, h)
                for d in range(2):
                    pe.wait_ge(s_sw, 2 * n + d + 1)
                    tiles = range(j, NT) if d == 0 else range(0, j + 1)
                    for i in tiles:
                        m = NT * d + i
                        first = j == (0 if d == 0 else i) and m % 3 == 0
                        ins = nc.tensor.matmul(state_bank(d, i), WT[:, n % 2, d, tokens(i)], VA[:, j, h, :],
                                               start=first, stop=(j == NT - 1), skip_group_check=True)
                ins.then_inc(s_mo, 1)

            for n in range(NT * H2 + 1):
                if n < NT * H2:
                    lstm_scores(n)
                if n:
                    lstm_mix(n - 1)

            pe.wait_ge(s_hf, H2)
            pe.wait_ge(s_w, 2 * NT * H2)
            for b in (4, 5, 6, 7, 0, 1, 2, 3):
                pe.wait_ge(s_y2, 1 if b >= CK else 2)
                src = YM if b < CK else YB
                for i in range(NT):
                    ins = nc.tensor.transpose(pb[b][:, tokens(i)], src[:, i, tokens(b % CK)], IDENT)
                ins.then_inc(s_y2t, 1)
            pe.wait_ge(s_y2l, DK)
            out_projection("wo2", s_y2l, s_mix)
            statistic("post")
            ffn("ffn2", "ffn2", "down2", s_mix2)
            statistic("fpost")
        @block.scalar
        def _(act):
            n_ac = [0]

            def link(ins):
                n_ac[0] += 1
                ins.then_inc(s_ac, 1)
                act.wait_ge(s_ac, n_ac[0])

            A = nc.scalar.activation

            def norm_tile(n, gain, i, per, j, hi, x=None, split=True):
                k = per * i + j if isinstance(i, int) else None
                src = at(X if x is None else x, i, j, per)
                if split:
                    wait(act, s_x[n], i, per, j + 1)
                    A(at(hi, i, j, per), src, ACT.Copy, scale=prm_at(gain, 0, i, per, j)).then_inc(s_gh[n].sem, 1)
                wait(act, s_acc[n], i, per, j - 1)
                A(SQ[:, j % 2, :], src, ACT.Square).then_inc(s_sq[n].sem, 1)

            def norm_root(n):
                ge(act, s_ms[n], 1)
                A(RS[:], pb[6], ACT.Sqrt, bias=EPS_C).then_inc(s_sd[n].sem, 1)

            act.wait_ge(s_prm, 32)
            for k in range(DK):
                if k % 2 == 0:
                    act.wait_ge(s_xin[k // 2], 16)
                A(AH[:, k, :], X[:, k, :], ACT.Copy, scale=prm("g_mix", k)).then_inc(s_gh["mix"].sem, 1)
                if k >= 2:
                    ge(act, s_acc["mix"], k - 1)
                A(SQ[:, k % 2, :], X[:, k, :], ACT.Square).then_inc(s_sq["mix"].sem, 1)
            norm_root("mix")
            A(RC, pb[7][:, 0:NT], ACT.Sqrt, bias=EPS_C).then_inc(s_rcd, 1)

            def head_root(u):
                act.wait_ge(s_hms, u + 1)
                q = u < CK
                A(SC[:, u % 2, :], pb[2 + u % 2], ACT.Sqrt, bias=EPS64_C if q else EPS_C,
                  scale=1.0 if q else 1.0 / HD).then_inc(s_hsd, 1)

            for u in range(8):
                act.wait_ge(s_z, u + 1)
                if u >= 2:
                    act.wait_ge(s_hms, u - 1)
                A(TMP[:, 2 + u % 2, :], TMP[:, u % 2, :], ACT.Square).then_inc(s_zsq, 1)
                if u >= 1:
                    if u >= 3:
                        act.wait_ge(s_qk, u - 2)
                    head_root(u - 1)
            act.wait_ge(s_qk, 6)
            head_root(7)
            act.wait_ge(s_rc, 1)
            act.wait_ge(s_used, UNITS["v"][0] + 4)
            for t in range(NT):
                A(V[:, t, :], pb[4 + t], ACT.Copy, scale=RC[:, t:t + 1]).then_inc(s_v, 1)

            def conv_first(j):
                act.wait_ge(s_cx, j + 1)
                if j == 0:
                    act.wait_ge(s_qk, 8)
                    act.wait_ge(s_hms, 8)
                if j >= 1:
                    act.wait_ge(s_yc, j)
                A(TMP[:, 2, :], PAD[:, 0, 0:T], ACT.Identity, bias=prm("cb", j), scale=prm("cw", j)
                  ).then_inc(s_c0, 1)

            def conv_square(j):
                act.wait_ge(s_yc, j + 1)
                if j == 0:
                    ge(act, s_ms["mix"], 1)
                if j >= 2:
                    act.wait_ge(s_ycacc, j - 1)
                A(SQ[:, j % 2, :], YC[:, j, :], ACT.Square).then_inc(s_ycsq, 1)

            steps = NT * H1
            for n in range(steps + 1):
                if n < steps:
                    w = (NT - n // H1) * P
                    act.wait_ge(s_nm, n + 1)
                    A(SC[:, n % 2, 0:w], SC[:, n % 2, 0:w], ACT.Exp, bias=NM[:, n:n + 1],
                      accum_out=DEN[:, n:n + 1]).then_inc(s_e, 1)
                if n >= 1:
                    m = n - 1
                    w = (NT - m // H1) * P
                    act.wait_ge(s_pt, m + 1)
                    if m >= 2:
                        act.wait_ge(s_pv, m - 1)
                    A(PT[:, m % 2, 0:w], pb[4 + m % 2][:, 0:w], ACT.Copy).then_inc(s_ptc, 1)
                if n % 8 == 6:
                    conv_first(n // 8)
                if n % 8 == 1 and n > 8:
                    conv_square(n // 8 - 1)
            conv_square(3)
            act.wait_ge(s_ya, steps)
            act.wait_ge(s_ycacc, CK)
            for i in range(NT):
                A(SQ[:, 0, :], YA[:, i, :], ACT.Square, accum_out=YS[:, i:i + 1]).then_inc(s_yss, 1)
                act.wait_ge(s_yss, i + 1)
            link(A(YS, YS, ACT.Sqrt, bias=EPS_C, scale=1.0 / CW))
            act.wait_ge(s_ycms, 1)
            A(TMP[:, 3, :], pb[0], ACT.Sqrt, bias=EPS_C, scale=float(D) / CW).then_inc(s_ycsd, 1)
            for j in range(CK):
                act.wait_ge(s_yn, j + 1)
                A(YH[:, j, :], SC[:, j % 2, :], ACT.Copy).then_inc(s_ynh, 1)
            act.wait_ge(s_yt, 1)
            act.wait_ge(s_yl, CK)
            for b in range(CK):
                A(YH[:, CK + b, :], pb[4 + b], ACT.Copy, scale=prm("g_oa", b)).then_inc(s_yh, 1)
            def x_tiles(n, gain, hi):
                for m in range(DK):
                    norm_tile(n, gain, m // 2, 2, m % 2, hi)

            x_tiles("ffn", "g_ffn", AH)
            if stop == "mixer1":
                return

            def ffn(f, norm, func, down):
                S = FS[f]
                norm_root(norm)

                def chunk(i, j):
                    wait(act, S["pad"], i, 2, j + 1)
                    wait(act, S["h"], i, 2, j - 1)
                    A(TMP[:, j, :], PAD[:, j, 0:T], ACT.Identity, bias=prm_at("fcb" + sfx, 0, i, 2, j),
                      scale=prm_at("fcw" + sfx, 0, i, 2, j)).then_inc(S["t1"].sem, 1)
                    wait(act, S["t3"], i, 2, j + 1)
                    A(TMP[:, j, :], TMP[:, j, :], func).then_inc(S["act"].sem, 1)
                    wait(act, S["h"], i, 2, j + 1)
                    A(at(SH, i, j, 2), TMP[:, 2 + j, :], ACT.Copy).then_inc(S["sh"].sem, 1)

                sfx = "" if f == "ffn" else "2"
                for j in range(2):
                    chunk(0, j)
                with act.Fori(1, FC // 2) as i:
                    for j in range(2):
                        chunk(i, j)

                u0 = UNITS[down][0]

                def tile(i, j):
                    if f == "ffn":
                        norm_tile("ple", "g_ple", i, 2, j, AH)
                    else:
                        wait(act, s_used, i, 2 * NS, u0 + NS * (j + 1))
                        A(at(MIX2, i, j, 2), pb[4 + j], ACT.Copy).then_inc(s_mix2, 1)
                        wait(act, s_mix2, i, 2, j + 1)
                        norm_tile("fpost", None, i, 2, j, None, x=MIX2, split=False)

                for j in range(2):
                    tile(0, j)
                with act.Fori(1, DK // 2) as i:
                    for j in range(2):
                        tile(i, j)

            ffn("ffn", "ffn", ACT.Silu, "down")

            norm_root("ple")
            act.wait_ge(s_used, UNITS["pgate"][0])
            act.dma_start(PIN[:], dram["p"]).then_inc(s_pin, 16)
            for m in range(DK):
                act.wait_ge(s_pgt, m + 1)
                A(SG[:, m, :], TMP[:, m % 2, :], ACT.Sigmoid).then_inc(s_sg, 1)
                if m == 3:
                    act.wait_ge(s_pin, 16)
                    for q in range(2):
                        A(PH[:, q, :], PIN[:, q, :], ACT.Copy).then_inc(s_ph, 1)
            x_tiles("mix2", "pre2", GH)
            if stop == "block1":
                return

            norm_root("mix2")
            A(RC, pb[7][:, 0:NT], ACT.Sqrt, bias=EPS_C).then_inc(s_rcd, 1)
            act.wait_ge(s_row, 1)
            rows = slice(0, 8)
            A(TMP[rows, 0, :], SQ[rows, 0, :], ACT.Identity, bias=prm("gib", 0, rows)).then_inc(s_gabs, 1)
            link(A(TMP[rows, 1, :], SQ[32:40, 0, :], ACT.Identity, bias=prm("gfb", 0, slice(32, 40))))
            link(A(TMP[rows, 2, :], TMP[rows, 1, :], ACT.Abs))
            link(A(TMP[rows, 2, :], TMP[rows, 2, :], ACT.Exp, scale=-1.0))
            A(TMP[rows, 2, :], TMP[rows, 2, :], ACT.Ln, bias=ONE_C[rows]).then_inc(s_rw8, 1)
            act.wait_ge(s_rc, 2)
            act.wait_ge(s_used, UNITS["bv"][0] + 4)
            for t in range(NT):
                A(VB[:, t, :], pb[4 + t], ACT.Copy, scale=RC[:, t:t + 1]).then_inc(s_vb, 1)
            act.wait_ge(s_gabs, 2)
            for g, src in enumerate((TMP[rows, 2, :], TMP[rows, 1, :], SQ[rows, 1, :], ACC[rows, :])):
                ins = A(TMP[32 * g:32 * g + 8, 3, :], src, ACT.Copy)
            ins.then_inc(s_stk, 1)
            act.wait_ge(s_stk, 1)
            act.dma_start(SQ[64:96, 1, :], dram["gla_w"]).then_inc(s_sel, 16)
            act.dma_start(LM[:], dram["masks"]).then_inc(s_lm, 16)
            act.wait_ge(s_stt, 1)
            link(A(CG, pb[1].rearrange("p (t g r) -> p t g r", t=NT, g=4)[:, :, :, 0:8], ACT.Copy))
            A(CG[:, :, 2:4, :], CG[:, :, 2:4, :], ACT.Exp, scale=-1.0).then_inc(s_cols, 1)

            def duplicate(pair):
                for n, dst in enumerate((K2, Q2)):
                    act.wait_ge(s_dup, 2 * pair + n + 1)
                    if pair and n == 0:
                        act.wait_ge(s_gs, 2 * NT)
                        act.wait_ge(s_lv, 18)
                    for hh in range(2):
                        for half in range(2):
                            ins = A(dst[half * HD:(half + 1) * HD, hh, :], TMP[hh * HD:(hh + 1) * HD, n, :],
                                    ACT.Copy, scale=0.125 if n else 1.0)
                    ins.then_inc(s_kqf, 1)

            def gate_logs(pair):
                for n in range(2):
                    h = 2 * pair + n
                    act.wait_ge(s_gpr, h + 1)
                    if h == 0:
                        act.wait_ge(s_stt, 1)
                    if h:
                        act.wait_ge(s_xg, h)
                    if h == 2:
                        act.wait_ge(s_lv, 18)
                    link(A(TMP[:, 2, :], pb[(4 if pair == 0 else 6) + n], ACT.Identity, bias=prm("glab", h)))
                    link(A(TMP[:, 3, :], TMP[:, 2, :], ACT.Abs))
                    link(A(TMP[:, 3, :], TMP[:, 3, :], ACT.Exp, scale=-1.0))
                    A(TMP[:, 3, :], TMP[:, 3, :], ACT.Ln, bias=ONE_C).then_inc(s_lax, 1)

            duplicate(0)
            gate_logs(0)

            def decay_step(h, l):
                act.wait_ge(s_dd, 9 * h + l + 1)
                s = 2 + l % 2
                A(TMP[:, s, :], TMP[:, s, :], ACT.Exp, scale=1.0 / 16.0).then_inc(s_ee, 1)

            def conv_pair(m):
                dst = (AQ if m < 2 else AK)[:, m % 2, :]
                act.wait_ge(s_apad, m + 1)
                A(dst, PAD[:, 0, 0:T], ACT.Identity, bias=prm("mcb", m), scale=prm("mcw", m)).then_inc(s_a1, 1)
                act.wait_ge(s_a3, m + 1)
                A(dst, dst, ACT.Silu).then_inc(s_aqk, 1)

            for h in range(H2):
                for l in range(9):
                    decay_step(h, l)
                if h == 0:
                    act.wait_ge(s_used, UNITS["ao"][0] + 4)
                    for t in range(NT):
                        A(AO[:, t, :], pb[4 + t], ACT.Sigmoid, scale=RC[:, t:t + 1]).then_inc(s_aof, 1)
                if h >= 2:
                    for m in range(2 * h - 4, 2 * h - 2):
                        conv_pair(m)
                for j in range(NT):
                    n = NT * h + j
                    act.wait_ge(s_gb, n + 1)
                    if n >= 2:
                        act.wait_ge(s_go, n - 1)
                    parts = [c for c in (slice(0, j * P), slice((j + 1) * P, T)) if c.stop > c.start]
                    for c in parts:
                        ins = A(SA[:, j % 2, c], pb[0][:, c], ACT.Copy)
                    ins.then_inc(s_sao, 1)
                act.wait_ge(s_go, NT * (h + 1))
                A(YB[:, :, h * DV:(h + 1) * DV], pb[3].rearrange("p (t c) -> p t c", t=NT), ACT.Copy
                  ).then_inc(s_oc, 1)
                if h == 1:
                    duplicate(1)
                    gate_logs(1)

            act.wait_ge(s_used, UNITS["br"][0] + 4)
            for t in range(NT):
                A(BR[:, t, :], pb[4 + t], ACT.Silu, scale=RC[:, t:t + 1]).then_inc(s_br, 1)
            act.wait_ge(s_sad, 4 * NT)
            act.wait_ge(s_lv, 36)
            act.dma_start(SEL[:], dram["selectors"]).then_inc(s_zero, 16)
            act.dma_start(NEG[:], dram["negmask"]).then_inc(s_zero, 16)
            act.wait_ge(s_ybq, 1)
            link(A(BSS, BSS, ACT.Sqrt, bias=EPS_C, scale=1.0 / DV))
            A(BSS, BSS, ACT.Copy).then_inc(s_gn, 1)
            act.wait_ge(s_used, UNITS["av"][0] + 4)
            for t in range(NT):
                A(VA[:, t, :, 0:DV], pb[4 + t].rearrange("p (h c) -> p h c", h=H2), ACT.Copy,
                  scale=RC[:, t:t + 1]).then_inc(s_va, 1)

            for n in range(NT * H2 + 1):
                if n < NT * H2:
                    h, j = divmod(n, NT)
                    if j == 0:
                        act.wait_ge(s_bc, h + 1)
                        act.wait_ge(s_ybq, 1)
                        if h:
                            act.wait_ge(s_ad, 2 * n)
                            act.wait_ge(s_w, 2 * n)
                        for d in range(2):
                            A(TMP[:, 2 + d, :], pb[d], ACT.Copy).then_inc(s_bcc, 1)
                        act.wait_ge(s_bcc, 2 * h + 2)
                    for d in range(2):
                        c = CG[:, j, d, h + H2 * d:h + H2 * d + 1]
                        act.wait_ge(s_ad, 2 * n + d + 1)
                        off = slice((j + 1) * P, T) if d == 0 else slice(0, j * P)
                        if off.stop > off.start:
                            A(WT[:, n % 2, d, off], TMP[:, 2 + d, off], ACT.Exp, bias=c)
                        A(WT[:, n % 2, d, tokens(j)], WT[:, n % 2, d, tokens(j)], ACT.Exp).then_inc(s_w, 1)
                if n and n % NT == 0:
                    h = n // NT - 1
                    act.wait_ge(s_hb, h + 1)
                    for i in range(NT):
                        m = NT + i
                        bank = PS[:, 4 + m // 3, (m % 3) * (DV + 1):(m % 3) * (DV + 1) + DV]
                        ins = A(TMP[:, h % 2, tokens(i)], bank, ACT.Copy, scale=DN[:, m:m + 1])
                    ins.then_inc(s_hst, 1)
            act.wait_ge(s_ybq, 2)
            link(A(MSS, MSS, ACT.Sqrt, bias=EPS_C, scale=1.0 / DV))
            A(MSS, MSS, ACT.Copy).then_inc(s_gn, 1)
            for n, b in enumerate((4, 5, 6, 7, 0, 1, 2, 3)):
                act.wait_ge(s_y2t, n + 1)
                A(YH[:, b, :], pb[b], ACT.Copy, scale=prm("mnorm" if b < CK else "gnorm", b % CK)
                  ).then_inc(s_y2h, 1)

            for m in range(DK):
                act.wait_ge(s_used, UNITS["wo2"][0] + m + 1)
                A(MIX[:, m, :], pb[m % 2], ACT.Copy).then_inc(s_mix, 1)
                act.wait_ge(s_mix, m + 1)
                norm_tile("post", None, m // 2, 2, m % 2, None, x=MIX, split=False)
            norm_root("post")
            x_tiles("ffn2", "fpre2", AH)
            ffn("ffn2", "ffn2", ACT.Gelu_apprx_tanh, "down2")
            norm_root("fpost")

        @block.vector
        def _(dve):
            V_ = nc.vector
            n_vc = [0]

            def link(ins):
                n_vc[0] += 1
                ins.then_inc(s_vc, 1)
                dve.wait_ge(s_vc, n_vc[0])

            def low(n, gain, i, per, j, hi, lo):
                wait(dve, s_gh[n], i, per, j + 1)
                V_.scalar_tensor_tensor(at(lo, i, j, per), at(X, i, j, per), prm_at(gain, 0, i, per, j),
                                        at(hi, i, j, per).bitcast(F32), ALU.mult, ALU.subtract
                                        ).then_inc(s_gl[n].sem, 1)

            def add_square(n, i, per, j):
                wait(dve, s_sq[n], i, per, j + 1)
                if isinstance(i, int) and i == 0 and j == 0:
                    V_.tensor_copy(ACC[:], SQ[:, 0, :]).then_inc(s_acc[n].sem, 1)
                else:
                    wait(dve, s_acc[n], i, per, j)
                    V_.tensor_tensor(ACC[:], ACC[:], SQ[:, j % 2, :], ALU.add).then_inc(s_acc[n].sem, 1)

            def norm_reciprocal(n, columns=0):
                ge(dve, s_sd[n], 1)
                V_.reciprocal(RS[:], RS[:]).then_inc(s_rs[n].sem, 1)
                ge(dve, s_rs[n], 1)
                if columns:
                    dve.wait_ge(s_rcd, columns)
                    V_.reciprocal(RC, RC).then_inc(s_rc, 1)

            link(V_.memset(PAD[:], 0.0))
            dve.wait_ge(s_prm, 32)
            for k in range(DK):
                low("mix", "g_mix", k // 2, 2, k % 2, AH, AL)
                add_square("mix", k // 2, 2, k % 2)
            norm_reciprocal("mix", 1)
            gq = UNITS["qk"][0]

            def normed(u):
                dve.wait_ge(s_hsd, u + 1)
                r = SC[:, u % 2, :]
                link(V_.reciprocal(r, r))
                V_.scalar_tensor_tensor((QT if u < CK else KT)[:, u % CK, :], TMP[:, u % 2, :],
                                        prm("qg" if u < CK else "kg"), r, ALU.mult, ALU.mult).then_inc(s_qk, 1)

            for u in range(8):
                dve.wait_ge(s_used, gq + u + 1)
                if u >= 2:
                    normed(u - 2)
                    dve.wait_ge(s_qk, u - 1)
                    dve.wait_ge(s_zsq, u - 1)
                V_.tensor_tensor(TMP[:, u % 2, :], pb[u % 2], RS[:], ALU.mult).then_inc(s_z, 1)
            for u in (6, 7):
                normed(u)

            uc = UNITS["conv"][0]

            def conv_c(j):
                dve.wait_ge(s_used, uc + 3 * j + 1)
                V_.tensor_tensor(TMP[:, 0, :], pb[(3 * j) % 2], RS[:], ALU.mult).then_inc(s_cuf, 1)

            def conv_x(j):
                dve.wait_ge(s_used, uc + 3 * j + 2)
                V_.tensor_tensor(TMP[:, 1, :], pb[(3 * j + 1) % 2], RS[:], ALU.mult).then_inc(s_cuf, 1)
                dve.wait_ge(s_cuf, 3 * j + 2)
                V_.tensor_tensor(PAD[:, 0, 2:T + 2], TMP[:, 0, :], TMP[:, 1, :], ALU.mult).then_inc(s_cx, 1)

            def conv_b(j):
                dve.wait_ge(s_c0, j + 1)
                t = TMP[:, 2, :]
                link(V_.scalar_tensor_tensor(t, PAD[:, 0, 1:T + 1], prm("cw", CK + j), t, ALU.mult, ALU.add))
                link(V_.scalar_tensor_tensor(t, PAD[:, 0, 2:T + 2], prm("cw", 2 * CK + j), t, ALU.mult, ALU.add))
                dve.wait_ge(s_used, uc + 3 * j + 3)
                V_.tensor_tensor(t, t, pb[(3 * j + 2) % 2], ALU.mult).then_inc(s_cuf, 1)
                dve.wait_ge(s_cuf, 3 * j + 3)
                V_.tensor_tensor(YC[:, j, :], t, RS[:], ALU.mult).then_inc(s_yc, 1)

            def conv_sum(j):
                dve.wait_ge(s_ycsq, j + 1)
                if j == 0:
                    V_.tensor_copy(ACC[:], SQ[:, 0, :]).then_inc(s_ycacc, 1)
                else:
                    dve.wait_ge(s_ycacc, j)
                    V_.tensor_tensor(ACC[:], ACC[:], SQ[:, j % 2, :], ALU.add).then_inc(s_ycacc, 1)

            def attention_out(n):
                i, h = NT - 1 - n // H1, n % H1
                dve.wait_ge(s_e, n + 1)
                link(V_.reciprocal(RD[:, n:n + 1], DEN[:, n:n + 1]))
                dve.wait_ge(s_pv, n + 1)
                V_.tensor_scalar(YA[:, i, h * HD:(h + 1) * HD], pb[6 + n % 2][:, 0:HD], RD[:, n:n + 1], None,
                                 ALU.mult).then_inc(s_ya, 1)

            dve.wait_ge(s_bt, 16)
            steps = NT * H1
            for n in range(steps + 3):
                if n < steps:
                    i, h = NT - 1 - n // H1, n % H1
                    w = (i + 1) * P
                    dve.wait_ge(s_s, n + 1)
                    if n >= 2:
                        dve.wait_ge(s_pt, n - 1)
                    V_.tensor_tensor_reduce(SC[:, n % 2, 0:w], pb[2 + n % 2][:, 0:w], BT[:, h, T - w:T], 1.0, -3e38,
                                            ALU.add, ALU.max, MX[:, n:n + 1]).then_inc(s_sc, 1)
                    dve.wait_ge(s_sc, n + 1)
                    V_.tensor_scalar(NM[:, n:n + 1], MX[:, n:n + 1], -1.0, None, ALU.mult).then_inc(s_nm, 1)
                if n >= 3:
                    attention_out(n - 3)
                j, r = divmod(n, 8)
                if r == 3 and j < CK:
                    if j:
                        dve.wait_ge(s_yc, j)
                    conv_c(j)
                if r == 5 and j < CK:
                    conv_x(j)
                if r == 0 and 1 <= j:
                    conv_b(j - 1)
                if r == 2 and 1 <= j:
                    conv_sum(j - 1)
            dve.wait_ge(s_ac, 1)
            link(V_.reciprocal(YS, YS))
            for i in range(NT):
                V_.tensor_scalar(YA[:, i, :], YA[:, i, :], YS[:, i:i + 1], None, ALU.mult).then_inc(s_yan, 1)
            dve.wait_ge(s_ycsd, 1)
            link(V_.reciprocal(TMP[:, 3, :], TMP[:, 3, :]))
            for j in range(CK):
                if j >= 2:
                    dve.wait_ge(s_yl, j - 1)
                V_.scalar_tensor_tensor(SC[:, j % 2, :], YC[:, j, :], prm("g_oc", j), TMP[:, 3, :],
                                        ALU.mult, ALU.mult).then_inc(s_yn, 1)
                dve.wait_ge(s_ynh, j + 1)
                dve.wait_ge(s_yn, j + 1)
                V_.tensor_tensor(YL[:, j, :], SC[:, j % 2, :], YH[:, j, :].bitcast(F32), ALU.subtract
                                 ).then_inc(s_yl, 1)
            for b in range(CK):
                dve.wait_ge(s_yh, b + 1)
                V_.scalar_tensor_tensor(YL[:, CK + b, :], pb[4 + b], prm("g_oa", b),
                                        YH[:, CK + b, :].bitcast(F32), ALU.mult, ALU.subtract).then_inc(s_yl, 1)

            for m in range(DK):
                dve.wait_ge(s_used, UNITS["wo"][0] + m + 1)
                V_.tensor_tensor(X[:, m, :], X[:, m, :], pb[m % 2], ALU.add).then_inc(s_x["ffn"].sem, 1)
                if m:
                    low("ffn", "g_ffn", (m - 1) // 2, 2, (m - 1) % 2, AH, AL)
                    add_square("ffn", (m - 1) // 2, 2, (m - 1) % 2)
            low("ffn", "g_ffn", 3, 2, 1, AH, AL)
            add_square("ffn", 3, 2, 1)
            if stop == "mixer1":
                return

            def ffn(f, norm, down):
                S, u0 = FS[f], UNITS[f][0]
                sfx, o = ("", 2) if f == "ffn" else ("2", 1)
                norm_reciprocal(norm)

                def chunk(i, j):
                    wait(dve, s_used, i, NS, u0 + 2 * j + 1)
                    wait(dve, S["t3"], i, 2, j - 1)
                    V_.tensor_tensor(PAD[:, j, o:o + T], pb[2 * j], RS[:], ALU.mult).then_inc(S["pad"].sem, 1)
                    wait(dve, S["t1"], i, 2, j + 1)
                    wait(dve, S["pad"], i, 2, j + 1)
                    t = TMP[:, j, :]
                    V_.scalar_tensor_tensor(t, PAD[:, j, 1:T + 1], prm_at("fcw" + sfx, FC, i, 2, j), t,
                                            ALU.mult, ALU.add).then_inc(S["ta"].sem, 1)
                    wait(dve, S["ta"], i, 2, j + 1)
                    V_.scalar_tensor_tensor(t, PAD[:, j, 2:T + 2], prm_at("fcw" + sfx, 2 * FC, i, 2, j), t,
                                            ALU.mult, ALU.add).then_inc(S["t3"].sem, 1)
                    wait(dve, s_used, i, NS, u0 + 2 * j + 2)
                    wait(dve, S["sl"], i, 2, j - 1)
                    V_.tensor_tensor(TMP[:, 2 + j, :], pb[2 * j + 1], RS[:], ALU.mult).then_inc(S["up"].sem, 1)
                    wait(dve, S["act"], i, 2, j + 1)
                    wait(dve, S["up"], i, 2, j + 1)
                    V_.tensor_tensor(TMP[:, 2 + j, :], TMP[:, j, :], TMP[:, 2 + j, :], ALU.mult
                                     ).then_inc(S["h"].sem, 1)
                    wait(dve, S["sh"], i, 2, j + 1)
                    V_.tensor_tensor(at(SL, i, j, 2), TMP[:, 2 + j, :], at(SH, i, j, 2).bitcast(F32),
                                     ALU.subtract).then_inc(S["sl"].sem, 1)

                for j in range(2):
                    chunk(0, j)
                with dve.Fori(1, FC // 2) as i:
                    for j in range(2):
                        chunk(i, j)

                u0 = UNITS[down][0]

                def tile(i, j):
                    if f == "ffn":
                        wait(dve, s_used, i, 2 * NS, u0 + NS * (j + 1))
                        V_.tensor_tensor(at(X, i, j, 2), at(X, i, j, 2), pb[4 + j], ALU.add
                                         ).then_inc(s_x["ple"].sem, 1)
                        low("ple", "g_ple", i, 2, j, AH, AL)
                        add_square("ple", i, 2, j)
                    else:
                        add_square("fpost", i, 2, j)

                for j in range(2):
                    tile(0, j)
                with dve.Fori(1, DK // 2) as i:
                    for j in range(2):
                        tile(i, j)

            ffn("ffn", "ffn", "down")

            norm_reciprocal("ple")
            for m in range(DK):
                dve.wait_ge(s_used, UNITS["pgate"][0] + m + 1)
                if m >= 2:
                    dve.wait_ge(s_sg, m - 1)
                V_.tensor_tensor(TMP[:, m % 2, :], pb[m % 2], RS[:], ALU.mult).then_inc(s_pgt, 1)
            for q in range(2):
                dve.wait_ge(s_ph, q + 1)
                V_.tensor_tensor(PL[:, q, :], PIN[:, q, :], PH[:, q, :].bitcast(F32), ALU.subtract
                                 ).then_inc(s_pl, 1)

            def g4(m):
                low("mix2", "pre2", m // 2, 2, m % 2, GH, GL)
                add_square("mix2", m // 2, 2, m % 2)

            for m in range(DK):
                if m % 4 == 3:
                    dve.wait_ge(s_used, UNITS["pproj"][0] + m // 4 + 1)
                else:
                    dve.wait_ge(s_ppj, m - m // 4 + 1)
                dve.wait_ge(s_sg, min(m + 1, DK))
                V_.tensor_tensor(SG[:, m, :], SG[:, m, :], pb[2 + m % 2], ALU.mult).then_inc(s_pm, 1)
                dve.wait_ge(s_pm, m + 1)
                V_.tensor_tensor(X[:, m, :], X[:, m, :], SG[:, m, :], ALU.add).then_inc(s_x["mix2"].sem, 1)
                if m:
                    g4(m - 1)
            g4(DK - 1)
            if stop == "block1":
                return

            link(V_.memset(PAD[:, :, T + 1:T + 2], 0.0))
            norm_reciprocal("mix2", 2)
            rows = slice(0, 8)
            dve.wait_ge(s_used, UNITS["small"][0] + 1)
            V_.tensor_tensor(SQ[:, 0, :], pb[0], RS[:], ALU.mult).then_inc(s_row, 1)
            dve.wait_ge(s_rw8, 1)
            LF, IG, B, BRV = TMP[rows, 3, :], TMP[rows, 0, :], SQ[rows, 1, :], ACC[rows, :]
            CF, CB, MF, MB = TMP[rows, 2, :], TMP[rows, 1, :], *MROWS
            link(V_.scalar_tensor_tensor(LF, TMP[rows, 1, :], 0.0, TMP[rows, 2, :], ALU.min, ALU.subtract))
            V_.tensor_tensor_scan(B, LF, LF, 0.0, ALU.add, ALU.min)
            link(V_.tensor_tensor_scan(BRV[:, ::-1], LF[:, ::-1], LF[:, ::-1], 0.0, ALU.add, ALU.min))
            V_.tensor_tensor(CF, IG, B, ALU.subtract)
            link(V_.tensor_tensor(CB, IG, BRV, ALU.subtract))
            V_.tensor_tensor_scan(MF, CF, CF, 0.0, ALU.max, ALU.max)
            V_.tensor_tensor_scan(MB[:, ::-1], CB[:, ::-1], CB[:, ::-1], 0.0, ALU.max, ALU.max)
            link(V_.memset(TMP[:, 3, :], 0.0))
            V_.tensor_tensor(B, B, MF, ALU.add)
            V_.tensor_tensor(BRV, BRV, MB, ALU.add).then_inc(s_gabs, 1)

            def projected(pair, bank):
                for n in range(2):
                    dve.wait_ge(s_used, UNITS[f"kq{pair}"][0] + n + 1)
                    if pair == 0 and n == 0:
                        dve.wait_ge(s_stk, 1)
                    V_.tensor_tensor(TMP[:, n, :], pb[bank + n], RS[:], ALU.mult).then_inc(s_dup, 1)

            def decays(pair):
                for n in range(2):
                    h = 2 * pair + n
                    dve.wait_ge(s_lax, h + 1)
                    L = TMP[:, 3, :]
                    link(V_.scalar_tensor_tensor(L, TMP[:, 2, :], 0.0, L, ALU.min, ALU.subtract))
                    V_.tensor_tensor_scan(XG[0:HD, n, :], L[0:HD, :], L[0:HD, :], 0.0, ALU.add, ALU.min)
                    V_.memset(XG[HD:P, n, 0:1], 0.0)
                    V_.tensor_tensor_scan(XG[HD:P, n, 1:T], L[HD:P, 0:T - 1], L[HD:P, 0:T - 1], 0.0,
                                          ALU.add, ALU.min).then_inc(s_xg, 1)
                dve.wait_ge(s_xg, 2 * pair + 2)

            projected(0, 0)
            dve.wait_ge(s_pm, DK)
            V_.memset(QB[:], 0.0)
            V_.memset(KB_[:], 0.0)
            V_.memset(QS[:], 0.0)
            link(V_.memset(KS[:], 0.0))
            decays(0)
            dve.wait_ge(s_lm, 16)

            def exponent(h, l):
                b = (BIG + SMALL)[l]
                x = XG[:, h % 2, :].rearrange("p (n w) -> p n w", w=2 * b)
                ref = x[:, :, b - 1:b].to_broadcast([P, T // (2 * b), 2 * b])
                d = TMP[:, 2 + l % 2, :]
                g = 9 * h + l
                if g >= 2:
                    dve.wait_ge(s_lv, g - 1)
                link(V_.tensor_tensor(d.rearrange("p (n w) -> p n w", w=2 * b), x, ref, ALU.subtract))
                V_.scalar_tensor_tensor(d, d, -1.0, d, ALU.mult, ALU.min).then_inc(s_dd, 1)

            def decayed(h, l):
                b = (BIG + SMALL)[l]
                q, k = (QB[:, l, :], KB_[:, l, :]) if l < 2 else (QS[:, l - 2, :], KS[:, l - 2, :])
                dve.wait_ge(s_ee, 9 * h + l + 1)
                if h and l == 0:
                    dve.wait_ge(s_gb, NT * h)
                v = [t.rearrange("p (n s w) -> p n s w", s=2, w=b) for t in
                     (q, k, Q2[:, h % 2, :], K2[:, h % 2, :], TMP[:, 2 + l % 2, :])]
                for half, (qs, ks) in enumerate(((1, 0), (0, 1))):
                    r = slice(half * HD, (half + 1) * HD)
                    V_.tensor_tensor(v[0][r, :, qs, :], v[2][r, :, qs, :], v[4][r, :, qs, :], ALU.mult)
                    ins = V_.tensor_tensor(v[1][r, :, ks, :], v[3][r, :, ks, :], v[4][r, :, ks, :], ALU.mult)
                ins.then_inc(s_lv, 1)

            def conv_tile(m):
                dve.wait_ge(s_used, UNITS["aqk"][0] + m + 1)
                if m:
                    dve.wait_ge(s_a3, m)
                V_.tensor_tensor(PAD[:, 0, 1:T + 1], pb[4 + m % 2], RS[:], ALU.mult).then_inc(s_apad, 1)
                dst = (AQ if m < 2 else AK)[:, m % 2, :]
                dve.wait_ge(s_apad, m + 1)
                dve.wait_ge(s_a1, m + 1)
                link(V_.scalar_tensor_tensor(dst, PAD[:, 0, 1:T + 1], prm("mcw", 4 + m), dst,
                                             ALU.mult, ALU.add))
                V_.scalar_tensor_tensor(dst, PAD[:, 0, 2:T + 2], prm("mcw", 8 + m), dst,
                                        ALU.mult, ALU.add).then_inc(s_a3, 1)

            masked = TMP[:, 0:2, :].rearrange("p a (l c) -> p (a l) c", c=P)
            for h in range(H2):
                if h == 0:
                    dve.wait_ge(s_kqf, 2)
                if h == 2:
                    dve.wait_ge(s_kqf, 4)
                exponent(h, 0)
                for l in range(9):
                    if l < 8:
                        exponent(h, l + 1)
                    decayed(h, l)
                if h >= 2:
                    for m in range(2 * h - 4, 2 * h - 2):
                        conv_tile(m)
                for j in range(NT):
                    n = NT * h + j
                    dve.wait_ge(s_gs, n + 1)
                    if n >= 2:
                        dve.wait_ge(s_go, n - 1)
                    link(V_.tensor_tensor(masked, PS[:, 1:3, :].rearrange("p a (l c) -> p (a l) c", c=P),
                                          LM.rearrange("p (l c) -> p l c", c=P), ALU.mult))
                    V_.tensor_reduce(SA[:, j % 2, tokens(j)], masked.rearrange("p l c -> p c l"),
                                     mybir.AxisListType.X, ALU.add).then_inc(s_sad, 1)
                    dve.wait_ge(s_sad, n + 1)
                if h == 1:
                    projected(1, 4)
                    decays(1)

            def head_squares(y, sums):
                for i in range(NT):
                    link(V_.tensor_tensor(TMP[:, 2, :], y[:, i, :], y[:, i, :], ALU.mult))
                    ins = V_.tensor_reduce(sums[:, H2 * i:H2 * i + H2],
                                           TMP[:, 2, :].rearrange("p (h c) -> p h c", h=H2),
                                           mybir.AxisListType.X, ALU.add)
                    if i < NT - 1:
                        link(ins)
                ins.then_inc(s_ybq, 1)

            def gated(y, r, gate):
                for i in range(NT):
                    for h in range(H2):
                        c = slice(h * DV, (h + 1) * DV)
                        ins = V_.scalar_tensor_tensor(y[:, i, c], y[:, i, c], r[:, H2 * i + h:H2 * i + h + 1],
                                                      gate[:, i, c], ALU.mult, ALU.mult)
                ins.then_inc(s_y2, 1)

            dve.wait_ge(s_oc, H2)
            head_squares(YB, BSS)
            dve.wait_ge(s_gs, 4 * NT)
            V_.memset(VA[:, :, :, DV:DV + 1], 1.0).then_inc(s_va, 1)
            dve.wait_ge(s_gn, 1)
            link(V_.reciprocal(BSS, BSS))
            dve.wait_ge(s_br, NT)
            gated(YB, BSS, BR)

            dve.wait_ge(s_zero, 32)
            dve.wait_ge(s_go, 4 * NT)

            def exponents(n):
                h, j = divmod(n, NT)
                if j == 0:
                    dve.wait_ge(s_bcc, 2 * h + 2)
                if n >= 2:
                    dve.wait_ge(s_mo, n - 1)
                for d in range(2):
                    c = CG[:, j, d, h + H2 * d:h + H2 * d + 1]
                    V_.scalar_tensor_tensor(WT[:, n % 2, d, tokens(j)], TMP[:, 2 + d, tokens(j)], c, NEG[:, d, :],
                                            ALU.add, ALU.add).then_inc(s_ad, 1)

            def weighted(n):
                j = n % NT
                dve.wait_ge(s_ms2, n + 1)
                for d in range(2):
                    dve.wait_ge(s_w, 2 * n + d + 1)
                    c = slice(j * P, T) if d == 0 else slice(0, (j + 1) * P)
                    w = WT[:, n % 2, d, c]
                    V_.scalar_tensor_tensor(w, pb[2 + n % 2][:, c], 0.125, w, ALU.mult, ALU.mult
                                            ).then_inc(s_sw, 1)

            def state_out(h):
                dve.wait_ge(s_mo, NT * (h + 1))
                for b, c in ((0, 3), (1, 3), (2, 2)):
                    v = PS[:, 4 + b, 0:c * (DV + 1)].rearrange("p (q c) -> p q c", c=DV + 1)
                    ins = V_.tensor_copy(DN[:, 3 * b:3 * b + c], v[:, :, DV])
                link(ins)
                link(V_.scalar_tensor_tensor(DN, DN, -1.0, DN, ALU.mult, ALU.max))
                for d in range(2):
                    m = DN[:, NT * d:NT * d + NT]
                    ins = V_.tensor_tensor(m, m, CG[:, :, 2 + d, h + H2 * d], ALU.max)
                link(ins)
                V_.reciprocal(DN, DN).then_inc(s_hb, 1)
                dve.wait_ge(s_hst, h + 1)
                for i in range(NT):
                    bank = PS[:, 4 + i // 3, (i % 3) * (DV + 1):(i % 3) * (DV + 1) + DV]
                    ins = V_.scalar_tensor_tensor(YM[:, i, h * DV:(h + 1) * DV], bank, DN[:, i:i + 1],
                                                  TMP[:, h % 2, tokens(i)], ALU.mult, ALU.add)
                ins.then_inc(s_hf, 1)
                dve.wait_ge(s_hf, h + 1)

            for n in range(NT * H2 + 1):
                if n < NT * H2:
                    exponents(n)
                if n:
                    weighted(n - 1)
                    if n % NT == 0:
                        state_out(n // NT - 1)
            V_.memset(PAD[:, 1, 0:1], 0.0)
            head_squares(YM, MSS)
            dve.wait_ge(s_gn, 2)
            link(V_.reciprocal(MSS, MSS))
            gated(YM, MSS, AO)
            for n, b in enumerate((4, 5, 6, 7, 0, 1, 2, 3)):
                dve.wait_ge(s_y2h, n + 1)
                V_.scalar_tensor_tensor(YL[:, b, :], pb[b], prm("mnorm" if b < CK else "gnorm", b % CK),
                                        YH[:, b, :].bitcast(F32), ALU.mult, ALU.subtract).then_inc(s_y2l, 1)
            for m in range(DK):
                add_square("post", m // 2, 2, m % 2)

            def add_normed(n, to, mix, gain, m):
                link(V_.scalar_tensor_tensor(mix[:, m, :], mix[:, m, :], prm(gain, m), RS[:], ALU.mult, ALU.mult))
                V_.tensor_tensor(X[:, m, :], X[:, m, :], mix[:, m, :], ALU.add).then_inc(s_x[to].sem, 1)

            norm_reciprocal("post")
            for m in range(DK):
                add_normed("post", "ffn2", MIX, "post2", m)
                if m:
                    low("ffn2", "fpre2", (m - 1) // 2, 2, (m - 1) % 2, AH, AL)
                    add_square("ffn2", (m - 1) // 2, 2, (m - 1) % 2)
            low("ffn2", "fpre2", 3, 2, 1, AH, AL)
            add_square("ffn2", 3, 2, 1)
            ffn("ffn2", "ffn2", "down2")
            norm_reciprocal("fpost")
            for m in range(DK):
                add_normed("fpost", "fpost", MIX2, "fpost2", m)


def _masks(np):
    r = np.arange(P)
    consts = np.zeros((P, 3, P), np.float32)
    consts[:, 0] = np.eye(P)
    consts[:, 1] = 1.0 / D
    consts[:, 2] = r[:, None] // HD == r[None] // HD
    dist = r[:, None] - np.arange(T)[None] + (T - P)
    seen = ((dist <= 128).astype(int) + (dist % 4 == 0) + (dist % 16 == 0)) * (dist >= 0)
    log = np.where(seen > 0, np.log(np.maximum(seen, 1)), -1e30)
    slopes = 2.0 ** -(8.0 * np.arange(1, H1 + 1) / H1)
    bias = (log[:, None] - slopes[None, :, None] * np.maximum(dist, 0)[:, None]).astype(np.float32)
    masks = np.zeros((P, 8, P), np.float32)
    for l, b in enumerate(SMALL):
        masks[:, l] = r[:, None] // (2 * b) == r[None] // (2 * b)
    masks[:, 7] = np.eye(P)
    sel = np.zeros((P, 8, P), np.float32)
    for i in range(8):
        sel[i, i] = -1.0
    neg = np.zeros((P, 2, P), np.float32)
    neg[:, 0] = np.where(r[:, None] <= r[None], 0.0, -1e30)
    neg[:, 1] = np.where(r[:, None] >= r[None], 0.0, -1e30)
    return consts, bias, masks.reshape(P, 8 * P), sel.reshape(P, 8 * P), neg


def _column_units(np, w):
    k, c = w.shape
    return w.reshape(k // P, P, c // P, P).transpose(2, 1, 0, 3).reshape(c // P, P, k)


def _row_units(np, w):
    return w.reshape(4, 2, P, T).transpose(0, 2, 1, 3).reshape(4, P, 2 * T)


def _down_units(np, w):
    k, c = w.shape
    v = w.reshape(k // P, P, c // P, P).transpose(2, 1, 0, 3)
    out = np.zeros((c // P * NS, P, UW), w.dtype)
    a = 0
    for q, n in enumerate(DOWN_TILES):
        out[q::NS, :, 0:n * P] = v[:, :, a:a + n].reshape(c // P, P, n * P)
        a += n
    return out


def _layout(np, a):
    g = lambda n: a[n][0]
    w_in, w2 = g("w_in"), g("w_in_2")
    cb, cc, cx, wq, wk, wv = np.split(w_in, 6, axis=1)
    conv = np.stack([_column_units(np, x) for x in (cc, cx, cb)], axis=1).reshape(12, P, UW)
    gate_up = lambda x, y: np.stack([_column_units(np, x), _column_units(np, y)], axis=1).reshape(2 * FC, P, UW)
    proj = _column_units(np, g("w_ple_proj")).reshape(2, 4, P, 2 * P).transpose(0, 2, 1, 3).reshape(2, P, UW)
    o = np.cumsum([0, 512, 512, 512, 16, 256, 256, 512, 512, 32])
    aqk, av, ao, ag, bq, bk, bv, br, blr = (w2[:, o[i]:o[i + 1]] for i in range(9))
    small = np.zeros((D, P), w2.dtype)
    small[:, 0:4], small[:, 4:8] = ag[:, 0:4], ag[:, 8:12]
    small[:, 32:36], small[:, 36:40] = ag[:, 4:8], ag[:, 12:16]
    small[:, 64:96] = blr
    ubk, ubq = _column_units(np, bk), _column_units(np, bq)
    w = np.concatenate([
        _column_units(np, wq), _column_units(np, wk), _row_units(np, wv), conv, _column_units(np, g("w_out")),
        gate_up(g("w_gate"), g("w_up")), _down_units(np, g("w_down")), _column_units(np, g("w_ple_gate")), proj,
        _column_units(np, small), _row_units(np, bv), ubk[0:1], ubq[0:1], _row_units(np, ao), ubk[1:2], ubq[1:2],
        _column_units(np, aqk), _row_units(np, br), _row_units(np, av), _column_units(np, g("w_out_2")),
        gate_up(g("ffn_w_gate_2"), g("ffn_w_up_2")), _down_units(np, g("ffn_w_down_2"))], axis=0)
    gw = np.zeros((32, H2, 2, HD), w2.dtype)
    for d in range(2):
        gw[16 * d:16 * d + 16, :, d] = g("gla_w2_2")[d].reshape(16, H2, HD)

    prm = np.zeros((P, NPRM), np.float32)

    def put(name, v, rows=slice(0, P)):
        prm[rows, PCOLS[name]:PCOLS[name] + v.shape[1]] = v

    cols = lambda v: v.reshape(-1, P).T
    taps = lambda v: np.concatenate([cols(x) for x in v], axis=1)
    put("eps", np.repeat(np.array([[EPS, HD * EPS, 1.0, 0.0]], np.float32), P, axis=0))
    for name, src in (("g_mix", "g_mix"), ("g_ffn", "g_ffn"), ("g_ple", "g_ple"), ("pre2", "norm_mix_pre_2"),
                      ("post2", "norm_mix_post_2"), ("fpre2", "norm_ffn_pre_2"), ("fpost2", "norm_ffn_post_2"),
                      ("g_oc", "g_out_conv"), ("g_oa", "g_out_attn"), ("cb", "conv_b"), ("mcb", "mlstm_conv_b_2"),
                      ("fcb", "ffn_conv_b"), ("fcb2", "ffn_conv_b_2"), ("mnorm", "mlstm_norm_2"),
                      ("gnorm", "gla_norm_2")):
        put(name, cols(g(src).reshape(-1)))
    for name, src in (("cw", "conv_w"), ("mcw", "mlstm_conv_w_2"), ("fcw", "ffn_conv_w"), ("fcw2", "ffn_conv_w_2")):
        put(name, taps(g(src)))
    put("qg", np.tile(g("q_norm_g"), 2)[:, None])
    put("kg", np.tile(g("k_norm_g"), 2)[:, None])
    put("glab", g("gla_b_2").reshape(2, H2, HD).transpose(0, 2, 1).reshape(P, H2))
    gb = g("mlstm_gate_b_2")
    put("gib", np.concatenate([gb[0:4], gb[8:12]])[:, None], slice(0, 8))
    put("gfb", np.concatenate([gb[4:8], gb[12:16]])[:, None], slice(32, 40))
    return w, gw.reshape(32, H2 * P), prm


def kernel(**inputs):
    import numpy as np
    import concourse.bacc as bacc
    from concourse.bass_utils import run_bass_kernel_spmd

    a = {k: np.asarray(v) for k, v in inputs.items()}
    w, gw, prm = _layout(np, a)
    consts, bias, masks, sel, neg = _masks(np)
    tiles = lambda v: np.ascontiguousarray(v.T.reshape(-1, P, T).transpose(1, 0, 2))
    arrays = {"x": tiles(a["x"][0]), "p": tiles(a["p"][0, 0]), "w": w, "gla_w": gw, "params": prm,
              "consts": consts, "bias": bias, "masks": masks, "selectors": sel, "negmask": neg}
    arrays = {k: np.ascontiguousarray(v) for k, v in arrays.items()}
    nc = bacc.Bacc("TRN2", target_bir_lowering=False, num_devices=1)
    dram = {k: nc.dram_tensor(f"in_{k}", v.shape, F32, kind="ExternalInput").ap() for k, v in arrays.items()}
    out = nc.dram_tensor("out", (P, DK, T), F32, kind="ExternalOutput").ap()
    build(nc, dram, out)
    r = run_bass_kernel_spmd(nc, [{f"in_{k}": v for k, v in arrays.items()}], core_ids=[0])
    y = r.results[0]["out"]
    return y.transpose(1, 0, 2).reshape(D, T).T.reshape(1, T, D)
```

```python
from contextlib import ExitStack

import concourse.bass as bass
from concourse import mybir

F32 = mybir.dt.float32
F32R = mybir.dt.float32r
ALU = mybir.AluOpType
ACT = mybir.ActivationFunctionType

P = 128
T = 512
NT = T // P
D = 1024
DK = D // P
DFF = 2816
FC = DFF // P
CW = 512
CK = CW // P
H1 = 8
HD = 64
H2 = 4
DV = 128
UW = 8 * P
NS = 4
EPS = 1e-6
BIG = (256, 128)
SMALL = (64, 32, 16, 8, 4, 2, 1)

NL = len(BIG) + len(SMALL)

PCOLS = {}


def _param_columns():
    at = 0
    for name, n in (("eps", 4), ("g_mix", DK), ("g_ffn", DK), ("g_ple", DK), ("pre2", DK), ("post2", DK),
                    ("fpre2", DK), ("fpost2", DK), ("g_oc", CK), ("g_oa", CK), ("cw", 3 * CK), ("cb", CK),
                    ("qg", 1), ("kg", 1), ("mcw", 3 * 4), ("mcb", 4), ("mnorm", H2), ("gnorm", H2),
                    ("glab", H2), ("gib", 1), ("gfb", 1), ("fcw", 3 * FC), ("fcb", FC), ("fcw2", 3 * FC),
                    ("fcb2", FC)):
        PCOLS[name] = at
        at += n
    return at


NPRM = _param_columns()

class Stage:

    def __init__(self, sem, base):
        self.sem = sem
        self.base = base


UNITS = {}


def _unit_table():
    at = 0
    for name, n in (("qk", 8), ("v", 4), ("conv", 12), ("wo", 8), ("ffn", 2 * FC), ("down", 32),
                    ("pproj", 2), ("pgate", 8),
                    ("bva", 1), ("small", 1), ("bvb", 3), ("kq0", 2), ("ao", 4), ("kq1", 2), ("aqk", 4), ("br", 4), ("av", 4),
                    ("wo2", 8), ("ffn2", 2 * FC), ("down2", 32)):
        UNITS[name] = (at, n)
        at += n
    return at


NU = _unit_table()
DOWN_TILES = (6, 6, 5, 5)


def tokens(j, n=1):
    return slice(j * P, (j + n) * P)


def build(nc, dram, out, stop=None):
    ctx = ExitStack()
    with ctx:
        base = [(nc.sbuf_base + 63) // 64 * 64]

        def put(name, shape, dt, at=None):
            size = 4
            for s in shape[1:]:
                size *= s
            if at is None:
                at = base[0]
                base[0] += (size + 31) // 32 * 32
            return nc.alloc_sbuf_tensor_at(name, shape, dt, offset=at)

        KB = 1024
        X = put("X", [P, DK, T], F32)
        S_at = base[0]
        SH = put("SH", [P, FC, T], F32R)
        SL = put("SL", [P, FC, T], F32R)
        A_at = base[0]
        AH = put("AH", [P, DK, T], F32R)
        AL = put("AL", [P, DK, T], F32R)
        RAW = put("RAW", [P, NS, UW], F32)
        WH = put("WH", [P, NS, UW], F32R)
        WL = put("WL", [P, NS, UW], F32R)
        TMP_at = base[0]
        TMP = put("TMP", [P, 4, T], F32)
        PAD = put("PAD", [P, 2, T + 2], F32)
        ACC = put("ACC", [P, T], F32)
        SQ = put("SQ", [P, 2, T], F32)
        RS = put("RS", [P, T], F32)
        PRM = put("PRM", [P, NPRM], F32)
        CST = put("CST", [P, 3, P], F32)
        COL = put("COL", [P, 256], F32)
        assert base[0] <= nc.sbuf_usable_end, (base[0], nc.sbuf_usable_end)
        IDENT, INVD, BONE = (CST[:, i, :] for i in range(3))

        YH = put("YH", [P, DK, T], F32R, S_at)
        YL = put("YL", [P, DK, T], F32R, S_at + 16 * KB)
        YC = put("YC", [P, CK, T], F32, S_at + 8 * KB)
        QT = put("QT", [P, CK, T], F32, S_at + 32 * KB)
        KT = put("KT", [P, CK, T], F32, S_at + 40 * KB)
        V = put("V", [P, NT, CW], F32, S_at + 48 * KB)
        BT = put("BT", [P, H1, T], F32, S_at + 56 * KB)
        YA = put("YA", [P, NT, CW], F32, S_at + 72 * KB)
        SC = put("SC", [P, 2, T], F32, S_at + 80 * KB)
        PT = put("PT", [P, 2, T], F32, S_at + 84 * KB)
        RC = COL[:, 252:256]
        MX, NM, DEN, RD = (COL[:, 32 * i:32 * i + 32] for i in range(1, 5))
        YS = COL[:, 160:164]

        PIN = put("PIN", [P, 2, T], F32, TMP_at)
        PH = put("PH", [P, 2, T], F32R, TMP_at + 4 * KB)
        PL = put("PL", [P, 2, T], F32R, TMP_at)
        SG = put("SG", [P, DK, T], F32, S_at + 32 * KB)
        PP = put("PP", [P, DK, T], F32, S_at + 48 * KB)

        GH = put("GH", [P, DK, T], F32R, S_at)
        GL = put("GL", [P, DK, T], F32R, S_at + 16 * KB)
        R = S_at + 32 * KB
        VB = put("VB", [P, NT, CW], F32, R)
        YB = put("YB", [P, H2, T], F32, R + 8 * KB)
        AO = put("AO", [P, NT, CW], F32, R + 16 * KB)
        Q2 = put("Q2", [P, 2, T], F32, R + 24 * KB)
        K2 = put("K2", [P, 2, T], F32, R + 28 * KB)
        XG = put("XG", [P, 2, T], F32, R + 32 * KB)
        SA = put("SA", [P, 2, T], F32, R + 36 * KB)
        QB = put("QB", [P, 2, T], F32, R + 40 * KB)
        KB_ = put("KB", [P, 2, T], F32, R + 44 * KB)
        LM = put("LM", [P, 8 * P], F32, R + 48 * KB)
        AK = put("AK", [P, 2, T], F32, R + 52 * KB)
        QS = put("QS", [P, 7, T], F32, A_at)
        KS = put("KS", [P, 7, T], F32, A_at + 14 * KB)
        AQ = put("AQ", [P, 2, T], F32, A_at + 28 * KB)
        BR = put("BR", [P, NT, CW], F32, A_at)
        VA = put("VA", [P, NT, H2, DV + 1], F32, A_at + 8 * KB)
        YM = put("YM", [P, NT, CW], F32, R + 24 * KB)
        SEL = put("SEL", [P, 8 * P], F32, R + 48 * KB)
        NEG = put("NEG", [P, 2, P], F32, R + 32 * KB)
        WT = put("WT", [P, 2, 2, T], F32, R + 36 * KB)
        MIX = put("MIX", [P, DK, T], F32, S_at + 32 * KB)
        MIX2 = put("MIX2", [P, DK, T], F32, A_at)

        PS = ctx.enter_context(nc.psum_tensor("PS", [P, 8, T], F32))
        pb = [PS[:, i, :] for i in range(8)]

        def sem(name):
            return ctx.enter_context(nc.semaphore(name))

        def prm(name, i=0, rows=slice(0, P)):
            return PRM[rows, PCOLS[name] + i:PCOLS[name] + i + 1]

        def at(t, i, j=0, per=1):
            if isinstance(i, int):
                return t[:, per * i + j, :]
            return t[:, bass.ds(i * per + j, 1), :].rearrange("p o n -> p (o n)")

        def prm_at(name, off, i, per, j):
            c = PCOLS[name] + off + j
            if isinstance(i, int):
                return PRM[:, c + per * i:c + per * i + 1]
            return PRM[:, bass.ds(i * per + c, 1)]

        passed = {nc.scalar.engine: sem("s_act_passed"), nc.gpsimd.engine: sem("s_pool_passed")}

        def ge(eng, s, v, more=0):
            if isinstance(s, Stage):
                s, more = s.sem, more + s.base
            eng.wait_ge(s, v + more)

        def wait(eng, s, i, per, v):
            if not isinstance(i, int):
                ge(eng, s, i * per, v)
                if eng.engine in passed:
                    eng.sem_inc(passed[eng.engine], 1)
            elif per * i + v > 0:
                ge(eng, s, per * i + v)

        CG = COL[:, 0:128].rearrange("p (t g r) -> p t g r", t=NT, g=4)
        BSS, MSS, DN, NRM = COL[:, 128:144], COL[:, 144:160], COL[:, 164:172], COL[:, 172:204]

        CUM = (XG[:, 0, :], XG[:, 1, :], YB[:, 2, :], YB[:, 3, :])
        GATE = ((TMP[:, 2, :], TMP[:, 3, :]), (TMP[:, 0, :], TMP[:, 1, :]),
                (AQ[:, 0, :], AQ[:, 1, :]), (AK[:, 0, :], AK[:, 1, :]))
        KQ = ((TMP[:, 0, :], TMP[:, 1, :]), (AQ[:, 0, :], AK[:, 0, :]))
        ROW = (AQ[0:8, 0, :], AQ[0:8, 1, :], AK[0:8, 0, :], AK[0:8, 1, :])
        MROWS = (PAD[0:8, 1, 0:T], SQ[0:8, 0, :])

        EPS_C, EPS64_C, ONE_C = prm("eps", 0), prm("eps", 1), prm("eps", 2)

        s_raw = [sem(f"s_raw{i}") for i in range(NS)]
        s_hi = sem("s_hi")
        s_split = sem("s_split")
        s_used = sem("s_used")
        s_xin = [sem(f"s_xin{i}") for i in range(4)]
        s_prm = sem("s_prm")
        s_bt = sem("s_bt")
        s_out = sem("s_out")
        s_pad = sem("s_pad")
        s_vc = sem("s_vc")
        s_ac = sem("s_ac")
        ALL = ("mix", "ffn", "ple", "mix2", "post", "ffn2", "fpost")
        SPLIT = tuple(n for n in ALL if n not in ("post", "fpost"))

        def stages(w, names, per):
            s = sem(f"s_{w}")
            return {n: Stage(s, per * i) for i, n in enumerate(names)}

        s_x = stages("x", ("ffn", "ple", "mix2", "ffn2", "fpost"), DK)
        s_gh, s_gl = stages("gh", SPLIT, DK), stages("gl", SPLIT, DK)
        s_sq, s_acc = stages("sq", ALL, DK), stages("acc", ALL, DK)
        s_ms, s_sd, s_rs = stages("ms", ALL, 1), stages("sd", ALL, 1), stages("rs", ALL, 1)
        s_z, s_zsq, s_hms, s_hsd, s_qk = (sem(f"s_{w}") for w in ("z", "zsq", "hms", "hsd", "qk"))
        s_v, s_rc, s_rcd = sem("s_v"), sem("s_rc"), sem("s_rcd")
        s_cuf, s_cx, s_c0, s_yc, s_ycsq, s_ycacc, s_ycms, s_ycsd, s_yn, s_yl = (
            sem(f"s_{w}") for w in ("cuf", "cx", "c0", "yc", "ycsq", "ycacc", "ycms", "ycsd", "yn", "yl"))
        s_s, s_sc, s_nm, s_e, s_pt, s_ptc, s_pv, s_ya, s_yss, s_yan, s_yt, s_yh = (
            sem(f"s_{w}") for w in ("s", "sc", "nm", "e", "pt", "ptc", "pv", "ya", "yss", "yan", "yt", "yh"))
        s_ynh = sem("s_ynh")
        FS = {"ffn": {}, "ffn2": {}}
        for w in ("pad", "t1", "ta", "t3", "act", "up", "h", "sh", "sl"):
            s_chunk = sem(f"s_ffn_{w}")
            FS["ffn"][w], FS["ffn2"][w] = Stage(s_chunk, 0), Stage(s_chunk, FC)
        s_pin, s_ph, s_pl, s_pgt, s_sg, s_pm, s_ppj, s_pp = (
            sem(f"s_{w}") for w in ("pin", "ph", "pl", "pgt", "sg", "pm", "ppj", "pp"))
        DIST = (TMP[:, 2, :], TMP[:, 3, :], ACC[:])
        s_lz = sem("s_lz")
        SBANK = (1, 6)
        PBANK = (2, 3, 7, 1)
        s_mix, s_mix2, s_bcc = sem("s_mix"), sem("s_mix2"), sem("s_bcc")
        (s_sel, s_row, s_rw8, s_gabs, s_stk, s_stt, s_cols, s_dup, s_kqf, s_gpr, s_lax, s_la, s_xg, s_lm) = (
            sem(f"s_{w}") for w in ("sel", "row", "rw8", "gabs", "stk", "stt", "cols", "dup", "kqf", "gpr", "lax",
                                      "la", "xg", "lm"))
        s_vb, s_aof, s_dd, s_ee, s_lv, s_gs, s_gb, s_sad, s_sao, s_go, s_oc, s_ybq = (
            sem(f"s_{w}") for w in ("vb", "aof", "dd", "ee", "lv", "gs", "gb", "sad", "sao", "go", "oc", "ybq"))
        s_apad, s_a1, s_a3, s_aqk, s_br, s_va, s_zero = (
            sem(f"s_{w}") for w in ("apad", "a1", "a3", "aqk", "br", "va", "zero"))
        s_bc, s_ms2, s_ad, s_w, s_sw, s_mo, s_hb, s_hf, s_hst, s_gn, s_y2, s_y2t, s_y2h, s_y2l = (
            sem(f"s_{w}") for w in ("bc", "ms2", "ad", "w", "sw", "mo", "hb", "hf", "hst", "gn", "y2", "y2t",
                                      "y2h", "y2l"))

        block = ctx.enter_context(nc.Block())

        LIMIT = {"mixer1": UNITS["ffn"][0], "block1": UNITS["bva"][0]}.get(stop, NU)

        def runs(u, limit):
            while u < limit:
                if u in (UNITS["down"][0], UNITS["down2"][0]):
                    yield u, 8, [t * P for t in DOWN_TILES]
                    u += 32
                    continue
                end = min(x for x in (UNITS["down"][0], UNITS["down2"][0], limit) if x > u)
                if end - u >= NS:
                    n = (end - u) // NS
                    yield u, n, [UW] * NS
                    u += n * NS
                else:
                    yield u, 1, [UW] * (end - u)
                    u = end

        def each_unit(eng, step, start=0, limit=LIMIT):
            for u0, iters, widths in runs(start, limit):
                n = len(widths)
                first = 1 if u0 == 0 or iters == 1 else 0
                if first:
                    for j in range(n):
                        step(u0, 0, n, j, widths[j])
                    if u0 == 0 and eng.engine == nc.sync.engine:
                        eng.dma_start(BT[:], dram["bias"]).then_inc(s_bt, 16)
                if iters > first:
                    with eng.Fori(first, iters) as i:
                        for j in range(n):
                            step(u0, i, n, j, widths[j])

        @block.sync
        def _(sp):
            for k in range(0, DK, 2):
                sp.dma_start(X[:, k:k + 2, :], dram["x"][:, k:k + 2, :]).then_inc(s_xin[k // 2], 16)
                if k == 0:
                    sp.dma_start(PRM[:], dram["params"]).then_inc(s_prm, 16)
                    sp.dma_start(CST[:], dram["consts"]).then_inc(s_prm, 16)

            def load(u0, i, n, j, width):
                slot = (u0 + j) % NS
                wait(sp, s_split, i, n, u0 + j - NS + 1)
                if isinstance(i, int):
                    src = dram["w"][u0 + j + n * i, :, 0:width]
                else:
                    src = dram["w"][bass.ds(i * n + (u0 + j), 1), :, 0:width].rearrange("o p w -> p (o w)")
                sp.dma_start(RAW[:, slot, 0:width], src).then_inc(s_raw[slot], 16)

            each_unit(sp, load)
            last = {"mixer1": "ffn", "block1": "mix2"}.get(stop, "fpost")
            for k in range(DK):
                ge(sp, s_x[last], k + 1)
                sp.dma_start(out[:, k, :], X[:, k, :]).then_inc(s_out, 16)
            sp.wait_ge(s_out, 16 * DK)

        @block.gpsimd
        def _(pool):
            def split(u0, i, n, j, width):
                slot = (u0 + j) % NS
                wait(pool, s_used, i, n, u0 + j - NS + 1)
                wait(pool, s_raw[slot], i, 16 * n // NS, 16 * ((u0 + j) // NS + 1))
                nc.gpsimd.tensor_scalar(WH[:, slot, 0:width], RAW[:, slot, 0:width], 1.0, 1.0, ALU.mult, ALU.mult).then_inc(s_hi, 1)
                wait(pool, s_hi, i, n, u0 + j + 1)
                nc.gpsimd.tensor_tensor(WL[:, slot, 0:width], RAW[:, slot, 0:width],
                                        WH[:, slot, 0:width].bitcast(F32), ALU.subtract).then_inc(s_split, 1)

            def split_unit(name, n):
                split(UNITS[name][0] + n, 0, NS, 0, UW)

            if stop is not None:
                each_unit(pool, split)
                return
            each_unit(pool, split, 0, UNITS["bva"][0])
            split_unit("bva", 0)
            split_unit("small", 0)
            split_unit("bvb", 0)
            pool.wait_ge(s_used, UNITS["bva"][0])
            for n, (t, name, k) in enumerate(((QS, "bvb", 1), (KS, "bvb", 2), (QB, "kq0", 0), (KB_, "kq0", 1))):
                nc.gpsimd.memset(t[:], 0.0).then_inc(s_lz, 1)
                split_unit(name, k)

            def distance(h, l):
                b = (BIG + SMALL)[l]
                g = NL * h + l
                if l == 0:
                    pool.wait_ge(s_xg, h + 1)
                if g == 0:
                    pool.wait_ge(s_stk, 1)
                if g >= 3:
                    pool.wait_ge(s_lv, g - 2)
                x = CUM[h].rearrange("p (n w) -> p n w", w=2 * b)
                ref = x[:, :, b - 1:b].to_broadcast([P, T // (2 * b), 2 * b])
                nc.gpsimd.tensor_tensor(DIST[g % 3].rearrange("p (n w) -> p n w", w=2 * b), x, ref,
                                        ALU.subtract).then_inc(s_dd, 1)

            split_unit("ao", 0)
            split_unit("ao", 1)
            for l in range(NL):
                distance(0, l)
                if l == 2 or l == 5:
                    split_unit("ao", 2 + l // 5)
            for h, first, second in ((1, (("kq1", 0), ("kq1", 1), ("aqk", 0)), (("aqk", 1), ("aqk", 2))),
                                     (2, (("aqk", 3),), ()),
                                     (3, (("br", 0), ("br", 1)), (("br", 2), ("br", 3)))):
                if h != 2:
                    distance(h, 0)
                    distance(h, 1)
                for u in first:
                    split_unit(*u)
                for l in range(0 if h == 2 else 2, NL):
                    distance(h, l)
                for u in second:
                    split_unit(*u)
            each_unit(pool, split, UNITS["av"][0], NU)

        @block.tensor
        def _(pe):
            def mm3(o, lh, ll, rh, rl, start, stop):
                nc.tensor.matmul(o, lh, rh, start=start, stop=False)
                nc.tensor.matmul(o, lh, rl, start=False, stop=False)
                return nc.tensor.matmul(o, ll, rh, start=False, stop=stop)

            def ready(u):
                pe.wait_ge(s_split, u + 1)

            def col_tiles(u, slots, tiles, o, hi, lo, each=None, start=True, stop=True):
                s = u % NS
                for n, k in zip(slots, tiles):
                    if each is not None:
                        ge(pe, each, k + 1)
                    c = tokens(n)
                    ins = mm3(o, WH[:, s, c], WL[:, s, c], hi[:, k, :], lo[:, k, :],
                              start and n == slots[0], stop and n == slots[-1])
                return ins

            def col_unit(u, o, hi, lo, each=None):
                return col_tiles(u, range(DK), range(DK), o, hi, lo, each)

            def row_unit(u, n, hi, lo, banks=4, each=None):
                s = u % NS
                if each is not None:
                    ge(pe, each, 2 * n + 2)
                for t in range(NT):
                    for kk in range(2):
                        k = 2 * n + kk
                        c = slice(kk * T, (kk + 1) * T)
                        ins = mm3(pb[banks + t], hi[:, k, tokens(t)], lo[:, k, tokens(t)], WH[:, s, c], WL[:, s, c],
                                  k == 0, k == DK - 1)
                return ins

            def statistic(n, with_columns=False, bank=6):
                ge(pe, s_acc[n], DK)
                ins = nc.tensor.matmul(pb[bank], INVD, ACC[:], start=True, stop=True)
                if with_columns:
                    for t in range(NT):
                        ins = nc.tensor.matmul(pb[bank + 1][:, t:t + 1], ACC[:, tokens(t)], INVD[:, 0:1],
                                               start=True, stop=True)
                ins.then_inc(s_ms[n].sem, 1)

            pe.wait_ge(s_prm, 32)
            u0 = UNITS["qk"][0]

            def head_sums(u):
                pe.wait_ge(s_zsq, u + 1)
                if u >= 2:
                    pe.wait_ge(s_hsd, u - 1)
                nc.tensor.matmul(pb[2 + u % 2], BONE, TMP[:, 2 + u % 2, :], start=True, stop=True
                                 ).then_inc(s_hms, 1)

            for u in range(8):
                ready(u0 + u)
                if u >= 2:
                    pe.wait_ge(s_z, u - 1)
                col_unit(u0 + u, pb[u % 2], AH, AL, s_gl["mix"] if u == 0 else None).then_inc(s_used, 1)
                if u == 0:
                    statistic("mix", True)
                if u >= 1:
                    head_sums(u - 1)

            for n in range(4):
                u = UNITS["v"][0] + n
                ready(u)
                if n == 0:
                    ge(pe, s_sd["mix"], 1)
                    pe.wait_ge(s_rcd, 1)
                row_unit(u, n, AH, AL).then_inc(s_used, 1)
                if n == 0:
                    head_sums(7)

            steps = NT * H1

            def score_step(n):
                i, h = NT - 1 - n // H1, n % H1
                w, hp, ht = (i + 1) * P, (h % 2) * HD, h // 2
                if n == 0:
                    pe.wait_ge(s_qk, 8)
                    pe.wait_ge(s_hsd, 8)
                if n >= 2:
                    pe.wait_ge(s_sc, n - 1)
                nc.tensor.matmul(pb[2 + n % 2][:, 0:w], QT[hp:hp + HD, ht, tokens(i)], KT[hp:hp + HD, ht, 0:w],
                                 start=True, stop=True).then_inc(s_s, 1)

            def turn_step(n):
                i = NT - 1 - n // H1
                pe.wait_ge(s_e, n + 1)
                if n == 0:
                    pe.wait_ge(s_v, NT)
                if n >= 2:
                    pe.wait_ge(s_ptc, n - 1)
                for j in range(i + 1):
                    ins = nc.tensor.transpose(pb[4 + n % 2][:, tokens(j)], SC[:, n % 2, tokens(j)], IDENT)
                ins.then_inc(s_pt, 1)

            def value_step(n):
                i, h = NT - 1 - n // H1, n % H1
                pe.wait_ge(s_ptc, n + 1)
                if n >= 2:
                    pe.wait_ge(s_ya, n - 1)
                for j in range(i + 1):
                    ins = nc.tensor.matmul(pb[6 + n % 2][:, 0:HD], PT[:, n % 2, tokens(j)],
                                           V[:, j, h * HD:(h + 1) * HD], start=(j == 0), stop=(j == i))
                ins.then_inc(s_pv, 1)

            for n in range(steps + 2):
                if n < steps:
                    score_step(n)
                    for t in range(3 * n, 3 * n + 3):
                        cu, k = divmod(t, DK)
                        u = UNITS["conv"][0] + cu
                        if k == 0:
                            ready(u)
                            if cu == 0:
                                pe.wait_ge(s_z, 8)
                            if cu >= 2:
                                pe.wait_ge(s_cuf, cu - 1)
                        ins = mm3(pb[cu % 2], WH[:, u % NS, tokens(k)], WL[:, u % NS, tokens(k)],
                                  AH[:, k, :], AL[:, k, :], k == 0, k == DK - 1)
                        if k == DK - 1:
                            ins.then_inc(s_used, 1)
                if 1 <= n <= steps:
                    turn_step(n - 1)
                if n >= 2:
                    value_step(n - 2)

            pe.wait_ge(s_ycacc, CK)
            pe.wait_ge(s_cuf, 12)
            nc.tensor.matmul(pb[0], INVD, ACC[:], start=True, stop=True).then_inc(s_ycms, 1)
            pe.wait_ge(s_ptc, steps)
            pe.wait_ge(s_ya, steps)
            for i in range(NT):
                pe.wait_ge(s_yan, i + 1)
                for b in range(CK):
                    ins = nc.tensor.transpose(pb[4 + b][:, tokens(i)], YA[:, i, tokens(b)], IDENT)
            ins.then_inc(s_yt, 1)

            def out_projection(name, each, free):
                for m in range(DK):
                    u = UNITS[name][0] + m
                    ready(u)
                    if m >= 2:
                        ge(pe, free, m - 1)
                    col_unit(u, pb[m % 2], YH, YL, each if m == 0 else None).then_inc(s_used, 1)

            pe.wait_ge(s_ycsd, 1)
            out_projection("wo", s_yl, s_x["ffn"])
            if stop == "mixer1":
                return

            def ffn(f, norm, down, free):
                S, u0 = FS[f], UNITS[f][0]
                statistic(norm)
                ge(pe, s_gl[norm], DK)

                def chunks(i):
                    for j in range(2):
                        for w, s in enumerate((S["pad"], S["up"])):
                            u = u0 + 2 * j + w
                            wait(pe, s_split, i, NS, u + 1)
                            wait(pe, s, i, 2, j - 1)
                            col_unit(u, pb[2 * j + w], AH, AL).then_inc(s_used, 1)

                chunks(0)
                with pe.Fori(1, FC // 2) as i:
                    chunks(i)

                u0 = UNITS[down][0]

                def down_pair(i):
                    for j in range(2):
                        k0 = 0
                        wait(pe, free, i, 2, j - 1)
                        for q, nt in enumerate(DOWN_TILES):
                            u = u0 + NS * j + q
                            wait(pe, s_split, i, 2 * NS, u + 1)
                            if q == 3 and isinstance(i, int) and j == 0:
                                ge(pe, S["sl"], FC)
                            ins = col_tiles(u, range(nt), range(k0, k0 + nt), pb[4 + j], SH, SL,
                                            start=(q == 0), stop=(q == 3))
                            ins.then_inc(s_used, 1)
                            k0 += nt

                ge(pe, S["sl"], FC - 1)
                down_pair(0)
                with pe.Fori(1, DK // 2) as i:
                    down_pair(i)

            ffn("ffn", "ffn", "down", s_x["ple"])

            pe.wait_ge(s_pl, 2)
            for m in range(DK):
                u = UNITS["pproj"][0] + m // 4
                ready(u)
                if m >= 4:
                    pe.wait_ge(s_pp, m - 3)
                ins = col_tiles(u, range(2 * (m % 4), 2 * (m % 4) + 2), range(2), pb[PBANK[m % 4]], PH, PL)
                if m % 4 == 3:
                    ins.then_inc(s_used, 1)
                else:
                    ins.then_inc(s_ppj, 1)
                if m == 3:
                    statistic("ple")
            for m in range(DK):
                u = UNITS["pgate"][0] + m
                ready(u)
                if m == 1:
                    pe.wait_ge(s_pp, DK)
                if m >= 2:
                    pe.wait_ge(s_pgt, m - 1)
                col_unit(u, pb[m % 2], AH, AL, s_gl["ple"] if m == 0 else None).then_inc(s_used, 1)
            if stop == "block1":
                return

            def key_query_units(pair, bank):
                for n in range(2):
                    u = UNITS[f"kq{pair}"][0] + n
                    ready(u)
                    col_unit(u, pb[bank + n], GH, GL).then_inc(s_used, 1)

            def decay_gates(pair, bank):
                for n in range(2):
                    h = 2 * pair + n
                    nc.tensor.matmul(pb[bank + n], SQ[64:96, 1, h * P:(h + 1) * P], SQ[64:96, 0, :],
                                     start=True, stop=True).then_inc(s_gpr, 1)

            u = UNITS["bva"][0]
            ready(u)
            ge(pe, s_sd["ple"], 1)
            row_unit(u, 0, GH, GL, each=s_gl["mix2"]).then_inc(s_used, 1)
            u = UNITS["small"][0]
            ready(u)
            pe.wait_ge(s_pgt, DK)
            col_unit(u, pb[0], GH, GL, s_gl["mix2"]).then_inc(s_used, 1)
            statistic("mix2", True, bank=2)
            for n in range(1, 4):
                u = UNITS["bvb"][0] + n - 1
                ready(u)
                row_unit(u, n, GH, GL).then_inc(s_used, 1)
                if n == 1:
                    pe.wait_ge(s_row, 1)
                    pe.wait_ge(s_sel, 16)
                    ge(pe, s_sd["mix2"], 1)
                    pe.wait_ge(s_rcd, 2)
                    decay_gates(0, 2)
                if n == 2:
                    pe.wait_ge(s_lax, 2)
                    decay_gates(1, 2)
            pe.wait_ge(s_row, 1)
            key_query_units(0, 0)
            pe.wait_ge(s_vb, NT)
            for n in range(4):
                u = UNITS["ao"][0] + n
                ready(u)
                row_unit(u, n, GH, GL).then_inc(s_used, 1)
            pe.wait_ge(s_stk, 1)
            pe.wait_ge(s_lax, 4)
            for t in range(NT):
                ins = nc.tensor.transpose(pb[3][:, tokens(t)], SA[:, 0, tokens(t)], IDENT)
            ins.then_inc(s_stt, 1)

            def level_step(h, j):
                n = NT * h + j
                if j == 0:
                    pe.wait_ge(s_lv, NL * (h + 1))
                    if h == 0:
                        pe.wait_ge(s_dup, 2)
                if n == 1:
                    pe.wait_ge(s_aof, NT)
                if n >= 2:
                    pe.wait_ge(s_sad, n - 1)
                for l in range(8):
                    k, q = (KS[:, l, tokens(j)], QS[:, l, tokens(j)]) if l < 7 else \
                        (K2[:, h % 2, tokens(j)], Q2[:, h % 2, tokens(j)])
                    ins = nc.tensor.matmul(PS[:, SBANK[n % 2] + l // 4, (l % 4) * P:(l % 4 + 1) * P], k, q,
                                           start=True, stop=True)
                ins.then_inc(s_gs, 1)
                if n:
                    pe.wait_ge(s_sao, n)
                for l, tiles in ((0, slice(2 * P, T) if j < 2 else slice(0, 2 * P)), (1, tokens(j ^ 1))):
                    ins = nc.tensor.matmul(pb[0][:, tiles], KB_[:, l, tokens(j)], QB[:, l, tiles],
                                           start=True, stop=True)
                ins.then_inc(s_gb, 1)

            def mix_step(h, j):
                n = NT * h + j
                pe.wait_ge(s_sad, n + 1)
                pe.wait_ge(s_sao, n + 1)
                if j == 0:
                    if h:
                        pe.wait_ge(s_oc, h)
                    else:
                        pe.wait_ge(s_cols, 1)
                for i in range(NT):
                    ins = nc.tensor.matmul(pb[3][:, tokens(i)], SA[:, j % 2, tokens(i)],
                                           VB[:, j, h * DV:(h + 1) * DV], start=(i == 0 and j == 0),
                                           stop=(i == NT - 1 and j == NT - 1), skip_group_check=True)
                ins.then_inc(s_go, 1)

            for h in range(H2):
                if h == 1:
                    key_query_units(1, 4)
                if h >= 2:
                    for m in range(2 * h - 4, 2 * h - 2):
                        u = UNITS["aqk"][0] + m
                        ready(u)
                        if m < 2:
                            pe.wait_ge(s_dup, 4)
                        else:
                            pe.wait_ge(s_apad, m - 1)
                        col_unit(u, pb[4 + m % 2], GH, GL).then_inc(s_used, 1)
                for j in range(NT + 1):
                    if j < NT:
                        level_step(h, j)
                    if j:
                        mix_step(h, j - 1)

            for name, done in (("br", None), ("av", s_br)):
                for n in range(4):
                    u = UNITS[name][0] + n
                    ready(u)
                    if n == 0:
                        pe.wait_ge(s_apad, 4)
                        pe.wait_ge(s_sad, NT * H2)
                        if done is not None:
                            pe.wait_ge(done, NT)
                    row_unit(u, n, GH, GL).then_inc(s_used, 1)

            def state_bank(d, i):
                n = NT * d + i
                return PS[:, 4 + n // 3, (n % 3) * (DV + 1):(n % 3 + 1) * (DV + 1)]

            def lstm_scores(n):
                h, j = divmod(n, NT)
                hp, ht = (h % 2) * HD, h // 2
                if j == 0:
                    if h == 0:
                        pe.wait_ge(s_zero, 32)
                        pe.wait_ge(s_sad, 4 * NT)
                        pe.wait_ge(s_sao, 4 * NT)
                    else:
                        pe.wait_ge(s_bcc, 2 * h)
                    for d in range(2):
                        r = h + H2 * d
                        ins = nc.tensor.matmul(pb[d], SEL[0:8, r * P:(r + 1) * P], MROWS[d],
                                               start=True, stop=True)
                    ins.then_inc(s_bc, 1)
                if n == 0:
                    pe.wait_ge(s_aqk, 4)
                    pe.wait_ge(s_oc, H2)
                if n >= 2:
                    pe.wait_ge(s_sw, 2 * (n - 1))
                nc.tensor.matmul(pb[2 + n % 2], AK[hp:hp + HD, ht, tokens(j)], AQ[hp:hp + HD, ht, :],
                                 start=True, stop=True).then_inc(s_ms2, 1)

            def lstm_mix(n):
                h, j = divmod(n, NT)
                if n == 0:
                    pe.wait_ge(s_va, NT + 1)
                if j == 0 and h:
                    pe.wait_ge(s_hf, h)
                for d in range(2):
                    pe.wait_ge(s_sw, 2 * n + d + 1)
                    tiles = range(j, NT) if d == 0 else range(0, j + 1)
                    for i in tiles:
                        m = NT * d + i
                        first = j == (0 if d == 0 else i) and m % 3 == 0
                        ins = nc.tensor.matmul(state_bank(d, i), WT[:, n % 2, d, tokens(i)], VA[:, j, h, :],
                                               start=first, stop=(j == NT - 1), skip_group_check=True)
                ins.then_inc(s_mo, 1)

            for n in range(NT * H2 + 1):
                if n < NT * H2:
                    lstm_scores(n)
                if n:
                    lstm_mix(n - 1)

            pe.wait_ge(s_hf, H2)
            pe.wait_ge(s_w, 2 * NT * H2)
            for b in (4, 5, 6, 7, 0, 1, 2, 3):
                pe.wait_ge(s_y2, 1 if b >= CK else 2)
                for i in range(NT):
                    src = YM[:, i, tokens(b)] if b < CK else YB[:, b - CK, tokens(i)]
                    ins = nc.tensor.transpose(pb[b][:, tokens(i)], src, IDENT)
                ins.then_inc(s_y2t, 1)
            pe.wait_ge(s_y2l, DK)
            out_projection("wo2", s_y2l, s_mix)
            statistic("post")
            ffn("ffn2", "ffn2", "down2", s_mix2)
            statistic("fpost")
        @block.scalar
        def _(act):
            n_ac = [0]

            def link(ins):
                n_ac[0] += 1
                ins.then_inc(s_ac, 1)
                act.wait_ge(s_ac, n_ac[0])

            A = nc.scalar.activation

            def norm_tile(n, gain, i, per, j, hi, x=None, split=True):
                k = per * i + j if isinstance(i, int) else None
                src = at(X if x is None else x, i, j, per)
                if split:
                    wait(act, s_x[n], i, per, j + 1)
                    A(at(hi, i, j, per), src, ACT.Copy, scale=prm_at(gain, 0, i, per, j)).then_inc(s_gh[n].sem, 1)
                wait(act, s_acc[n], i, per, j - 1)
                A(SQ[:, j % 2, :], src, ACT.Square).then_inc(s_sq[n].sem, 1)

            def norm_root(n, bank=6):
                ge(act, s_ms[n], 1)
                A(RS[:], pb[bank], ACT.Sqrt, bias=EPS_C).then_inc(s_sd[n].sem, 1)

            act.wait_ge(s_prm, 32)
            for k in range(DK):
                if k % 2 == 0:
                    act.wait_ge(s_xin[k // 2], 16)
                A(AH[:, k, :], X[:, k, :], ACT.Copy, scale=prm("g_mix", k)).then_inc(s_gh["mix"].sem, 1)
                if k >= 2:
                    ge(act, s_acc["mix"], k - 1)
                A(SQ[:, k % 2, :], X[:, k, :], ACT.Square).then_inc(s_sq["mix"].sem, 1)
            norm_root("mix")
            A(RC, pb[7][:, 0:NT], ACT.Sqrt, bias=EPS_C).then_inc(s_rcd, 1)

            def head_root(u):
                act.wait_ge(s_hms, u + 1)
                q = u < CK
                A(SC[:, u % 2, :], pb[2 + u % 2], ACT.Sqrt, bias=EPS64_C if q else EPS_C,
                  scale=1.0 if q else 1.0 / HD).then_inc(s_hsd, 1)

            for u in range(8):
                act.wait_ge(s_z, u + 1)
                if u >= 2:
                    act.wait_ge(s_hms, u - 1)
                A(TMP[:, 2 + u % 2, :], TMP[:, u % 2, :], ACT.Square).then_inc(s_zsq, 1)
                if u >= 1:
                    if u >= 3:
                        act.wait_ge(s_qk, u - 2)
                    head_root(u - 1)
            act.wait_ge(s_qk, 6)
            head_root(7)
            act.wait_ge(s_rc, 1)
            act.wait_ge(s_used, UNITS["v"][0] + 4)
            for t in range(NT):
                A(V[:, t, :], pb[4 + t], ACT.Copy, scale=RC[:, t:t + 1]).then_inc(s_v, 1)

            def conv_first(j):
                act.wait_ge(s_cx, j + 1)
                if j == 0:
                    act.wait_ge(s_qk, 8)
                    act.wait_ge(s_hms, 8)
                if j >= 1:
                    act.wait_ge(s_yc, j)
                A(TMP[:, 2, :], PAD[:, 0, 0:T], ACT.Identity, bias=prm("cb", j), scale=prm("cw", j)
                  ).then_inc(s_c0, 1)

            def conv_square(j):
                act.wait_ge(s_yc, j + 1)
                if j == 0:
                    ge(act, s_ms["mix"], 1)
                if j >= 2:
                    act.wait_ge(s_ycacc, j - 1)
                A(SQ[:, j % 2, :], YC[:, j, :], ACT.Square).then_inc(s_ycsq, 1)

            steps = NT * H1
            for n in range(steps + 1):
                if n < steps:
                    w = (NT - n // H1) * P
                    act.wait_ge(s_nm, n + 1)
                    A(SC[:, n % 2, 0:w], SC[:, n % 2, 0:w], ACT.Exp, bias=NM[:, n:n + 1],
                      accum_out=DEN[:, n:n + 1]).then_inc(s_e, 1)
                if n >= 1:
                    m = n - 1
                    w = (NT - m // H1) * P
                    act.wait_ge(s_pt, m + 1)
                    if m >= 2:
                        act.wait_ge(s_pv, m - 1)
                    A(PT[:, m % 2, 0:w], pb[4 + m % 2][:, 0:w], ACT.Copy).then_inc(s_ptc, 1)
                if n % 8 == 6:
                    conv_first(n // 8)
                if n % 8 == 1 and n > 8:
                    conv_square(n // 8 - 1)
            conv_square(3)
            act.wait_ge(s_ya, steps)
            act.wait_ge(s_ycacc, CK)
            for i in range(NT):
                A(SQ[:, 0, :], YA[:, i, :], ACT.Square, accum_out=YS[:, i:i + 1]).then_inc(s_yss, 1)
                act.wait_ge(s_yss, i + 1)
            link(A(YS, YS, ACT.Sqrt, bias=EPS_C, scale=1.0 / CW))
            act.wait_ge(s_ycms, 1)
            A(TMP[:, 3, :], pb[0], ACT.Sqrt, bias=EPS_C, scale=float(D) / CW).then_inc(s_ycsd, 1)
            for j in range(CK):
                act.wait_ge(s_yn, j + 1)
                A(YH[:, j, :], SC[:, j % 2, :], ACT.Copy).then_inc(s_ynh, 1)
            act.wait_ge(s_yt, 1)
            act.wait_ge(s_yl, CK)
            for b in range(CK):
                A(YH[:, CK + b, :], pb[4 + b], ACT.Copy, scale=prm("g_oa", b)).then_inc(s_yh, 1)
            def x_tiles(n, gain, hi):
                for m in range(DK):
                    norm_tile(n, gain, m // 2, 2, m % 2, hi)

            x_tiles("ffn", "g_ffn", AH)
            if stop == "mixer1":
                return

            def ffn(f, norm, func, down):
                S = FS[f]
                norm_root(norm)

                def chunk(i, j):
                    wait(act, S["pad"], i, 2, j + 1)
                    wait(act, S["h"], i, 2, j - 1)
                    A(TMP[:, j, :], PAD[:, j, 0:T], ACT.Identity, bias=prm_at("fcb" + sfx, 0, i, 2, j),
                      scale=prm_at("fcw" + sfx, 0, i, 2, j)).then_inc(S["t1"].sem, 1)
                    wait(act, S["t3"], i, 2, j + 1)
                    A(TMP[:, j, :], TMP[:, j, :], func).then_inc(S["act"].sem, 1)
                    wait(act, S["h"], i, 2, j + 1)
                    A(at(SH, i, j, 2), TMP[:, 2 + j, :], ACT.Copy).then_inc(S["sh"].sem, 1)

                sfx = "" if f == "ffn" else "2"
                for j in range(2):
                    chunk(0, j)
                with act.Fori(1, FC // 2) as i:
                    for j in range(2):
                        chunk(i, j)

                u0 = UNITS[down][0]
                if f == "ffn":
                    ge(act, S["sl"], FC)
                    act.dma_start(PIN[:], dram["p"]).then_inc(s_pin, 16)
                    act.wait_ge(s_pin, 16)
                    for q in range(2):
                        A(PH[:, q, :], PIN[:, q, :], ACT.Copy).then_inc(s_ph, 1)

                def tile(i, j):
                    if f == "ffn":
                        norm_tile("ple", "g_ple", i, 2, j, AH)
                    else:
                        wait(act, s_used, i, 2 * NS, u0 + NS * (j + 1))
                        A(at(MIX2, i, j, 2), pb[4 + j], ACT.Copy).then_inc(s_mix2, 1)
                        wait(act, s_mix2, i, 2, j + 1)
                        norm_tile("fpost", None, i, 2, j, None, x=MIX2, split=False)

                for j in range(2):
                    tile(0, j)
                with act.Fori(1, DK // 2) as i:
                    for j in range(2):
                        tile(i, j)

            ffn("ffn", "ffn", ACT.Silu, "down")

            for m in range(DK):
                if m % 4 == 3:
                    act.wait_ge(s_used, UNITS["pproj"][0] + m // 4 + 1)
                else:
                    act.wait_ge(s_ppj, m - m // 4 + 1)
                A(PP[:, m, :], pb[PBANK[m % 4]], ACT.Copy).then_inc(s_pp, 1)
                if m == 3:
                    norm_root("ple")
            for m in range(DK + 2):
                if m < DK:
                    act.wait_ge(s_pgt, m + 1)
                    A(SG[:, m, :], TMP[:, m % 2, :], ACT.Sigmoid).then_inc(s_sg, 1)
                if m >= 2:
                    norm_tile("mix2", "pre2", (m - 2) // 2, 2, m % 2, GH)
            if stop == "block1":
                return

            norm_root("mix2", 2)
            ge(act, s_acc["mix2"], DK)
            act.dma_start(SQ[64:96, 1, :], dram["gla_w"]).then_inc(s_sel, 16)
            A(RC, pb[3][:, 0:NT], ACT.Sqrt, bias=EPS_C).then_inc(s_rcd, 1)
            act.wait_ge(s_row, 1)
            rows = slice(0, 8)
            A(ROW[0], SQ[rows, 0, :], ACT.Identity, bias=prm("gib", 0, rows)).then_inc(s_gabs, 1)
            link(A(ROW[1], SQ[32:40, 0, :], ACT.Identity, bias=prm("gfb", 0, slice(32, 40))))
            link(A(ROW[2], ROW[1], ACT.Abs))
            link(A(ROW[2], ROW[2], ACT.Exp, scale=-1.0))
            A(ROW[2], ROW[2], ACT.Ln, bias=ONE_C[rows]).then_inc(s_rw8, 1)

            def stack_rows():
                act.wait_ge(s_gabs, 2)
                for g, src in enumerate((ROW[2], ROW[1], SQ[rows, 1, :], ACC[rows, :])):
                    ins = A(SA[32 * g:32 * g + 8, 0, :], src, ACT.Copy)
                ins.then_inc(s_stk, 1)

            def gate_columns():
                act.wait_ge(s_stt, 1)
                link(A(CG, pb[3].rearrange("p (t g r) -> p t g r", t=NT, g=4)[:, :, :, 0:8], ACT.Copy))
                A(CG[:, :, 2:4, :], CG[:, :, 2:4, :], ACT.Exp, scale=-1.0).then_inc(s_cols, 1)

            def duplicate(h):
                pair, hh = divmod(h, 2)
                if pair:
                    act.wait_ge(s_gs, NT * (h - 1))
                for n, dst in enumerate((K2, Q2)):
                    act.wait_ge(s_dup, 2 * pair + n + 1)
                    for half in range(2):
                        ins = A(dst[half * HD:(half + 1) * HD, hh, :], KQ[pair][n][hh * HD:(hh + 1) * HD],
                                ACT.Copy, scale=0.125 if n else 1.0)
                    ins.then_inc(s_kqf, 1)

            def gate_log(h):
                gate, log = GATE[h]
                act.wait_ge(s_gpr, h + 1)
                link(A(gate, pb[2 + h % 2], ACT.Identity, bias=prm("glab", h)))
                link(A(log, gate, ACT.Abs))
                link(A(log, log, ACT.Exp, scale=-1.0))
                A(log, log, ACT.Ln, bias=ONE_C).then_inc(s_lax, 1)

            gate_log(0)
            gate_log(1)
            act.wait_ge(s_rc, 2)
            act.wait_ge(s_used, UNITS["bvb"][0] + 3)
            for t in range(NT):
                A(VB[:, t, :], pb[4 + t], ACT.Copy, scale=RC[:, t:t + 1]).then_inc(s_vb, 1)
            stack_rows()
            for h in (2, 3):
                act.wait_ge(s_stk, 1)
                gate_log(h)
            act.wait_ge(s_xg, 2)
            duplicate(0)
            duplicate(1)
            act.dma_start(LM[:], dram["masks"]).then_inc(s_lm, 16)

            def decay_step(h, l):
                g, b = NL * h + l, (BIG + SMALL)[l]
                act.wait_ge(s_dd, g + 1)
                d = DIST[g % 3].rearrange("p (n s w) -> p n s w", s=2, w=b)
                A(d[:, :, 0, :], d[:, :, 0, :], ACT.Exp, scale=-1.0 / 16.0)
                A(d[:, :, 1, :], d[:, :, 1, :], ACT.Exp, scale=1.0 / 16.0).then_inc(s_ee, 1)

            def conv_pair(m):
                dst = (AQ if m < 2 else AK)[:, m % 2, :]
                act.wait_ge(s_apad, m + 1)
                A(dst, PAD[:, 0, 0:T], ACT.Identity, bias=prm("mcb", m), scale=prm("mcw", m)).then_inc(s_a1, 1)
                act.wait_ge(s_a3, m + 1)
                A(dst, dst, ACT.Silu).then_inc(s_aqk, 1)

            for h in range(H2):
                for l in range(NL):
                    decay_step(h, l)
                if h == 0:
                    gate_columns()
                    act.wait_ge(s_used, UNITS["ao"][0] + 4)
                    for t in range(NT):
                        A(AO[:, t, :], pb[4 + t], ACT.Sigmoid, scale=RC[:, t:t + 1]).then_inc(s_aof, 1)
                if h == 1:
                    duplicate(2)
                if h >= 2:
                    for m in range(2 * h - 4, 2 * h - 2):
                        conv_pair(m)
                for j in range(NT):
                    n = NT * h + j
                    act.wait_ge(s_gb, n + 1)
                    if n >= 2:
                        act.wait_ge(s_go, n - 1)
                    parts = [c for c in (slice(0, j * P), slice((j + 1) * P, T)) if c.stop > c.start]
                    for c in parts:
                        ins = A(SA[:, j % 2, c], pb[0][:, c], ACT.Copy)
                    ins.then_inc(s_sao, 1)
                act.wait_ge(s_go, NT * (h + 1))
                act.wait_ge(s_lv, NL * min(h + 1, H2))
                A(YB[:, h, :], pb[3], ACT.Copy).then_inc(s_oc, 1)
                if h == 1:
                    duplicate(3)

            act.wait_ge(s_used, UNITS["br"][0] + 4)
            for t in range(NT):
                A(BR[:, t, :], pb[4 + t], ACT.Silu, scale=RC[:, t:t + 1]).then_inc(s_br, 1)
            act.wait_ge(s_sad, 4 * NT)
            act.wait_ge(s_lv, 36)
            act.dma_start(SEL[:], dram["selectors"]).then_inc(s_zero, 16)
            act.dma_start(NEG[:], dram["negmask"]).then_inc(s_zero, 16)
            act.wait_ge(s_ybq, 1)
            link(A(BSS, BSS, ACT.Sqrt, bias=EPS_C, scale=1.0 / DV))
            A(BSS, BSS, ACT.Copy).then_inc(s_gn, 1)
            act.wait_ge(s_used, UNITS["av"][0] + 4)
            for t in range(NT):
                A(VA[:, t, :, 0:DV], pb[4 + t].rearrange("p (h c) -> p h c", h=H2), ACT.Copy,
                  scale=RC[:, t:t + 1]).then_inc(s_va, 1)

            for n in range(NT * H2 + 1):
                if n < NT * H2:
                    h, j = divmod(n, NT)
                    if j == 0:
                        act.wait_ge(s_bc, h + 1)
                        act.wait_ge(s_ybq, 1)
                        if h:
                            act.wait_ge(s_ad, 2 * n)
                            act.wait_ge(s_w, 2 * n)
                        for d in range(2):
                            A(TMP[:, 2 + d, :], pb[d], ACT.Copy).then_inc(s_bcc, 1)
                        act.wait_ge(s_bcc, 2 * h + 2)
                    for d in range(2):
                        c = CG[:, j, d, h + H2 * d:h + H2 * d + 1]
                        act.wait_ge(s_ad, 2 * n + d + 1)
                        off = slice((j + 1) * P, T) if d == 0 else slice(0, j * P)
                        if off.stop > off.start:
                            A(WT[:, n % 2, d, off], TMP[:, 2 + d, off], ACT.Exp, bias=c)
                        A(WT[:, n % 2, d, tokens(j)], WT[:, n % 2, d, tokens(j)], ACT.Exp).then_inc(s_w, 1)
                if n and n % NT == 0:
                    h = n // NT - 1
                    act.wait_ge(s_hb, h + 1)
                    for i in range(NT):
                        m = NT + i
                        bank = PS[:, 4 + m // 3, (m % 3) * (DV + 1):(m % 3) * (DV + 1) + DV]
                        ins = A(TMP[:, h % 2, tokens(i)], bank, ACT.Copy, scale=DN[:, m:m + 1])
                    ins.then_inc(s_hst, 1)
            act.wait_ge(s_ybq, 2)
            link(A(MSS, MSS, ACT.Sqrt, bias=EPS_C, scale=1.0 / DV))
            A(MSS, MSS, ACT.Copy).then_inc(s_gn, 1)
            for n, b in enumerate((4, 5, 6, 7, 0, 1, 2, 3)):
                act.wait_ge(s_y2t, n + 1)
                A(YH[:, b, :], pb[b], ACT.Copy, scale=prm("mnorm" if b < CK else "gnorm", b % CK)
                  ).then_inc(s_y2h, 1)

            for m in range(DK):
                act.wait_ge(s_used, UNITS["wo2"][0] + m + 1)
                A(MIX[:, m, :], pb[m % 2], ACT.Copy).then_inc(s_mix, 1)
                act.wait_ge(s_mix, m + 1)
                norm_tile("post", None, m // 2, 2, m % 2, None, x=MIX, split=False)
            norm_root("post")
            x_tiles("ffn2", "fpre2", AH)
            ffn("ffn2", "ffn2", ACT.Gelu_apprx_tanh, "down2")
            norm_root("fpost")

        @block.vector
        def _(dve):
            V_ = nc.vector
            n_vc = [0]

            def link(ins):
                n_vc[0] += 1
                ins.then_inc(s_vc, 1)
                dve.wait_ge(s_vc, n_vc[0])

            def low(n, gain, i, per, j, hi, lo):
                wait(dve, s_gh[n], i, per, j + 1)
                V_.scalar_tensor_tensor(at(lo, i, j, per), at(X, i, j, per), prm_at(gain, 0, i, per, j),
                                        at(hi, i, j, per).bitcast(F32), ALU.mult, ALU.subtract
                                        ).then_inc(s_gl[n].sem, 1)

            def add_square(n, i, per, j):
                wait(dve, s_sq[n], i, per, j + 1)
                if isinstance(i, int) and i == 0 and j == 0:
                    V_.tensor_copy(ACC[:], SQ[:, 0, :]).then_inc(s_acc[n].sem, 1)
                else:
                    wait(dve, s_acc[n], i, per, j)
                    V_.tensor_tensor(ACC[:], ACC[:], SQ[:, j % 2, :], ALU.add).then_inc(s_acc[n].sem, 1)

            def norm_reciprocal(n, columns=0):
                ge(dve, s_sd[n], 1)
                V_.reciprocal(RS[:], RS[:]).then_inc(s_rs[n].sem, 1)
                ge(dve, s_rs[n], 1)
                if columns:
                    dve.wait_ge(s_rcd, columns)
                    V_.reciprocal(RC, RC).then_inc(s_rc, 1)

            link(V_.memset(PAD[:], 0.0))
            dve.wait_ge(s_prm, 32)
            for k in range(DK):
                low("mix", "g_mix", k // 2, 2, k % 2, AH, AL)
                add_square("mix", k // 2, 2, k % 2)
            norm_reciprocal("mix", 1)
            gq = UNITS["qk"][0]

            def normed(u):
                dve.wait_ge(s_hsd, u + 1)
                r = SC[:, u % 2, :]
                link(V_.reciprocal(r, r))
                V_.scalar_tensor_tensor((QT if u < CK else KT)[:, u % CK, :], TMP[:, u % 2, :],
                                        prm("qg" if u < CK else "kg"), r, ALU.mult, ALU.mult).then_inc(s_qk, 1)

            for u in range(8):
                dve.wait_ge(s_used, gq + u + 1)
                if u >= 2:
                    normed(u - 2)
                    dve.wait_ge(s_qk, u - 1)
                    dve.wait_ge(s_zsq, u - 1)
                V_.tensor_tensor(TMP[:, u % 2, :], pb[u % 2], RS[:], ALU.mult).then_inc(s_z, 1)
            for u in (6, 7):
                normed(u)

            uc = UNITS["conv"][0]

            def conv_c(j):
                dve.wait_ge(s_used, uc + 3 * j + 1)
                V_.tensor_tensor(TMP[:, 0, :], pb[(3 * j) % 2], RS[:], ALU.mult).then_inc(s_cuf, 1)

            def conv_x(j):
                dve.wait_ge(s_used, uc + 3 * j + 2)
                V_.tensor_tensor(TMP[:, 1, :], pb[(3 * j + 1) % 2], RS[:], ALU.mult).then_inc(s_cuf, 1)
                dve.wait_ge(s_cuf, 3 * j + 2)
                V_.tensor_tensor(PAD[:, 0, 2:T + 2], TMP[:, 0, :], TMP[:, 1, :], ALU.mult).then_inc(s_cx, 1)

            def conv_b(j):
                dve.wait_ge(s_c0, j + 1)
                t = TMP[:, 2, :]
                link(V_.scalar_tensor_tensor(t, PAD[:, 0, 1:T + 1], prm("cw", CK + j), t, ALU.mult, ALU.add))
                link(V_.scalar_tensor_tensor(t, PAD[:, 0, 2:T + 2], prm("cw", 2 * CK + j), t, ALU.mult, ALU.add))
                dve.wait_ge(s_used, uc + 3 * j + 3)
                V_.tensor_tensor(t, t, pb[(3 * j + 2) % 2], ALU.mult).then_inc(s_cuf, 1)
                dve.wait_ge(s_cuf, 3 * j + 3)
                V_.tensor_tensor(YC[:, j, :], t, RS[:], ALU.mult).then_inc(s_yc, 1)

            def conv_sum(j):
                dve.wait_ge(s_ycsq, j + 1)
                if j == 0:
                    V_.tensor_copy(ACC[:], SQ[:, 0, :]).then_inc(s_ycacc, 1)
                else:
                    dve.wait_ge(s_ycacc, j)
                    V_.tensor_tensor(ACC[:], ACC[:], SQ[:, j % 2, :], ALU.add).then_inc(s_ycacc, 1)

            def attention_out(n):
                i, h = NT - 1 - n // H1, n % H1
                dve.wait_ge(s_e, n + 1)
                link(V_.reciprocal(RD[:, n:n + 1], DEN[:, n:n + 1]))
                dve.wait_ge(s_pv, n + 1)
                V_.tensor_scalar(YA[:, i, h * HD:(h + 1) * HD], pb[6 + n % 2][:, 0:HD], RD[:, n:n + 1], None,
                                 ALU.mult).then_inc(s_ya, 1)

            dve.wait_ge(s_bt, 16)
            steps = NT * H1
            for n in range(steps + 3):
                if n < steps:
                    i, h = NT - 1 - n // H1, n % H1
                    w = (i + 1) * P
                    dve.wait_ge(s_s, n + 1)
                    if n >= 2:
                        dve.wait_ge(s_pt, n - 1)
                    V_.tensor_tensor_reduce(SC[:, n % 2, 0:w], pb[2 + n % 2][:, 0:w], BT[:, h, T - w:T], 1.0, -3e38,
                                            ALU.add, ALU.max, MX[:, n:n + 1]).then_inc(s_sc, 1)
                    dve.wait_ge(s_sc, n + 1)
                    V_.tensor_scalar(NM[:, n:n + 1], MX[:, n:n + 1], -1.0, None, ALU.mult).then_inc(s_nm, 1)
                if n >= 3:
                    attention_out(n - 3)
                j, r = divmod(n, 8)
                if r == 3 and j < CK:
                    if j:
                        dve.wait_ge(s_yc, j)
                    conv_c(j)
                if r == 5 and j < CK:
                    conv_x(j)
                if r == 0 and 1 <= j:
                    conv_b(j - 1)
                if r == 2 and 1 <= j:
                    conv_sum(j - 1)
            dve.wait_ge(s_ac, 1)
            link(V_.reciprocal(YS, YS))
            for i in range(NT):
                V_.tensor_scalar(YA[:, i, :], YA[:, i, :], YS[:, i:i + 1], None, ALU.mult).then_inc(s_yan, 1)
            dve.wait_ge(s_ycsd, 1)
            link(V_.reciprocal(TMP[:, 3, :], TMP[:, 3, :]))
            for j in range(CK):
                if j >= 2:
                    dve.wait_ge(s_yl, j - 1)
                V_.scalar_tensor_tensor(SC[:, j % 2, :], YC[:, j, :], prm("g_oc", j), TMP[:, 3, :],
                                        ALU.mult, ALU.mult).then_inc(s_yn, 1)
                dve.wait_ge(s_ynh, j + 1)
                dve.wait_ge(s_yn, j + 1)
                V_.tensor_tensor(YL[:, j, :], SC[:, j % 2, :], YH[:, j, :].bitcast(F32), ALU.subtract
                                 ).then_inc(s_yl, 1)
            for b in range(CK):
                dve.wait_ge(s_yh, b + 1)
                V_.scalar_tensor_tensor(YL[:, CK + b, :], pb[4 + b], prm("g_oa", b),
                                        YH[:, CK + b, :].bitcast(F32), ALU.mult, ALU.subtract).then_inc(s_yl, 1)

            for m in range(DK):
                dve.wait_ge(s_used, UNITS["wo"][0] + m + 1)
                V_.tensor_tensor(X[:, m, :], X[:, m, :], pb[m % 2], ALU.add).then_inc(s_x["ffn"].sem, 1)
                if m:
                    low("ffn", "g_ffn", (m - 1) // 2, 2, (m - 1) % 2, AH, AL)
                    add_square("ffn", (m - 1) // 2, 2, (m - 1) % 2)
            low("ffn", "g_ffn", 3, 2, 1, AH, AL)
            add_square("ffn", 3, 2, 1)
            if stop == "mixer1":
                return

            def ffn(f, norm, down):
                S, u0 = FS[f], UNITS[f][0]
                sfx, o = ("", 2) if f == "ffn" else ("2", 1)
                norm_reciprocal(norm)

                def chunk(i, j):
                    wait(dve, s_used, i, NS, u0 + 2 * j + 1)
                    wait(dve, S["t3"], i, 2, j - 1)
                    V_.tensor_tensor(PAD[:, j, o:o + T], pb[2 * j], RS[:], ALU.mult).then_inc(S["pad"].sem, 1)
                    wait(dve, S["t1"], i, 2, j + 1)
                    wait(dve, S["pad"], i, 2, j + 1)
                    t = TMP[:, j, :]
                    V_.scalar_tensor_tensor(t, PAD[:, j, 1:T + 1], prm_at("fcw" + sfx, FC, i, 2, j), t,
                                            ALU.mult, ALU.add).then_inc(S["ta"].sem, 1)
                    wait(dve, S["ta"], i, 2, j + 1)
                    V_.scalar_tensor_tensor(t, PAD[:, j, 2:T + 2], prm_at("fcw" + sfx, 2 * FC, i, 2, j), t,
                                            ALU.mult, ALU.add).then_inc(S["t3"].sem, 1)
                    wait(dve, s_used, i, NS, u0 + 2 * j + 2)
                    wait(dve, S["sl"], i, 2, j - 1)
                    V_.tensor_tensor(TMP[:, 2 + j, :], pb[2 * j + 1], RS[:], ALU.mult).then_inc(S["up"].sem, 1)
                    wait(dve, S["act"], i, 2, j + 1)
                    wait(dve, S["up"], i, 2, j + 1)
                    V_.tensor_tensor(TMP[:, 2 + j, :], TMP[:, j, :], TMP[:, 2 + j, :], ALU.mult
                                     ).then_inc(S["h"].sem, 1)
                    wait(dve, S["sh"], i, 2, j + 1)
                    V_.tensor_tensor(at(SL, i, j, 2), TMP[:, 2 + j, :], at(SH, i, j, 2).bitcast(F32),
                                     ALU.subtract).then_inc(S["sl"].sem, 1)

                for j in range(2):
                    chunk(0, j)
                with dve.Fori(1, FC // 2) as i:
                    for j in range(2):
                        chunk(i, j)

                u0 = UNITS[down][0]
                if f == "ffn":
                    for q in range(2):
                        dve.wait_ge(s_ph, q + 1)
                        V_.tensor_tensor(PL[:, q, :], PIN[:, q, :], PH[:, q, :].bitcast(F32), ALU.subtract
                                         ).then_inc(s_pl, 1)

                def tile(i, j):
                    if f == "ffn":
                        wait(dve, s_used, i, 2 * NS, u0 + NS * (j + 1))
                        V_.tensor_tensor(at(X, i, j, 2), at(X, i, j, 2), pb[4 + j], ALU.add
                                         ).then_inc(s_x["ple"].sem, 1)
                        low("ple", "g_ple", i, 2, j, AH, AL)
                        add_square("ple", i, 2, j)
                    else:
                        add_square("fpost", i, 2, j)

                for j in range(2):
                    tile(0, j)
                with dve.Fori(1, DK // 2) as i:
                    for j in range(2):
                        tile(i, j)

            ffn("ffn", "ffn", "down")

            norm_reciprocal("ple")

            def g4(m):
                low("mix2", "pre2", m // 2, 2, m % 2, GH, GL)
                add_square("mix2", m // 2, 2, m % 2)

            dve.wait_ge(s_pp, DK)
            for m in range(DK + 2):
                if m < DK:
                    dve.wait_ge(s_used, UNITS["pgate"][0] + m + 1)
                    if m >= 2:
                        dve.wait_ge(s_sg, m - 1)
                    V_.tensor_tensor(TMP[:, m % 2, :], pb[m % 2], RS[:], ALU.mult).then_inc(s_pgt, 1)
                if 1 <= m <= DK:
                    n = m - 1
                    dve.wait_ge(s_sg, n + 1)
                    V_.tensor_tensor(SG[:, n, :], SG[:, n, :], PP[:, n, :], ALU.mult).then_inc(s_pm, 1)
                    dve.wait_ge(s_pm, n + 1)
                    V_.tensor_tensor(X[:, n, :], X[:, n, :], SG[:, n, :], ALU.add).then_inc(s_x["mix2"].sem, 1)
                if m >= 2:
                    g4(m - 2)
            if stop == "block1":
                return

            link(V_.memset(PAD[:, :, T + 1:T + 2], 0.0))
            norm_reciprocal("mix2", 2)
            rows = slice(0, 8)
            dve.wait_ge(s_used, UNITS["small"][0] + 1)
            V_.tensor_tensor(SQ[:, 0, :], pb[0], RS[:], ALU.mult).then_inc(s_row, 1)
            V_.memset(SA[:, 0, :], 0.0)
            dve.wait_ge(s_rw8, 1)
            LF, IG, B, BRV = ROW[3], ROW[0], SQ[rows, 1, :], ACC[rows, :]
            CF, CB, MF, MB = ROW[2], ROW[1], *MROWS
            link(V_.scalar_tensor_tensor(LF, ROW[1], 0.0, ROW[2], ALU.min, ALU.subtract))
            V_.tensor_tensor_scan(B, LF, LF, 0.0, ALU.add, ALU.min)
            link(V_.tensor_tensor_scan(BRV[:, ::-1], LF[:, ::-1], LF[:, ::-1], 0.0, ALU.add, ALU.min))
            V_.tensor_tensor(CF, IG, B, ALU.subtract)
            link(V_.tensor_tensor(CB, IG, BRV, ALU.subtract))
            V_.tensor_tensor_scan(MF, CF, CF, 0.0, ALU.max, ALU.max)
            link(V_.tensor_tensor_scan(MB[:, ::-1], CB[:, ::-1], CB[:, ::-1], 0.0, ALU.max, ALU.max))
            V_.tensor_tensor(B, B, MF, ALU.add)
            V_.tensor_tensor(BRV, BRV, MB, ALU.add).then_inc(s_gabs, 1)

            def projected(pair, bank):
                for n in range(2):
                    dve.wait_ge(s_used, UNITS[f"kq{pair}"][0] + n + 1)
                    V_.tensor_tensor(KQ[pair][n], pb[bank + n], RS[:], ALU.mult).then_inc(s_dup, 1)

            def cumulated(h):
                dve.wait_ge(s_lax, h + 1)
                gate, L = GATE[h]
                link(V_.scalar_tensor_tensor(L, gate, 0.0, L, ALU.min, ALU.subtract))
                V_.tensor_tensor_scan(CUM[h][0:HD], L[0:HD, :], L[0:HD, :], 0.0, ALU.add, ALU.min)
                V_.memset(CUM[h][HD:P, 0:1], 0.0)
                V_.tensor_tensor_scan(CUM[h][HD:P, 1:T], L[HD:P, 0:T - 1], L[HD:P, 0:T - 1], 0.0,
                                      ALU.add, ALU.min).then_inc(s_xg, 1)

            cumulated(0)
            cumulated(1)
            dve.wait_ge(s_xg, 2)
            projected(0, 0)
            dve.wait_ge(s_lz, 4)
            dve.wait_ge(s_lm, 16)

            def decayed(h, l):
                b = (BIG + SMALL)[l]
                q, k = (QB[:, l, :], KB_[:, l, :]) if l < 2 else (QS[:, l - 2, :], KS[:, l - 2, :])
                g = NL * h + l
                dve.wait_ge(s_ee, g + 1)
                if h and l == 0:
                    dve.wait_ge(s_gb, NT * h)
                v = [t.rearrange("p (n s w) -> p n s w", s=2, w=b) for t in
                     (q, k, Q2[:, h % 2, :], K2[:, h % 2, :], DIST[g % 3])]
                for half, (qs, ks) in enumerate(((1, 0), (0, 1))):
                    r = slice(half * HD, (half + 1) * HD)
                    V_.tensor_tensor(v[0][r, :, qs, :], v[2][r, :, qs, :], v[4][r, :, qs, :], ALU.mult)
                    ins = V_.tensor_tensor(v[1][r, :, ks, :], v[3][r, :, ks, :], v[4][r, :, ks, :], ALU.mult)
                ins.then_inc(s_lv, 1)

            def conv_tile(m):
                dve.wait_ge(s_used, UNITS["aqk"][0] + m + 1)
                if m:
                    dve.wait_ge(s_a3, m)
                V_.tensor_tensor(PAD[:, 0, 1:T + 1], pb[4 + m % 2], RS[:], ALU.mult).then_inc(s_apad, 1)
                dst = (AQ if m < 2 else AK)[:, m % 2, :]
                dve.wait_ge(s_apad, m + 1)
                dve.wait_ge(s_a1, m + 1)
                link(V_.scalar_tensor_tensor(dst, PAD[:, 0, 1:T + 1], prm("mcw", 4 + m), dst,
                                             ALU.mult, ALU.add))
                V_.scalar_tensor_tensor(dst, PAD[:, 0, 2:T + 2], prm("mcw", 8 + m), dst,
                                        ALU.mult, ALU.add).then_inc(s_a3, 1)

            masked = TMP[:, 0:2, :].rearrange("p a (l c) -> p (a l) c", c=P)
            for h in range(H2):
                dve.wait_ge(s_kqf, 2 * (h + 1))
                for l in range(NL):
                    decayed(h, l)
                if h == 1:
                    projected(1, 4)
                if h >= 2:
                    for m in range(2 * h - 4, 2 * h - 2):
                        conv_tile(m)
                for j in range(NT):
                    n = NT * h + j
                    dve.wait_ge(s_gs, n + 1)
                    if n >= 2:
                        dve.wait_ge(s_go, n - 1)
                    link(V_.tensor_tensor(masked, PS[:, SBANK[n % 2]:SBANK[n % 2] + 2, :].rearrange(
                                              "p a (l c) -> p (a l) c", c=P),
                                          LM.rearrange("p (l c) -> p l c", c=P), ALU.mult))
                    V_.tensor_reduce(SA[:, j % 2, tokens(j)], masked.rearrange("p l c -> p c l"),
                                     mybir.AxisListType.X, ALU.add).then_inc(s_sad, 1)
                    dve.wait_ge(s_sad, n + 1)
                if h == 0:
                    cumulated(2)
                    cumulated(3)
                    dve.wait_ge(s_xg, H2)

            def head_squares(y, sums):
                for i in range(NT):
                    link(V_.tensor_tensor(TMP[:, 2, :], y[:, i, :], y[:, i, :], ALU.mult))
                    ins = V_.tensor_reduce(sums[:, H2 * i:H2 * i + H2],
                                           TMP[:, 2, :].rearrange("p (h c) -> p h c", h=H2),
                                           mybir.AxisListType.X, ALU.add)
                    if i < NT - 1:
                        link(ins)
                ins.then_inc(s_ybq, 1)

            def gated(y, r, gate, by_head):
                for i in range(NT):
                    for h in range(H2):
                        c = slice(h * DV, (h + 1) * DV)
                        g, v = (H2 * h + i, y[:, h, tokens(i)]) if by_head else (H2 * i + h, y[:, i, c])
                        ins = V_.scalar_tensor_tensor(v, v, r[:, g:g + 1], gate[:, i, c], ALU.mult, ALU.mult)
                ins.then_inc(s_y2, 1)

            dve.wait_ge(s_oc, H2)
            head_squares(YB, BSS)
            dve.wait_ge(s_gs, 4 * NT)
            V_.memset(VA[:, :, :, DV:DV + 1], 1.0).then_inc(s_va, 1)
            dve.wait_ge(s_gn, 1)
            link(V_.reciprocal(BSS, BSS))
            dve.wait_ge(s_br, NT)
            gated(YB, BSS, BR, True)

            dve.wait_ge(s_zero, 32)
            dve.wait_ge(s_go, 4 * NT)

            def exponents(n):
                h, j = divmod(n, NT)
                if j == 0:
                    dve.wait_ge(s_bcc, 2 * h + 2)
                if n >= 2:
                    dve.wait_ge(s_mo, n - 1)
                for d in range(2):
                    c = CG[:, j, d, h + H2 * d:h + H2 * d + 1]
                    V_.scalar_tensor_tensor(WT[:, n % 2, d, tokens(j)], TMP[:, 2 + d, tokens(j)], c, NEG[:, d, :],
                                            ALU.add, ALU.add).then_inc(s_ad, 1)

            def weighted(n):
                j = n % NT
                dve.wait_ge(s_ms2, n + 1)
                for d in range(2):
                    dve.wait_ge(s_w, 2 * n + d + 1)
                    c = slice(j * P, T) if d == 0 else slice(0, (j + 1) * P)
                    w = WT[:, n % 2, d, c]
                    V_.scalar_tensor_tensor(w, pb[2 + n % 2][:, c], 0.125, w, ALU.mult, ALU.mult
                                            ).then_inc(s_sw, 1)

            def state_out(h):
                dve.wait_ge(s_mo, NT * (h + 1))
                for b, c in ((0, 3), (1, 3), (2, 2)):
                    v = PS[:, 4 + b, 0:c * (DV + 1)].rearrange("p (q c) -> p q c", c=DV + 1)
                    ins = V_.tensor_copy(DN[:, 3 * b:3 * b + c], v[:, :, DV])
                link(ins)
                link(V_.scalar_tensor_tensor(DN, DN, -1.0, DN, ALU.mult, ALU.max))
                for d in range(2):
                    m = DN[:, NT * d:NT * d + NT]
                    ins = V_.tensor_tensor(m, m, CG[:, :, 2 + d, h + H2 * d], ALU.max)
                link(ins)
                V_.reciprocal(DN, DN).then_inc(s_hb, 1)
                dve.wait_ge(s_hst, h + 1)
                for i in range(NT):
                    bank = PS[:, 4 + i // 3, (i % 3) * (DV + 1):(i % 3) * (DV + 1) + DV]
                    ins = V_.scalar_tensor_tensor(YM[:, i, h * DV:(h + 1) * DV], bank, DN[:, i:i + 1],
                                                  TMP[:, h % 2, tokens(i)], ALU.mult, ALU.add)
                ins.then_inc(s_hf, 1)
                dve.wait_ge(s_hf, h + 1)

            for n in range(NT * H2 + 1):
                if n < NT * H2:
                    exponents(n)
                if n:
                    weighted(n - 1)
                    if n % NT == 0:
                        state_out(n // NT - 1)
            V_.memset(PAD[:, 1, 0:1], 0.0)
            head_squares(YM, MSS)
            dve.wait_ge(s_gn, 2)
            link(V_.reciprocal(MSS, MSS))
            gated(YM, MSS, AO, False)
            for n, b in enumerate((4, 5, 6, 7, 0, 1, 2, 3)):
                dve.wait_ge(s_y2h, n + 1)
                V_.scalar_tensor_tensor(YL[:, b, :], pb[b], prm("mnorm" if b < CK else "gnorm", b % CK),
                                        YH[:, b, :].bitcast(F32), ALU.mult, ALU.subtract).then_inc(s_y2l, 1)
            for m in range(DK):
                add_square("post", m // 2, 2, m % 2)

            def add_normed(n, to, mix, gain, m):
                link(V_.scalar_tensor_tensor(mix[:, m, :], mix[:, m, :], prm(gain, m), RS[:], ALU.mult, ALU.mult))
                V_.tensor_tensor(X[:, m, :], X[:, m, :], mix[:, m, :], ALU.add).then_inc(s_x[to].sem, 1)

            norm_reciprocal("post")
            for m in range(DK):
                add_normed("post", "ffn2", MIX, "post2", m)
                if m:
                    low("ffn2", "fpre2", (m - 1) // 2, 2, (m - 1) % 2, AH, AL)
                    add_square("ffn2", (m - 1) // 2, 2, (m - 1) % 2)
            low("ffn2", "fpre2", 3, 2, 1, AH, AL)
            add_square("ffn2", 3, 2, 1)
            ffn("ffn2", "ffn2", "down2")
            norm_reciprocal("fpost")
            for m in range(DK):
                add_normed("fpost", "fpost", MIX2, "fpost2", m)


def _masks(np):
    r = np.arange(P)
    consts = np.zeros((P, 3, P), np.float32)
    consts[:, 0] = np.eye(P)
    consts[:, 1] = 1.0 / D
    consts[:, 2] = r[:, None] // HD == r[None] // HD
    dist = r[:, None] - np.arange(T)[None] + (T - P)
    seen = ((dist <= 128).astype(int) + (dist % 4 == 0) + (dist % 16 == 0)) * (dist >= 0)
    log = np.where(seen > 0, np.log(np.maximum(seen, 1)), -1e30)
    slopes = 2.0 ** -(8.0 * np.arange(1, H1 + 1) / H1)
    bias = (log[:, None] - slopes[None, :, None] * np.maximum(dist, 0)[:, None]).astype(np.float32)
    masks = np.zeros((P, 8, P), np.float32)
    for l, b in enumerate(SMALL):
        masks[:, l] = r[:, None] // (2 * b) == r[None] // (2 * b)
    masks[:, 7] = np.eye(P)
    sel = np.zeros((P, 8, P), np.float32)
    for i in range(8):
        sel[i, i] = -1.0
    neg = np.zeros((P, 2, P), np.float32)
    neg[:, 0] = np.where(r[:, None] <= r[None], 0.0, -1e30)
    neg[:, 1] = np.where(r[:, None] >= r[None], 0.0, -1e30)
    return consts, bias, masks.reshape(P, 8 * P), sel.reshape(P, 8 * P), neg


def _column_units(np, w):
    k, c = w.shape
    return w.reshape(k // P, P, c // P, P).transpose(2, 1, 0, 3).reshape(c // P, P, k)


def _row_units(np, w):
    return w.reshape(4, 2, P, T).transpose(0, 2, 1, 3).reshape(4, P, 2 * T)


def _down_units(np, w):
    k, c = w.shape
    v = w.reshape(k // P, P, c // P, P).transpose(2, 1, 0, 3)
    out = np.zeros((c // P * NS, P, UW), w.dtype)
    a = 0
    for q, n in enumerate(DOWN_TILES):
        out[q::NS, :, 0:n * P] = v[:, :, a:a + n].reshape(c // P, P, n * P)
        a += n
    return out


def _layout(np, a):
    g = lambda n: a[n][0]
    w_in, w2 = g("w_in"), g("w_in_2")
    cb, cc, cx, wq, wk, wv = np.split(w_in, 6, axis=1)
    conv = np.stack([_column_units(np, x) for x in (cc, cx, cb)], axis=1).reshape(12, P, UW)
    gate_up = lambda x, y: np.stack([_column_units(np, x), _column_units(np, y)], axis=1).reshape(2 * FC, P, UW)
    proj = _column_units(np, g("w_ple_proj")).reshape(2, 4, P, 2 * P).transpose(0, 2, 1, 3).reshape(2, P, UW)
    o = np.cumsum([0, 512, 512, 512, 16, 256, 256, 512, 512, 32])
    aqk, av, ao, ag, bq, bk, bv, br, blr = (w2[:, o[i]:o[i + 1]] for i in range(9))
    small = np.zeros((D, P), w2.dtype)
    small[:, 0:4], small[:, 4:8] = ag[:, 0:4], ag[:, 8:12]
    small[:, 32:36], small[:, 36:40] = ag[:, 4:8], ag[:, 12:16]
    small[:, 64:96] = blr
    ubk, ubq, ubv = _column_units(np, bk), _column_units(np, bq), _row_units(np, bv)
    w = np.concatenate([
        _column_units(np, wq), _column_units(np, wk), _row_units(np, wv), conv, _column_units(np, g("w_out")),
        gate_up(g("w_gate"), g("w_up")), _down_units(np, g("w_down")), proj, _column_units(np, g("w_ple_gate")),
        ubv[0:1], _column_units(np, small), ubv[1:4], ubk[0:1], ubq[0:1], _row_units(np, ao), ubk[1:2], ubq[1:2],
        _column_units(np, aqk), _row_units(np, br), _row_units(np, av), _column_units(np, g("w_out_2")),
        gate_up(g("ffn_w_gate_2"), g("ffn_w_up_2")), _down_units(np, g("ffn_w_down_2"))], axis=0)
    gw = np.zeros((32, H2, 2, HD), w2.dtype)
    for d in range(2):
        gw[16 * d:16 * d + 16, :, d] = g("gla_w2_2")[d].reshape(16, H2, HD)

    prm = np.zeros((P, NPRM), np.float32)

    def put(name, v, rows=slice(0, P)):
        prm[rows, PCOLS[name]:PCOLS[name] + v.shape[1]] = v

    cols = lambda v: v.reshape(-1, P).T
    taps = lambda v: np.concatenate([cols(x) for x in v], axis=1)
    put("eps", np.repeat(np.array([[EPS, HD * EPS, 1.0, 0.0]], np.float32), P, axis=0))
    for name, src in (("g_mix", "g_mix"), ("g_ffn", "g_ffn"), ("g_ple", "g_ple"), ("pre2", "norm_mix_pre_2"),
                      ("post2", "norm_mix_post_2"), ("fpre2", "norm_ffn_pre_2"), ("fpost2", "norm_ffn_post_2"),
                      ("g_oc", "g_out_conv"), ("g_oa", "g_out_attn"), ("cb", "conv_b"), ("mcb", "mlstm_conv_b_2"),
                      ("fcb", "ffn_conv_b"), ("fcb2", "ffn_conv_b_2"), ("mnorm", "mlstm_norm_2"),
                      ("gnorm", "gla_norm_2")):
        put(name, cols(g(src).reshape(-1)))
    for name, src in (("cw", "conv_w"), ("mcw", "mlstm_conv_w_2"), ("fcw", "ffn_conv_w"), ("fcw2", "ffn_conv_w_2")):
        put(name, taps(g(src)))
    put("qg", np.tile(g("q_norm_g"), 2)[:, None])
    put("kg", np.tile(g("k_norm_g"), 2)[:, None])
    put("glab", g("gla_b_2").reshape(2, H2, HD).transpose(0, 2, 1).reshape(P, H2))
    gb = g("mlstm_gate_b_2")
    put("gib", np.concatenate([gb[0:4], gb[8:12]])[:, None], slice(0, 8))
    put("gfb", np.concatenate([gb[4:8], gb[12:16]])[:, None], slice(32, 40))
    return w, gw.reshape(32, H2 * P), prm


def kernel(**inputs):
    import numpy as np
    import concourse.bacc as bacc
    from concourse.bass_utils import run_bass_kernel_spmd

    a = {k: np.asarray(v) for k, v in inputs.items()}
    w, gw, prm = _layout(np, a)
    consts, bias, masks, sel, neg = _masks(np)
    tiles = lambda v: np.ascontiguousarray(v.T.reshape(-1, P, T).transpose(1, 0, 2))
    arrays = {"x": tiles(a["x"][0]), "p": tiles(a["p"][0, 0]), "w": w, "gla_w": gw, "params": prm,
              "consts": consts, "bias": bias, "masks": masks, "selectors": sel, "negmask": neg}
    arrays = {k: np.ascontiguousarray(v) for k, v in arrays.items()}
    nc = bacc.Bacc("TRN2", target_bir_lowering=False, num_devices=1)
    dram = {k: nc.dram_tensor(f"in_{k}", v.shape, F32, kind="ExternalInput").ap() for k, v in arrays.items()}
    out = nc.dram_tensor("out", (P, DK, T), F32, kind="ExternalOutput").ap()
    build(nc, dram, out)
    r = run_bass_kernel_spmd(nc, [{f"in_{k}": v for k, v in arrays.items()}], core_ids=[0])
    y = r.results[0]["out"]
    return y.transpose(1, 0, 2).reshape(D, T).T.reshape(1, T, D)
```

```python
from contextlib import ExitStack

import concourse.bass as bass
from concourse import mybir

F32 = mybir.dt.float32
F32R = mybir.dt.float32r
ALU = mybir.AluOpType
ACT = mybir.ActivationFunctionType

P = 128
T = 512
NT = T // P
D = 1024
DK = D // P
DFF = 2816
FC = DFF // P
CW = 512
CK = CW // P
H1 = 8
HD = 64
H2 = 4
DV = 128
UW = 8 * P
NS = 4
EPS = 1e-6
BIG = (256, 128)
SMALL = (64, 32, 16, 8, 4, 2, 1)

NL = len(BIG) + len(SMALL)

PCOLS = {}


def _param_columns():
    at = 0
    for name, n in (("eps", 4), ("g_mix", DK), ("g_ffn", DK), ("g_ple", DK), ("pre2", DK), ("post2", DK),
                    ("fpre2", DK), ("fpost2", DK), ("g_oc", CK), ("g_oa", CK), ("cw", 3 * CK), ("cb", CK),
                    ("qg", 1), ("kg", 1), ("mcw", 3 * 4), ("mcb", 4), ("mnorm", H2), ("gnorm", H2),
                    ("glab", H2), ("gib", 1), ("gfb", 1), ("fcw", 3 * FC), ("fcb", FC), ("fcw2", 3 * FC),
                    ("fcb2", FC)):
        PCOLS[name] = at
        at += n
    return at


NPRM = _param_columns()

class Stage:

    def __init__(self, sem, base):
        self.sem = sem
        self.base = base


UNITS = {}


def _unit_table():
    at = 0
    for name, n in (("qk", 8), ("v", 4), ("conv", 12), ("wo", 8), ("ffn", 2 * FC), ("down", 32),
                    ("pproj", 2), ("pgate", 8),
                    ("bva", 2), ("small", 1), ("bvb", 2), ("kq0", 2), ("ao", 4), ("kq1", 2), ("aqk", 4), ("av", 4), ("br", 4),
                    ("wo2", 8), ("ffn2", 2 * FC), ("down2", 32)):
        UNITS[name] = (at, n)
        at += n
    return at


NU = _unit_table()
DOWN_TILES = (6, 6, 5, 5)


def tokens(j, n=1):
    return slice(j * P, (j + n) * P)


def build(nc, dram, out):
    ctx = ExitStack()
    with ctx:
        base = [(nc.sbuf_base + 63) // 64 * 64]

        def put(name, shape, dt, at=None):
            size = 4
            for s in shape[1:]:
                size *= s
            if at is None:
                at = base[0]
                base[0] += (size + 31) // 32 * 32
            return nc.alloc_sbuf_tensor_at(name, shape, dt, offset=at)

        KB = 1024
        X = put("X", [P, DK, T], F32)
        S_at = base[0]
        SH = put("SH", [P, FC, T], F32R)
        SL = put("SL", [P, FC, T], F32R)
        A_at = base[0]
        AH = put("AH", [P, DK, T], F32R)
        AL = put("AL", [P, DK, T], F32R)
        RAW = put("RAW", [P, NS, UW], F32)
        WH = put("WH", [P, NS, UW], F32R)
        WL = put("WL", [P, NS, UW], F32R)
        TMP_at = base[0]
        TMP = put("TMP", [P, 4, T], F32)
        PAD = put("PAD", [P, 2, T + 2], F32)
        ACC = put("ACC", [P, T], F32)
        SQ = put("SQ", [P, 2, T], F32)
        RS = put("RS", [P, T], F32)
        PRM = put("PRM", [P, NPRM], F32)
        CST = put("CST", [P, 3, P], F32)
        COL = put("COL", [P, 256], F32)
        assert base[0] <= nc.sbuf_usable_end, (base[0], nc.sbuf_usable_end)
        IDENT, INVD, BONE = (CST[:, i, :] for i in range(3))

        YH = put("YH", [P, DK, T], F32R, S_at)
        YL = put("YL", [P, DK, T], F32R, S_at + 16 * KB)
        YC = put("YC", [P, CK, T], F32, S_at + 8 * KB)
        QT = put("QT", [P, CK, T], F32, S_at + 32 * KB)
        KT = put("KT", [P, CK, T], F32, S_at + 40 * KB)
        V = put("V", [P, NT, CW], F32, S_at + 48 * KB)
        BT = put("BT", [P, H1, T], F32, S_at + 56 * KB)
        YA = put("YA", [P, NT, CW], F32, S_at + 72 * KB)
        SC = put("SC", [P, 2, T], F32, S_at + 80 * KB)
        PT = put("PT", [P, 2, T], F32, S_at + 84 * KB)
        RC = COL[:, 252:256]
        MX, NM, DEN, RD = (COL[:, 32 * i:32 * i + 32] for i in range(1, 5))
        YS = COL[:, 160:164]

        PIN = put("PIN", [P, 2, T], F32, TMP_at)
        PH = put("PH", [P, 2, T], F32R, TMP_at + 4 * KB)
        PL = put("PL", [P, 2, T], F32R, TMP_at)
        SG = put("SG", [P, DK, T], F32, S_at + 32 * KB)
        PP = put("PP", [P, DK, T], F32, S_at + 48 * KB)

        GH = put("GH", [P, DK, T], F32R, S_at)
        GL = put("GL", [P, DK, T], F32R, S_at + 16 * KB)
        R = S_at + 32 * KB
        VB = put("VB", [P, NT, CW], F32, R)
        YB = put("YB", [P, H2, T], F32, R + 8 * KB)
        AO = put("AO", [P, NT, CW], F32, R + 16 * KB)
        Q2 = put("Q2", [P, 2, T], F32, R + 24 * KB)
        K2 = put("K2", [P, 2, T], F32, R + 28 * KB)
        XG = put("XG", [P, 2, T], F32, R + 32 * KB)
        SA = put("SA", [P, 2, T], F32, R + 36 * KB)
        QB = put("QB", [P, 2, T], F32, R + 40 * KB)
        KB_ = put("KB", [P, 2, T], F32, R + 44 * KB)
        LM = put("LM", [P, 8 * P], F32, R + 48 * KB)
        AK = put("AK", [P, 2, T], F32, R + 52 * KB)
        QS = put("QS", [P, 7, T], F32, A_at)
        KS = put("KS", [P, 7, T], F32, A_at + 14 * KB)
        AQ = put("AQ", [P, 2, T], F32, A_at + 28 * KB)
        BR = put("BR", [P, H2, T], F32, A_at)
        VA = put("VA", [P, NT, H2, DV + 1], F32, A_at + 8 * KB)
        NUM = put("NUM", [P, 2 * NT, DV + 1], F32, A_at + 17 * KB)
        YM = put("YM", [P, H2, T], F32, R + 24 * KB)
        SEL = put("SEL", [P, 8 * P], F32, R + 48 * KB)
        NEG = put("NEG", [P, 2, P], F32, R + 32 * KB)
        WT = put("WT", [P, 2, 2, T], F32, R + 36 * KB)
        MIX = put("MIX", [P, DK, T], F32, S_at + 32 * KB)
        MIX2 = put("MIX2", [P, DK, T], F32, A_at)

        PS = ctx.enter_context(nc.psum_tensor("PS", [P, 8, T], F32))
        pb = [PS[:, i, :] for i in range(8)]

        def sem(name):
            return ctx.enter_context(nc.semaphore(name))

        def prm(name, i=0, rows=slice(0, P)):
            return PRM[rows, PCOLS[name] + i:PCOLS[name] + i + 1]

        def at(t, i, j=0, per=1):
            if isinstance(i, int):
                return t[:, per * i + j, :]
            return t[:, bass.ds(i * per + j, 1), :].rearrange("p o n -> p (o n)")

        def prm_at(name, off, i, per, j):
            c = PCOLS[name] + off + j
            if isinstance(i, int):
                return PRM[:, c + per * i:c + per * i + 1]
            return PRM[:, bass.ds(i * per + c, 1)]

        passed = {nc.scalar.engine: sem("s_act_passed"), nc.gpsimd.engine: sem("s_pool_passed")}

        def ge(eng, s, v, more=0):
            if isinstance(s, Stage):
                s, more = s.sem, more + s.base
            eng.wait_ge(s, v + more)

        def wait(eng, s, i, per, v):
            if not isinstance(i, int):
                ge(eng, s, i * per, v)
                if eng.engine in passed:
                    eng.sem_inc(passed[eng.engine], 1)
            elif per * i + v > 0:
                ge(eng, s, per * i + v)

        CG = COL[:, 0:128].rearrange("p (t g r) -> p t g r", t=NT, g=4)
        BSS, MSS, DN, NRM = COL[:, 128:144], COL[:, 144:160], COL[:, 164:172], COL[:, 172:204]

        CUM = (XG[:, 0, :], XG[:, 1, :], YB[:, 2, :], YB[:, 3, :])
        GATE = ((TMP[:, 2, :], TMP[:, 3, :]), (TMP[:, 0, :], TMP[:, 1, :]),
                (AQ[:, 0, :], AQ[:, 1, :]), (AK[:, 0, :], AK[:, 1, :]))
        KQ = ((TMP[:, 0, :], TMP[:, 1, :]), (XG[:, 0, :], XG[:, 1, :]))
        ROW = (AQ[0:8, 0, :], AQ[0:8, 1, :], AK[0:8, 0, :], AK[0:8, 1, :])
        MROWS = (PAD[0:8, 1, 0:T], SQ[0:8, 0, :])

        EPS_C, EPS64_C, ONE_C = prm("eps", 0), prm("eps", 1), prm("eps", 2)

        s_raw = [sem(f"s_raw{i}") for i in range(NS)]
        s_hi = sem("s_hi")
        s_split = sem("s_split")
        s_used = sem("s_used")
        s_xin = [sem(f"s_xin{i}") for i in range(4)]
        s_prm = sem("s_prm")
        s_cst = sem("s_cst")
        s_bt = sem("s_bt")
        s_out = sem("s_out")
        s_pad = sem("s_pad")
        s_vc = sem("s_vc")
        s_ac = sem("s_ac")
        ALL = ("mix", "ffn", "ple", "mix2", "post", "ffn2", "fpost")
        SPLIT = tuple(n for n in ALL if n not in ("post", "fpost"))

        def stages(w, names, per):
            s = sem(f"s_{w}")
            return {n: Stage(s, per * i) for i, n in enumerate(names)}

        s_x = stages("x", ("ffn", "ple", "mix2", "ffn2", "fpost"), DK)
        s_gh, s_gl = stages("gh", SPLIT, DK), stages("gl", SPLIT, DK)
        s_sq, s_acc = stages("sq", ALL, DK), stages("acc", ALL, DK)
        s_ms, s_sd, s_rs = stages("ms", ALL, 1), stages("sd", ALL, 1), stages("rs", ALL, 1)
        s_z, s_zsq, s_hms, s_hsd, s_qk = (sem(f"s_{w}") for w in ("z", "zsq", "hms", "hsd", "qk"))
        s_v, s_rc, s_rcd = sem("s_v"), sem("s_rc"), sem("s_rcd")
        s_cuf, s_cx, s_c0, s_yc, s_ycsq, s_ycacc, s_ycms, s_ycsd, s_yn, s_yl = (
            sem(f"s_{w}") for w in ("cuf", "cx", "c0", "yc", "ycsq", "ycacc", "ycms", "ycsd", "yn", "yl"))
        s_s, s_sc, s_nm, s_e, s_pt, s_ptc, s_pv, s_ya, s_yss, s_yan, s_yt, s_yh = (
            sem(f"s_{w}") for w in ("s", "sc", "nm", "e", "pt", "ptc", "pv", "ya", "yss", "yan", "yt", "yh"))
        s_ynh = sem("s_ynh")
        FS = {"ffn": {}, "ffn2": {}}
        for w in ("pad", "t1", "ta", "t3", "act", "up", "h", "sh", "sl"):
            s_chunk = sem(f"s_ffn_{w}")
            FS["ffn"][w], FS["ffn2"][w] = Stage(s_chunk, 0), Stage(s_chunk, FC)
        s_pin, s_ph, s_pl, s_pgt, s_sg, s_pm, s_ppj, s_pp = (
            sem(f"s_{w}") for w in ("pin", "ph", "pl", "pgt", "sg", "pm", "ppj", "pp"))
        DIST = (TMP[:, 2, :], TMP[:, 3, :], ACC[:])
        s_gr = sem("s_gr")
        s_gx = sem("s_gx")
        s_brr, s_bsr, s_ym, s_yg = sem("s_brr"), sem("s_bsr"), sem("s_ym"), sem("s_yg")
        s_ysr = sem("s_ysr")
        s_num = sem("s_num")
        s_ybr = sem("s_ybr")
        s_y2p = sem("s_y2p")
        STAB = (TMP[:, 2:4, :], KB_)
        TBANK = (7, 0, 1, 7, 0, 1, 7, 4)
        s_mn = sem("s_mn")
        OWN = 3
        s_lz = sem("s_lz")
        SBANK = (1, 6)
        PBANK = (2, 3, 7, 1)
        s_mix, s_mix2, s_bcc = sem("s_mix"), sem("s_mix2"), sem("s_bcc")
        (s_sel, s_row, s_rw8, s_gabs, s_stk, s_stt, s_cols, s_dup, s_kqf, s_gpr, s_lax, s_la, s_xg, s_lm) = (
            sem(f"s_{w}") for w in ("sel", "row", "rw8", "gabs", "stk", "stt", "cols", "dup", "kqf", "gpr", "lax",
                                      "la", "xg", "lm"))
        s_vb, s_aof, s_dd, s_ee, s_lv, s_gs, s_gb, s_sad, s_sao, s_go, s_oc, s_ybq = (
            sem(f"s_{w}") for w in ("vb", "aof", "dd", "ee", "lv", "gs", "gb", "sad", "sao", "go", "oc", "ybq"))
        s_apad, s_a1, s_a3, s_aqk, s_br, s_va, s_zero = (
            sem(f"s_{w}") for w in ("apad", "a1", "a3", "aqk", "br", "va", "zero"))
        s_bc, s_ms2, s_ad, s_w, s_sw, s_mo, s_hb, s_hf, s_hst, s_gn, s_y2t, s_y2h, s_y2l = (
            sem(f"s_{w}") for w in ("bc", "ms2", "ad", "w", "sw", "mo", "hb", "hf", "hst", "gn", "y2t",
                                      "y2h", "y2l"))

        block = ctx.enter_context(nc.Block())

        def runs(u, limit):
            while u < limit:
                if u in (UNITS["down"][0], UNITS["down2"][0]):
                    yield u, 8, [t * P for t in DOWN_TILES]
                    u += 32
                    continue
                end = min(x for x in (UNITS["down"][0], UNITS["down2"][0], limit) if x > u)
                if end - u >= NS:
                    n = (end - u) // NS
                    yield u, n, [UW] * NS
                    u += n * NS
                else:
                    yield u, 1, [UW] * (end - u)
                    u = end

        def each_unit(eng, step, start=0, limit=NU):
            for u0, iters, widths in runs(start, limit):
                n = len(widths)
                first = 1 if u0 == 0 or iters == 1 else 0
                if first:
                    for j in range(n):
                        step(u0, 0, n, j, widths[j])
                    if u0 == 0 and eng.engine == nc.sync.engine:
                        eng.dma_start(BT[:], dram["bias"]).then_inc(s_bt, 16)
                if iters > first:
                    with eng.Fori(first, iters) as i:
                        for j in range(n):
                            step(u0, i, n, j, widths[j])

        @block.sync
        def _(sp):
            def load_x(k):
                sp.dma_start(X[:, k:k + 2, :], dram["x"][:, k:k + 2, :]).then_inc(s_xin[k // 2], 16)

            load_x(0)
            sp.dma_start(PRM[:], dram["params"]).then_inc(s_prm, 16)

            def load(u0, i, n, j, width):
                slot = (u0 + j) % NS
                wait(sp, s_split, i, n, u0 + j - NS + 1)
                if isinstance(i, int):
                    src = dram["w"][u0 + j + n * i, :, 0:width]
                else:
                    src = dram["w"][bass.ds(i * n + (u0 + j), 1), :, 0:width].rearrange("o p w -> p (o w)")
                sp.dma_start(RAW[:, slot, 0:width], src).then_inc(s_raw[slot], 16)
                if u0 == 0 and isinstance(i, int):
                    if j < 3:
                        load_x(2 * j + 2)
                    if j == 0:
                        sp.dma_start(CST[:], dram["consts"]).then_inc(s_cst, 16)

            each_unit(sp, load)
            for k in range(DK):
                ge(sp, s_x["fpost"], k + 1)
                sp.dma_start(out[:, k, :], X[:, k, :]).then_inc(s_out, 16)
            sp.wait_ge(s_out, 16 * DK)

        @block.gpsimd
        def _(pool):
            def split(u0, i, n, j, width):
                slot = (u0 + j) % NS
                wait(pool, s_used, i, n, u0 + j - NS + 1)
                wait(pool, s_raw[slot], i, 16 * n // NS, 16 * ((u0 + j) // NS + 1))
                nc.gpsimd.tensor_scalar(WH[:, slot, 0:width], RAW[:, slot, 0:width], 1.0, 1.0, ALU.mult, ALU.mult).then_inc(s_hi, 1)
                wait(pool, s_hi, i, n, u0 + j + 1)
                nc.gpsimd.tensor_tensor(WL[:, slot, 0:width], RAW[:, slot, 0:width],
                                        WH[:, slot, 0:width].bitcast(F32), ALU.subtract).then_inc(s_split, 1)

            def split_unit(name, n):
                split(UNITS[name][0] + n, 0, NS, 0, UW)

            each_unit(pool, split, 0, UNITS["wo"][0] + NS)
            pool.wait_ge(s_ysr, 1)
            for i in range(NT):
                nc.gpsimd.tensor_tensor(YA[:, i, :], YA[:, i, :], YS[:, i:i + 1].to_broadcast([P, CW]), ALU.mult
                                        ).then_inc(s_yan, 1)
            each_unit(pool, split, UNITS["wo"][0] + NS, UNITS["bva"][0])
            split_unit("bva", 0)
            split_unit("bva", 1)
            split_unit("small", 0)
            pool.wait_ge(s_used, UNITS["bva"][0])
            for n, (t, name, k) in enumerate(((QS, "bvb", 0), (KS, "bvb", 1), (QB, "kq0", 0), (KB_, "kq0", 1))):
                nc.gpsimd.memset(t[:], 0.0).then_inc(s_lz, 1)
                split_unit(name, k)

            def distance(h, l):
                b = (BIG + SMALL)[l]
                g = NL * h + l
                if l == 0:
                    pool.wait_ge(s_xg, h + 1)
                if g == 0:
                    pool.wait_ge(s_stk, 1)
                if g >= 3:
                    pool.wait_ge(s_lv, g - 2)
                x = CUM[h].rearrange("p (n w) -> p n w", w=2 * b)
                ref = x[:, :, b - 1:b].to_broadcast([P, T // (2 * b), 2 * b])
                nc.gpsimd.tensor_tensor(DIST[g % 3].rearrange("p (n w) -> p n w", w=2 * b), x, ref,
                                        ALU.subtract).then_inc(s_dd, 1)

            split_unit("ao", 0)
            split_unit("ao", 1)
            for l in range(NL):
                distance(0, l)
                if l == 2 or l == 5:
                    split_unit("ao", 2 + l // 5)
            for h, first, second in ((1, (("kq1", 0), ("kq1", 1), ("aqk", 0)), (("aqk", 1), ("aqk", 2))),
                                     (2, (("aqk", 3),), ()),
                                     (3, (("av", 0), ("av", 1)), (("av", 2), ("av", 3)))):
                for l in range(3):
                    distance(h, l)
                for u in first:
                    split_unit(*u)
                for l in range(3, NL):
                    distance(h, l)
                for u in second:
                    split_unit(*u)
            pool.wait_ge(s_bsr, 1)
            for h in range(H2):
                y = YB[:, h, :].rearrange("p (i c) -> p i c", i=NT)
                r = BSS[:, NT * h:NT * h + NT].rearrange("p (i o) -> p i o", o=1).to_broadcast([P, NT, DV])
                nc.gpsimd.tensor_tensor(y, y, r, ALU.mult).then_inc(s_ybr, 1)
            each_unit(pool, split, UNITS["br"][0], UNITS["wo2"][0] + NS)
            for m in range(H2):
                pool.wait_ge(s_y2h, m + 1)
                nc.gpsimd.tensor_tensor(YL[:, H2 + m, :], BR[:, m, :], YH[:, H2 + m, :].bitcast(F32),
                                        ALU.subtract).then_inc(s_y2p, 1)
            each_unit(pool, split, UNITS["wo2"][0] + NS, UNITS["ffn2"][0] + NS)

            def over_rms(n, mix, done, tiles):
                ge(pool, s_rs[n], 1)
                pool.wait_ge(done, DK)
                for m in tiles:
                    nc.gpsimd.tensor_tensor(mix[:, m, :], mix[:, m, :], RS[:], ALU.mult).then_inc(s_mn, 1)

            over_rms("post", MIX, s_mix, range(DK))
            each_unit(pool, split, UNITS["ffn2"][0] + NS, NU)
            over_rms("fpost", MIX2, s_mix2, range(OWN, DK))

        @block.tensor
        def _(pe):
            def mm3(o, lh, ll, rh, rl, start, stop):
                nc.tensor.matmul(o, lh, rh, start=start, stop=False)
                nc.tensor.matmul(o, lh, rl, start=False, stop=False)
                return nc.tensor.matmul(o, ll, rh, start=False, stop=stop)

            def ready(u):
                pe.wait_ge(s_split, u + 1)

            def col_tiles(u, slots, tiles, o, hi, lo, each=None, start=True, stop=True):
                s = u % NS
                for n, k in zip(slots, tiles):
                    if each is not None:
                        ge(pe, each, k + 1)
                    c = tokens(n)
                    ins = mm3(o, WH[:, s, c], WL[:, s, c], hi[:, k, :], lo[:, k, :],
                              start and n == slots[0], stop and n == slots[-1])
                return ins

            def col_unit(u, o, hi, lo, each=None):
                return col_tiles(u, range(DK), range(DK), o, hi, lo, each)

            def side_by_side(u0, banks, hi, lo, each, before):
                for n in range(len(banks)):
                    ready(u0 + n)
                for k in range(DK):
                    if k in before:
                        before[k]()
                    ge(pe, each, k + 1)
                    for n, b in enumerate(banks):
                        s = (u0 + n) % NS
                        ins = mm3(pb[b], WH[:, s, tokens(k)], WL[:, s, tokens(k)], hi[:, k, :], lo[:, k, :],
                                  k == 0, k == DK - 1)
                        if k == DK - 1:
                            ins.then_inc(s_used, 1)

            def row_unit(u, n, hi, lo, banks=4, each=None):
                s = u % NS
                if each is not None:
                    ge(pe, each, 2 * n + 2)
                for t in range(NT):
                    for kk in range(2):
                        k = 2 * n + kk
                        c = slice(kk * T, (kk + 1) * T)
                        ins = mm3(pb[banks + t], hi[:, k, tokens(t)], lo[:, k, tokens(t)], WH[:, s, c], WL[:, s, c],
                                  k == 0, k == DK - 1)
                return ins

            def statistic(n, with_columns=False, bank=6):
                ge(pe, s_acc[n], DK)
                ins = nc.tensor.matmul(pb[bank], INVD, ACC[:], start=True, stop=True)
                if with_columns:
                    for t in range(NT):
                        ins = nc.tensor.matmul(pb[bank + 1][:, t:t + 1], ACC[:, tokens(t)], INVD[:, 0:1],
                                               start=True, stop=True)
                ins.then_inc(s_ms[n].sem, 1)

            pe.wait_ge(s_cst, 16)
            u0 = UNITS["qk"][0]

            def head_sums(u):
                pe.wait_ge(s_zsq, u + 1)
                if u >= 2:
                    pe.wait_ge(s_hsd, u - 1)
                nc.tensor.matmul(pb[2 + u % 2], BONE, TMP[:, 2 + u % 2, :], start=True, stop=True
                                 ).then_inc(s_hms, 1)

            for u in range(8):
                ready(u0 + u)
                if u >= 2:
                    pe.wait_ge(s_z, u - 1)
                col_unit(u0 + u, pb[u % 2], AH, AL, s_gl["mix"] if u == 0 else None).then_inc(s_used, 1)
                if u == 0:
                    statistic("mix", True)
                if u >= 1:
                    head_sums(u - 1)

            for n in range(4):
                u = UNITS["v"][0] + n
                ready(u)
                if n == 0:
                    ge(pe, s_sd["mix"], 1)
                    pe.wait_ge(s_rcd, 1)
                row_unit(u, n, AH, AL).then_inc(s_used, 1)
                if n == 0:
                    head_sums(7)

            steps = NT * H1

            def score_step(n):
                i, h = NT - 1 - n // H1, n % H1
                w, hp, ht = (i + 1) * P, (h % 2) * HD, h // 2
                if n == 0:
                    pe.wait_ge(s_qk, 8)
                    pe.wait_ge(s_hsd, 8)
                if n >= 2:
                    pe.wait_ge(s_sc, n - 1)
                nc.tensor.matmul(pb[2 + n % 2][:, 0:w], QT[hp:hp + HD, ht, tokens(i)], KT[hp:hp + HD, ht, 0:w],
                                 start=True, stop=True).then_inc(s_s, 1)

            def turn_step(n):
                i = NT - 1 - n // H1
                pe.wait_ge(s_e, n + 1)
                if n == 0:
                    pe.wait_ge(s_v, NT)
                if n >= 2:
                    pe.wait_ge(s_ptc, n - 1)
                for j in range(i + 1):
                    ins = nc.tensor.transpose(pb[4 + n % 2][:, tokens(j)], SC[:, n % 2, tokens(j)], IDENT)
                ins.then_inc(s_pt, 1)

            def value_step(n):
                i, h = NT - 1 - n // H1, n % H1
                pe.wait_ge(s_ptc, n + 1)
                if n >= 2:
                    pe.wait_ge(s_ya, n - 1)
                for j in range(i + 1):
                    ins = nc.tensor.matmul(pb[6 + n % 2][:, 0:HD], PT[:, n % 2, tokens(j)],
                                           V[:, j, h * HD:(h + 1) * HD], start=(j == 0), stop=(j == i))
                ins.then_inc(s_pv, 1)

            for n in range(steps + 2):
                if n < steps:
                    score_step(n)
                    for t in range(3 * n, 3 * n + 3):
                        cu, k = divmod(t, DK)
                        u = UNITS["conv"][0] + cu
                        if k == 0:
                            ready(u)
                            if cu == 0:
                                pe.wait_ge(s_z, 8)
                            if cu >= 2:
                                pe.wait_ge(s_cuf, cu - 1)
                        ins = mm3(pb[cu % 2], WH[:, u % NS, tokens(k)], WL[:, u % NS, tokens(k)],
                                  AH[:, k, :], AL[:, k, :], k == 0, k == DK - 1)
                        if k == DK - 1:
                            ins.then_inc(s_used, 1)
                if 1 <= n <= steps:
                    turn_step(n - 1)
                if n >= 2:
                    value_step(n - 2)

            pe.wait_ge(s_ycacc, CK)
            pe.wait_ge(s_cuf, 12)
            nc.tensor.matmul(pb[0], INVD, ACC[:], start=True, stop=True).then_inc(s_ycms, 1)
            def turn_attention():
                pe.wait_ge(s_ptc, steps)
                pe.wait_ge(s_ya, steps)
                for i in range(NT):
                    pe.wait_ge(s_yan, i + 1)
                    for b in range(CK):
                        ins = nc.tensor.transpose(pb[4 + b][:, tokens(i)], YA[:, i, tokens(b)], IDENT)
                ins.then_inc(s_yt, 1)

            pe.wait_ge(s_ycsd, 1)
            pe.wait_ge(s_sc, steps)
            side_by_side(UNITS["wo"][0], range(NS), YH, YL, s_yl, {CK: turn_attention})
            for m in range(NS, DK):
                ready(UNITS["wo"][0] + m)
                ge(pe, s_x["ffn"], m - NS + 1)
                col_unit(UNITS["wo"][0] + m, pb[m % NS], YH, YL).then_inc(s_used, 1)

            def ffn(f, norm, down, free):
                S, u0 = FS[f], UNITS[f][0]

                def chunks(i):
                    for j in range(2):
                        for w, s in enumerate((S["pad"], S["up"])):
                            u = u0 + 2 * j + w
                            wait(pe, s_split, i, NS, u + 1)
                            wait(pe, s, i, 2, j - 1)
                            col_unit(u, pb[2 * j + w], AH, AL).then_inc(s_used, 1)

                if f == "ffn2":
                    pe.wait_ge(s_mix, DK)
                else:
                    ge(pe, s_x["ffn"], DK)
                side_by_side(u0, range(4), AH, AL, s_gl[norm], {DK - 1: lambda: statistic(norm)})
                with pe.Fori(1, FC // 2) as i:
                    chunks(i)

                u0 = UNITS[down][0]

                def down_pair(i):
                    for j in range(2):
                        k0 = 0
                        wait(pe, free, i, 2, j - 1)
                        for q, nt in enumerate(DOWN_TILES):
                            u = u0 + NS * j + q
                            wait(pe, s_split, i, 2 * NS, u + 1)
                            if q == 3 and isinstance(i, int) and j == 0:
                                ge(pe, S["sl"], FC)
                            ins = col_tiles(u, range(nt), range(k0, k0 + nt), pb[4 + j], SH, SL,
                                            start=(q == 0), stop=(q == 3))
                            ins.then_inc(s_used, 1)
                            k0 += nt

                ge(pe, S["sl"], FC - 1)
                down_pair(0)
                with pe.Fori(1, DK // 2) as i:
                    down_pair(i)

            ffn("ffn", "ffn", "down", s_x["ple"])

            pe.wait_ge(s_pl, 2)
            for m in range(DK):
                u = UNITS["pproj"][0] + m // 4
                ready(u)
                if m >= 4:
                    pe.wait_ge(s_pp, m - 3)
                ins = col_tiles(u, range(2 * (m % 4), 2 * (m % 4) + 2), range(2), pb[PBANK[m % 4]], PH, PL)
                if m % 4 == 3:
                    ins.then_inc(s_used, 1)
                else:
                    ins.then_inc(s_ppj, 1)
                if m == 3:
                    statistic("ple")
            for m in range(DK):
                u = UNITS["pgate"][0] + m
                ready(u)
                if m == 1:
                    pe.wait_ge(s_pp, DK)
                if m >= 2:
                    pe.wait_ge(s_pgt, m - 1)
                col_unit(u, pb[m % 2], AH, AL, s_gl["ple"] if m == 0 else None).then_inc(s_used, 1)

            def key_query_units(pair, bank):
                for n in range(2):
                    u = UNITS[f"kq{pair}"][0] + n
                    ready(u)
                    col_unit(u, pb[bank + n], GH, GL).then_inc(s_used, 1)

            def decay_gates(pair, bank):
                for n in range(2):
                    h = 2 * pair + n
                    nc.tensor.matmul(pb[bank + n], SA[64:96, 1, h * P:(h + 1) * P], SQ[64:96, 0, :],
                                     start=True, stop=True).then_inc(s_gpr, 1)

            ge(pe, s_sd["ple"], 1)
            for n in range(2):
                u = UNITS["bva"][0] + n
                ready(u)
                row_unit(u, n, GH, GL, each=s_gl["mix2"]).then_inc(s_used, 1)
            u = UNITS["small"][0]
            ready(u)
            pe.wait_ge(s_pgt, DK)
            col_unit(u, pb[0], GH, GL, s_gl["mix2"]).then_inc(s_used, 1)
            statistic("mix2", True, bank=2)
            for n in range(2, 4):
                u = UNITS["bvb"][0] + n - 2
                ready(u)
                row_unit(u, n, GH, GL).then_inc(s_used, 1)
                if n == 2:
                    pe.wait_ge(s_row, 1)
                    pe.wait_ge(s_sel, 16)
                    ge(pe, s_sd["mix2"], 1)
                    pe.wait_ge(s_rcd, 2)
                    decay_gates(0, 2)
            pe.wait_ge(s_row, 1)
            key_query_units(0, 0)
            pe.wait_ge(s_vb, NT)
            for n in range(4):
                u = UNITS["ao"][0] + n
                ready(u)
                row_unit(u, n, GH, GL).then_inc(s_used, 1)
            pe.wait_ge(s_stk, 1)
            pe.wait_ge(s_gr, 2)
            for t in range(NT):
                ins = nc.tensor.transpose(pb[3][:, tokens(t)], SA[:, 0, tokens(t)], IDENT)
            ins.then_inc(s_stt, 1)

            def level_step(h, j):
                n = NT * h + j
                if j == 0:
                    pe.wait_ge(s_lv, NL * (h + 1))
                    if h == 0:
                        pe.wait_ge(s_dup, 2)
                if n == 1:
                    pe.wait_ge(s_aof, NT)
                    decay_gates(1, 4)
                if n >= 2:
                    pe.wait_ge(s_sad, n - 1)
                for l in range(8):
                    k, q = (KS[:, l, tokens(j)], QS[:, l, tokens(j)]) if l < 7 else \
                        (K2[:, h % 2, tokens(j)], Q2[:, h % 2, tokens(j)])
                    ins = nc.tensor.matmul(PS[:, SBANK[n % 2] + l // 4, (l % 4) * P:(l % 4 + 1) * P], k, q,
                                           start=True, stop=True)
                ins.then_inc(s_gs, 1)
                if n:
                    pe.wait_ge(s_sao, n)
                for l, tiles in ((0, slice(2 * P, T) if j < 2 else slice(0, 2 * P)), (1, tokens(j ^ 1))):
                    ins = nc.tensor.matmul(pb[0][:, tiles], KB_[:, l, tokens(j)], QB[:, l, tiles],
                                           start=True, stop=True)
                ins.then_inc(s_gb, 1)

            def mix_step(h, j):
                n = NT * h + j
                pe.wait_ge(s_sad, n + 1)
                pe.wait_ge(s_sao, n + 1)
                if j == 0:
                    if h:
                        pe.wait_ge(s_oc, h)
                    else:
                        pe.wait_ge(s_cols, 1)
                for i in range(NT):
                    ins = nc.tensor.matmul(pb[3][:, tokens(i)], SA[:, j % 2, tokens(i)],
                                           VB[:, j, h * DV:(h + 1) * DV], start=(i == 0 and j == 0),
                                           stop=(i == NT - 1 and j == NT - 1), skip_group_check=True)
                ins.then_inc(s_go, 1)

            for h in range(H2):
                if h == 1:
                    pe.wait_ge(s_gr, H2)
                    key_query_units(1, 4)
                if h >= 2:
                    for m in range(2 * h - 4, 2 * h - 2):
                        u = UNITS["aqk"][0] + m
                        ready(u)
                        if m < 2:
                            pe.wait_ge(s_dup, 4)
                        else:
                            pe.wait_ge(s_apad, m - 1)
                        col_unit(u, pb[4 + m % 2], GH, GL).then_inc(s_used, 1)
                for j in range(NT + 1):
                    if j < NT:
                        level_step(h, j)
                    if j:
                        mix_step(h, j - 1)

            pe.wait_ge(s_apad, 4)
            pe.wait_ge(s_sad, NT * H2)
            for n in range(4):
                u = UNITS["av"][0] + n
                ready(u)
                row_unit(u, n, GH, GL).then_inc(s_used, 1)

            def state_bank(d, i):
                n = NT * d + i
                return PS[:, 4 + n // 3, (n % 3) * (DV + 1):(n % 3 + 1) * (DV + 1)]

            def stabilisers(h):
                if h == 0:
                    pe.wait_ge(s_zero, 32)
                    pe.wait_ge(s_sad, 4 * NT)
                    pe.wait_ge(s_sao, 4 * NT)
                else:
                    pe.wait_ge(s_bcc, 2 * h)
                for d in range(2):
                    r = h + H2 * d
                    ins = nc.tensor.matmul(pb[d], SEL[0:8, r * P:(r + 1) * P], MROWS[d], start=True, stop=True)
                ins.then_inc(s_bc, 1)

            def lstm_scores(n):
                h, j = divmod(n, NT)
                hp, ht = (h % 2) * HD, h // 2
                if n == 0:
                    pe.wait_ge(s_aqk, 4)
                    pe.wait_ge(s_oc, H2)
                if n >= 2:
                    pe.wait_ge(s_sw, 2 * (n - 1))
                nc.tensor.matmul(pb[2 + n % 2], AK[hp:hp + HD, ht, tokens(j)], AQ[hp:hp + HD, ht, :],
                                 start=True, stop=True).then_inc(s_ms2, 1)

            def lstm_mix(n):
                h, j = divmod(n, NT)
                if n == 0:
                    pe.wait_ge(s_va, NT + 1)
                if j == 0 and h:
                    pe.wait_ge(s_num, h)
                for d in range(2):
                    pe.wait_ge(s_sw, 2 * n + d + 1)
                    tiles = range(j, NT) if d == 0 else range(0, j + 1)
                    for i in tiles:
                        m = NT * d + i
                        first = j == (0 if d == 0 else i) and m % 3 == 0
                        ins = nc.tensor.matmul(state_bank(d, i), WT[:, n % 2, d, tokens(i)], VA[:, j, h, :],
                                               start=first, stop=(j == NT - 1), skip_group_check=True)
                ins.then_inc(s_mo, 1)

            def output_gate(n):
                m, third = divmod(n, 3)
                u = UNITS["br"][0] + m
                if third == 0:
                    ready(u)
                    if m:
                        pe.wait_ge(s_brr, m)
                    else:
                        pe.wait_ge(s_va, NT + 1)
                ks = (range(0, 3), range(3, 6), range(6, 8))[third]
                ins = col_tiles(u, ks, ks, pb[7], GH, GL, start=(third == 0), stop=(third == 2))
                if third == 2:
                    ins.then_inc(s_used, 1)

            def turn_output(n):
                if n < H2:
                    pe.wait_ge(s_ybr, n + 1)
                else:
                    pe.wait_ge(s_ym, n - H2 + 1)
                if 3 <= n < 7:
                    pe.wait_ge(s_yg, n - 2)
                src = YB[:, n, :] if n < H2 else YM[:, n - H2, :]
                for i in range(NT):
                    ins = nc.tensor.transpose(pb[TBANK[n]][:, tokens(i)], src[:, tokens(i)], IDENT)
                ins.then_inc(s_y2t, 1)

            stabilisers(0)
            for n in range(NT * H2 + 1):
                if n < NT * H2:
                    lstm_scores(n)
                if n < 3 * H2:
                    output_gate(n)
                    if n % NT == 1:
                        stabilisers(n // NT + 1)
                elif n == 3 * H2 + 1:
                    pe.wait_ge(s_brr, H2)
                    pe.wait_ge(s_bcc, 2 * H2)
                    for m in range(3):
                        turn_output(m)
                elif n == 3 * H2 + 2:
                    turn_output(3)
                elif n == 3 * H2 + 3:
                    for m in range(4, 7):
                        turn_output(m)
                if n:
                    lstm_mix(n - 1)

            pe.wait_ge(s_sw, 2 * NT * H2)
            pe.wait_ge(s_y2l, 2)
            u0 = UNITS["wo2"][0]
            order = (4, 5, 6, 7, 0, 1, 2, 3)
            for n in range(NS):
                ready(u0 + n)
            for q, k in enumerate(order):
                if q == 5:
                    pe.wait_ge(s_num, H2)
                    turn_output(7)
                if k >= H2:
                    pe.wait_ge(s_y2p, k - H2 + 1)
                else:
                    pe.wait_ge(s_y2l, k + 1)
                for n in range(NS):
                    s = (u0 + n) % NS
                    ins = mm3(pb[n], WH[:, s, tokens(k)], WL[:, s, tokens(k)], YH[:, k, :], YL[:, k, :],
                              q == 0, q == DK - 1)
                    if q == DK - 1:
                        ins.then_inc(s_used, 1)
            for m in range(NS, DK):
                ready(u0 + m)
                pe.wait_ge(s_mix, m - NS + 1)
                col_unit(u0 + m, pb[m % NS], YH, YL).then_inc(s_used, 1)
            statistic("post")
            ge(pe, s_sd["post"], 1)
            ffn("ffn2", "ffn2", "down2", s_mix2)
            statistic("fpost")
        @block.scalar
        def _(act):
            n_ac = [0]

            def link(ins):
                n_ac[0] += 1
                ins.then_inc(s_ac, 1)
                act.wait_ge(s_ac, n_ac[0])

            A = nc.scalar.activation

            def norm_tile(n, gain, i, per, j, hi, x=None, split=True):
                src = at(X, i, j, per) if x is None else x
                if split:
                    wait(act, s_x[n], i, per, j + 1)
                    A(at(hi, i, j, per), src, ACT.Copy, scale=prm_at(gain, 0, i, per, j)).then_inc(s_gh[n].sem, 1)
                wait(act, s_acc[n], i, per, j - 1)
                A(SQ[:, j % 2, :], src, ACT.Square).then_inc(s_sq[n].sem, 1)

            def norm_root(n, bank=6):
                ge(act, s_ms[n], 1)
                A(RS[:], pb[bank], ACT.Sqrt, bias=EPS_C).then_inc(s_sd[n].sem, 1)

            act.wait_ge(s_prm, 16)
            for k in range(DK):
                if k % 2 == 0:
                    act.wait_ge(s_xin[k // 2], 16)
                A(AH[:, k, :], X[:, k, :], ACT.Copy, scale=prm("g_mix", k)).then_inc(s_gh["mix"].sem, 1)
                if k >= 2:
                    ge(act, s_acc["mix"], k - 1)
                A(SQ[:, k % 2, :], X[:, k, :], ACT.Square).then_inc(s_sq["mix"].sem, 1)
            norm_root("mix")
            A(RC, pb[7][:, 0:NT], ACT.Sqrt, bias=EPS_C).then_inc(s_rcd, 1)

            def head_root(u):
                act.wait_ge(s_hms, u + 1)
                q = u < CK
                A(SC[:, u % 2, :], pb[2 + u % 2], ACT.Sqrt, bias=EPS64_C if q else EPS_C,
                  scale=1.0 if q else 1.0 / HD).then_inc(s_hsd, 1)

            for u in range(8):
                act.wait_ge(s_z, u + 1)
                if u >= 2:
                    act.wait_ge(s_hms, u - 1)
                A(TMP[:, 2 + u % 2, :], TMP[:, u % 2, :], ACT.Square).then_inc(s_zsq, 1)
                if u >= 1:
                    if u >= 3:
                        act.wait_ge(s_qk, u - 2)
                    head_root(u - 1)
            act.wait_ge(s_qk, 6)
            head_root(7)
            act.wait_ge(s_rc, 1)
            act.wait_ge(s_used, UNITS["v"][0] + 4)
            for t in range(NT):
                A(V[:, t, :], pb[4 + t], ACT.Copy, scale=RC[:, t:t + 1]).then_inc(s_v, 1)

            def conv_first(j):
                act.wait_ge(s_cx, j + 1)
                if j == 0:
                    act.wait_ge(s_qk, 8)
                    act.wait_ge(s_hms, 8)
                if j >= 1:
                    act.wait_ge(s_yc, j)
                A(TMP[:, 2, :], PAD[:, 0, 0:T], ACT.Identity, bias=prm("cb", j), scale=prm("cw", j)
                  ).then_inc(s_c0, 1)

            def conv_square(j):
                act.wait_ge(s_yc, j + 1)
                if j == 0:
                    ge(act, s_ms["mix"], 1)
                if j >= 2:
                    act.wait_ge(s_ycacc, j - 1)
                A(SQ[:, j % 2, :], YC[:, j, :], ACT.Square).then_inc(s_ycsq, 1)

            def attention_square(i):
                act.wait_ge(s_ya, H1 * (NT - i))
                A(TMP[:, 3, :], YA[:, i, :], ACT.Square, accum_out=YS[:, i:i + 1]).then_inc(s_yss, 1)
                act.wait_ge(s_yss, NT - i)

            steps = NT * H1
            for n in range(steps + 1):
                if n < steps:
                    w = (NT - n // H1) * P
                    act.wait_ge(s_nm, n + 1)
                    A(SC[:, n % 2, 0:w], SC[:, n % 2, 0:w], ACT.Exp, bias=NM[:, n:n + 1],
                      accum_out=DEN[:, n:n + 1]).then_inc(s_e, 1)
                if n >= 1:
                    m = n - 1
                    w = (NT - m // H1) * P
                    act.wait_ge(s_pt, m + 1)
                    if m >= 2:
                        act.wait_ge(s_pv, m - 1)
                    A(PT[:, m % 2, 0:w], pb[4 + m % 2][:, 0:w], ACT.Copy).then_inc(s_ptc, 1)
                if n % H1 == 4 and n > H1:
                    attention_square(NT - n // H1)
                if n % 8 == 6:
                    conv_first(n // 8)
                if n % 8 == 1 and n > 8:
                    conv_square(n // 8 - 1)
            conv_square(3)
            attention_square(0)
            link(A(YS, YS, ACT.Sqrt, bias=EPS_C, scale=1.0 / CW))
            act.wait_ge(s_ycms, 1)
            A(TMP[:, 3, :], pb[0], ACT.Sqrt, bias=EPS_C, scale=float(D) / CW).then_inc(s_ycsd, 1)
            for j in range(CK):
                act.wait_ge(s_yn, j + 1)
                A(YH[:, j, :], SC[:, j % 2, :], ACT.Copy).then_inc(s_ynh, 1)
            act.wait_ge(s_yt, 1)
            act.wait_ge(s_yl, CK)
            for b in range(CK):
                A(YH[:, CK + b, :], pb[4 + b], ACT.Copy, scale=prm("g_oa", b)).then_inc(s_yh, 1)
            def x_tiles(n, gain, hi):
                for m in range(DK):
                    norm_tile(n, gain, m // 2, 2, m % 2, hi)

            x_tiles("ffn", "g_ffn", AH)

            def ffn(f, norm, func, down):
                S = FS[f]
                norm_root(norm)

                def chunk(i, j):
                    wait(act, S["pad"], i, 2, j + 1)
                    wait(act, S["h"], i, 2, j - 1)
                    A(TMP[:, j, :], PAD[:, j, 0:T], ACT.Identity, bias=prm_at("fcb" + sfx, 0, i, 2, j),
                      scale=prm_at("fcw" + sfx, 0, i, 2, j)).then_inc(S["t1"].sem, 1)
                    wait(act, S["t3"], i, 2, j + 1)
                    A(TMP[:, j, :], TMP[:, j, :], func).then_inc(S["act"].sem, 1)
                    wait(act, S["h"], i, 2, j + 1)
                    A(at(SH, i, j, 2), TMP[:, 2 + j, :], ACT.Copy).then_inc(S["sh"].sem, 1)

                sfx = "" if f == "ffn" else "2"
                for j in range(2):
                    chunk(0, j)
                with act.Fori(1, FC // 2) as i:
                    for j in range(2):
                        chunk(i, j)

                u0 = UNITS[down][0]
                if f == "ffn":
                    ge(act, S["sl"], FC)
                    act.dma_start(PIN[:], dram["p"]).then_inc(s_pin, 16)
                    act.wait_ge(s_pin, 16)
                    for q in range(2):
                        A(PH[:, q, :], PIN[:, q, :], ACT.Copy).then_inc(s_ph, 1)

                def tile(i, j):
                    if f == "ffn":
                        norm_tile("ple", "g_ple", i, 2, j, AH)
                    else:
                        wait(act, s_used, i, 2 * NS, u0 + NS * (j + 1))
                        norm_tile("fpost", None, i, 2, j, None, x=pb[4 + j], split=False)
                        A(at(MIX2, i, j, 2), pb[4 + j], ACT.Copy, scale=prm_at("fpost2", 0, i, 2, j)
                          ).then_inc(s_mix2, 1)

                for j in range(2):
                    tile(0, j)
                with act.Fori(1, DK // 2) as i:
                    for j in range(2):
                        tile(i, j)

            ffn("ffn", "ffn", ACT.Silu, "down")

            for m in range(DK):
                if m % 4 == 3:
                    act.wait_ge(s_used, UNITS["pproj"][0] + m // 4 + 1)
                else:
                    act.wait_ge(s_ppj, m - m // 4 + 1)
                A(PP[:, m, :], pb[PBANK[m % 4]], ACT.Copy).then_inc(s_pp, 1)
                if m == 3:
                    norm_root("ple")
                    act.dma_start(SA[64:96, 1, :], dram["gla_w"]).then_inc(s_sel, 16)
            for m in range(DK + 2):
                if m < DK:
                    act.wait_ge(s_pgt, m + 1)
                    A(SG[:, m, :], TMP[:, m % 2, :], ACT.Sigmoid).then_inc(s_sg, 1)
                if m >= 2:
                    norm_tile("mix2", "pre2", (m - 2) // 2, 2, m % 2, GH)

            norm_root("mix2", 2)
            A(RC, pb[3][:, 0:NT], ACT.Sqrt, bias=EPS_C).then_inc(s_rcd, 1)
            act.wait_ge(s_row, 1)
            rows = slice(0, 8)
            A(ROW[0], SQ[rows, 0, :], ACT.Identity, bias=prm("gib", 0, rows)).then_inc(s_gabs, 1)
            link(A(ROW[1], SQ[32:40, 0, :], ACT.Identity, bias=prm("gfb", 0, slice(32, 40))))
            link(A(ROW[2], ROW[1], ACT.Abs))
            link(A(ROW[2], ROW[2], ACT.Exp, scale=-1.0))

            def stack_rows():
                act.wait_ge(s_gabs, 2)
                for g, src in enumerate((ROW[2], ROW[1], SQ[rows, 1, :], ACC[rows, :])):
                    ins = A(SA[32 * g:32 * g + 8, 0, :], src, ACT.Copy)
                ins.then_inc(s_stk, 1)

            def gate_columns():
                act.wait_ge(s_stt, 1)
                link(A(CG, pb[3].rearrange("p (t g r) -> p t g r", t=NT, g=4)[:, :, :, 0:8], ACT.Copy))
                A(CG[:, :, 2:4, :], CG[:, :, 2:4, :], ACT.Exp, scale=-1.0).then_inc(s_cols, 1)

            def duplicate(h):
                pair, hh = divmod(h, 2)
                if pair:
                    act.wait_ge(s_gs, NT * (h - 1))
                for n, dst in enumerate((K2, Q2)):
                    act.wait_ge(s_dup, 2 * pair + n + 1)
                    for half in range(2):
                        ins = A(dst[half * HD:(half + 1) * HD, hh, :], KQ[pair][n][hh * HD:(hh + 1) * HD],
                                ACT.Copy, scale=0.125 if n else 1.0)
                    ins.then_inc(s_kqf, 1)

            def gate_exp(h):
                gate, log = GATE[h]
                act.wait_ge(s_gpr, h + 1)
                A(gate, pb[2 * (h // 2) + 2 + h % 2], ACT.Identity, bias=prm("glab", h)).then_inc(s_gr, 1)
                act.wait_ge(s_gr, h + 1)
                link(A(log, gate, ACT.Abs))
                A(log, log, ACT.Exp, scale=-1.0).then_inc(s_gx, 1)

            def gate_log(h):
                act.wait_ge(s_gx, h + 1)
                A(GATE[h][1], GATE[h][1], ACT.Ln, bias=ONE_C).then_inc(s_lax, 1)

            gate_exp(0)
            gate_exp(1)
            A(ROW[2], ROW[2], ACT.Ln, bias=ONE_C[rows]).then_inc(s_rw8, 1)
            gate_log(0)
            gate_log(1)
            act.wait_ge(s_rc, 2)
            act.wait_ge(s_used, UNITS["bvb"][0] + 2)
            for t in range(NT):
                A(VB[:, t, :], pb[4 + t], ACT.Copy, scale=RC[:, t:t + 1]).then_inc(s_vb, 1)
            stack_rows()
            act.wait_ge(s_xg, 2)
            duplicate(0)
            duplicate(1)
            act.dma_start(LM[:], dram["masks"]).then_inc(s_lm, 16)

            def decay_step(h, l):
                g, b = NL * h + l, (BIG + SMALL)[l]
                act.wait_ge(s_dd, g + 1)
                d = DIST[g % 3].rearrange("p (n s w) -> p n s w", s=2, w=b)
                A(d[:, :, 0, :], d[:, :, 0, :], ACT.Exp, scale=-1.0 / 16.0)
                A(d[:, :, 1, :], d[:, :, 1, :], ACT.Exp, scale=1.0 / 16.0).then_inc(s_ee, 1)

            def conv_pair(m):
                dst = (AQ if m < 2 else AK)[:, m % 2, :]
                act.wait_ge(s_apad, m + 1)
                A(dst, PAD[:, 0, 0:T], ACT.Identity, bias=prm("mcb", m), scale=prm("mcw", m)).then_inc(s_a1, 1)
                act.wait_ge(s_a3, m + 1)
                A(dst, dst, ACT.Silu).then_inc(s_aqk, 1)

            def head_out(h):
                act.wait_ge(s_go, NT * (h + 1))
                act.wait_ge(s_lv, NL * min(h + 1, H2))
                A(YB[:, h, :], pb[3], ACT.Copy).then_inc(s_oc, 1)

            for h in range(H2):
                for l in range(3 if h else 0, NL):
                    decay_step(h, l)
                if h:
                    head_out(h - 1)
                if h == 0:
                    gate_columns()
                    act.wait_ge(s_used, UNITS["ao"][0] + 4)
                    for t in range(NT):
                        A(AO[:, t, :], pb[4 + t], ACT.Sigmoid, scale=RC[:, t:t + 1]).then_inc(s_aof, 1)
                if h >= 2:
                    for m in range(2 * h - 4, 2 * h - 2):
                        conv_pair(m)
                for j in range(NT):
                    n = NT * h + j
                    if h == 0 and j == 1:
                        act.wait_ge(s_stk, 1)
                    if h == 0 and j in (1, 2):
                        gate_exp(1 + j)
                    if h == 0 and j == 3:
                        gate_log(2)
                        gate_log(3)
                    if h in (1, 2) and j == 2:
                        duplicate(h + 1)
                    if j == 3 and h < H2 - 1:
                        for l in range(3):
                            decay_step(h + 1, l)
                    act.wait_ge(s_gb, n + 1)
                    if n >= 2:
                        act.wait_ge(s_go, n - 1)
                    parts = [c for c in (slice(0, j * P), slice((j + 1) * P, T)) if c.stop > c.start]
                    for c in parts:
                        ins = A(SA[:, j % 2, c], pb[0][:, c], ACT.Copy)
                    ins.then_inc(s_sao, 1)
            head_out(H2 - 1)

            act.wait_ge(s_sad, 4 * NT)
            act.wait_ge(s_lv, 36)
            act.dma_start(SEL[:], dram["selectors"]).then_inc(s_zero, 16)
            act.dma_start(NEG[:], dram["negmask"]).then_inc(s_zero, 16)
            act.wait_ge(s_ybq, 1)
            A(BSS, BSS, ACT.Sqrt, bias=EPS_C, scale=1.0 / DV).then_inc(s_gn, 1)
            act.wait_ge(s_used, UNITS["av"][0] + 4)
            for t in range(NT):
                A(VA[:, t, :, 0:DV], pb[4 + t].rearrange("p (h c) -> p h c", h=H2), ACT.Copy,
                  scale=RC[:, t:t + 1]).then_inc(s_va, 1)

            def high_gated(heads):
                for m in heads:
                    act.wait_ge(s_yg, m + 1)
                    A(YH[:, H2 + m, :], BR[:, m, :], ACT.Copy).then_inc(s_y2h, 1)

            def high_turned(heads):
                for m in heads:
                    act.wait_ge(s_y2t, H2 + m + 1)
                    A(YH[:, m, :], pb[TBANK[H2 + m]], ACT.Copy, scale=prm("mnorm", m)).then_inc(s_y2h, 1)

            def stabilisers_copied(h):
                act.wait_ge(s_bc, h + 1)
                act.wait_ge(s_ybq, 1)
                if h >= 2:
                    act.wait_ge(s_ad, 2 * NT * (h - 1))
                    act.wait_ge(s_w, 2 * NT * (h - 1))
                for d in range(2):
                    A(STAB[h % 2][:, d, :], pb[d], ACT.Copy).then_inc(s_bcc, 1)

            def scaled_states(h):
                act.wait_ge(s_hb, h + 1)
                for i in range(NT):
                    m = NT + i
                    ins = A(TMP[:, h % 2, tokens(i)], NUM[:, m, 0:DV], ACT.Copy, scale=DN[:, m:m + 1])
                ins.then_inc(s_hst, 1)

            stabilisers_copied(0)
            for n in range(NT * H2 + 1):
                if n < NT * H2:
                    h, j = divmod(n, NT)
                    if j == 0:
                        act.wait_ge(s_bcc, 2 * h + 2)
                    for d in range(2):
                        c = CG[:, j, d, h + H2 * d:h + H2 * d + 1]
                        act.wait_ge(s_ad, 2 * n + d + 1)
                        off = slice((j + 1) * P, T) if d == 0 else slice(0, j * P)
                        if off.stop > off.start:
                            A(WT[:, n % 2, d, off], STAB[h % 2][:, d, off], ACT.Exp, bias=c)
                        A(WT[:, n % 2, d, tokens(j)], WT[:, n % 2, d, tokens(j)], ACT.Exp).then_inc(s_w, 1)
                    if j == 2 and h < H2 - 1:
                        stabilisers_copied(h + 1)
                if n and n % NT == 0:
                    h = n // NT - 1
                    act.wait_ge(s_mo, n)
                    if h:
                        act.wait_ge(s_hf, h)
                    for b, c in ((0, 3), (1, 3), (2, 2)):
                        ins = A(NUM[:, 3 * b:3 * b + c, :].rearrange("p q c -> p (q c)"),
                                PS[:, 4 + b, 0:c * (DV + 1)], ACT.Copy)
                    ins.then_inc(s_num, 1)
                if n % NT == 1 and n > 1:
                    scaled_states(n // NT - 1)
                if n == 3 * H2 + 1:
                    act.wait_ge(s_brr, H2)
                    for m in range(H2):
                        A(BR[:, m, :], BR[:, m, :], ACT.Silu).then_inc(s_br, 1)
                    act.wait_ge(s_ybq, 2)
                    A(MSS[:, 0:3 * NT], MSS[:, 0:3 * NT], ACT.Sqrt, bias=EPS_C, scale=1.0 / DV).then_inc(s_gn, 1)
                if n == 3 * H2 + 2:
                    high_gated(range(0, 3))
                if n == 3 * H2 + 3:
                    high_gated(range(3, 4))
                    high_turned(range(0, 3))
            scaled_states(H2 - 1)
            act.wait_ge(s_ybq, 3)
            A(MSS[:, 3 * NT:], MSS[:, 3 * NT:], ACT.Sqrt, bias=EPS_C, scale=1.0 / DV).then_inc(s_gn, 1)
            high_turned(range(3, 4))

            for m in range(DK):
                act.wait_ge(s_used, UNITS["wo2"][0] + m + 1)
                norm_tile("post", None, m // 2, 2, m % 2, None, x=pb[m % NS], split=False)
                A(MIX[:, m, :], pb[m % NS], ACT.Copy, scale=prm("post2", m)).then_inc(s_mix, 1)
            norm_root("post")
            x_tiles("ffn2", "fpre2", AH)
            ffn("ffn2", "ffn2", ACT.Gelu_apprx_tanh, "down2")
            norm_root("fpost")

        @block.vector
        def _(dve):
            V_ = nc.vector
            n_vc = [0]

            def link(ins):
                n_vc[0] += 1
                ins.then_inc(s_vc, 1)
                dve.wait_ge(s_vc, n_vc[0])

            def low(n, gain, i, per, j, hi, lo):
                wait(dve, s_gh[n], i, per, j + 1)
                V_.scalar_tensor_tensor(at(lo, i, j, per), at(X, i, j, per), prm_at(gain, 0, i, per, j),
                                        at(hi, i, j, per).bitcast(F32), ALU.mult, ALU.subtract
                                        ).then_inc(s_gl[n].sem, 1)

            def add_square(n, i, per, j):
                wait(dve, s_sq[n], i, per, j + 1)
                if isinstance(i, int) and i == 0 and j == 0:
                    V_.tensor_copy(ACC[:], SQ[:, 0, :]).then_inc(s_acc[n].sem, 1)
                else:
                    wait(dve, s_acc[n], i, per, j)
                    V_.tensor_tensor(ACC[:], ACC[:], SQ[:, j % 2, :], ALU.add).then_inc(s_acc[n].sem, 1)

            def norm_reciprocal(n, columns=0):
                ge(dve, s_sd[n], 1)
                V_.reciprocal(RS[:], RS[:]).then_inc(s_rs[n].sem, 1)
                ge(dve, s_rs[n], 1)
                if columns:
                    dve.wait_ge(s_rcd, columns)
                    V_.reciprocal(RC, RC).then_inc(s_rc, 1)

            link(V_.memset(PAD[:], 0.0))
            dve.wait_ge(s_prm, 16)
            for k in range(DK):
                low("mix", "g_mix", k // 2, 2, k % 2, AH, AL)
                add_square("mix", k // 2, 2, k % 2)
            norm_reciprocal("mix", 1)
            gq = UNITS["qk"][0]

            def normed(u):
                dve.wait_ge(s_hsd, u + 1)
                r = SC[:, u % 2, :]
                link(V_.reciprocal(r, r))
                V_.scalar_tensor_tensor((QT if u < CK else KT)[:, u % CK, :], TMP[:, u % 2, :],
                                        prm("qg" if u < CK else "kg"), r, ALU.mult, ALU.mult).then_inc(s_qk, 1)

            for u in range(8):
                dve.wait_ge(s_used, gq + u + 1)
                if u >= 2:
                    normed(u - 2)
                    dve.wait_ge(s_qk, u - 1)
                    dve.wait_ge(s_zsq, u - 1)
                V_.tensor_tensor(TMP[:, u % 2, :], pb[u % 2], RS[:], ALU.mult).then_inc(s_z, 1)
            for u in (6, 7):
                normed(u)

            uc = UNITS["conv"][0]

            def conv_c(j):
                dve.wait_ge(s_used, uc + 3 * j + 1)
                V_.tensor_tensor(TMP[:, 0, :], pb[(3 * j) % 2], RS[:], ALU.mult).then_inc(s_cuf, 1)

            def conv_x(j):
                dve.wait_ge(s_used, uc + 3 * j + 2)
                V_.tensor_tensor(TMP[:, 1, :], pb[(3 * j + 1) % 2], RS[:], ALU.mult).then_inc(s_cuf, 1)
                dve.wait_ge(s_cuf, 3 * j + 2)
                V_.tensor_tensor(PAD[:, 0, 2:T + 2], TMP[:, 0, :], TMP[:, 1, :], ALU.mult).then_inc(s_cx, 1)

            def conv_b(j):
                dve.wait_ge(s_c0, j + 1)
                t = TMP[:, 2, :]
                link(V_.scalar_tensor_tensor(t, PAD[:, 0, 1:T + 1], prm("cw", CK + j), t, ALU.mult, ALU.add))
                link(V_.scalar_tensor_tensor(t, PAD[:, 0, 2:T + 2], prm("cw", 2 * CK + j), t, ALU.mult, ALU.add))
                dve.wait_ge(s_used, uc + 3 * j + 3)
                V_.tensor_tensor(t, t, pb[(3 * j + 2) % 2], ALU.mult).then_inc(s_cuf, 1)
                dve.wait_ge(s_cuf, 3 * j + 3)
                V_.tensor_tensor(YC[:, j, :], t, RS[:], ALU.mult).then_inc(s_yc, 1)

            def conv_sum(j):
                dve.wait_ge(s_ycsq, j + 1)
                if j == 0:
                    V_.tensor_copy(ACC[:], SQ[:, 0, :]).then_inc(s_ycacc, 1)
                else:
                    dve.wait_ge(s_ycacc, j)
                    V_.tensor_tensor(ACC[:], ACC[:], SQ[:, j % 2, :], ALU.add).then_inc(s_ycacc, 1)

            def attention_out(n):
                i, h = NT - 1 - n // H1, n % H1
                dve.wait_ge(s_e, n + 1)
                link(V_.reciprocal(RD[:, n:n + 1], DEN[:, n:n + 1]))
                dve.wait_ge(s_pv, n + 1)
                V_.tensor_scalar(YA[:, i, h * HD:(h + 1) * HD], pb[6 + n % 2][:, 0:HD], RD[:, n:n + 1], None,
                                 ALU.mult).then_inc(s_ya, 1)

            dve.wait_ge(s_bt, 16)
            steps = NT * H1
            for n in range(steps + 3):
                if n < steps:
                    i, h = NT - 1 - n // H1, n % H1
                    w = (i + 1) * P
                    dve.wait_ge(s_s, n + 1)
                    if n >= 2:
                        dve.wait_ge(s_pt, n - 1)
                    V_.tensor_tensor_reduce(SC[:, n % 2, 0:w], pb[2 + n % 2][:, 0:w], BT[:, h, T - w:T], 1.0, -3e38,
                                            ALU.add, ALU.max, MX[:, n:n + 1]).then_inc(s_sc, 1)
                    dve.wait_ge(s_sc, n + 1)
                    V_.tensor_scalar(NM[:, n:n + 1], MX[:, n:n + 1], -1.0, None, ALU.mult).then_inc(s_nm, 1)
                if n >= 3:
                    attention_out(n - 3)
                j, r = divmod(n, 8)
                if r == 3 and j < CK:
                    if j:
                        dve.wait_ge(s_yc, j)
                    conv_c(j)
                if r == 5 and j < CK:
                    conv_x(j)
                if r == 0 and 1 <= j:
                    conv_b(j - 1)
                if r == 2 and 1 <= j:
                    conv_sum(j - 1)
            dve.wait_ge(s_ac, 1)
            V_.reciprocal(YS, YS).then_inc(s_ysr, 1)
            dve.wait_ge(s_ycsd, 1)
            link(V_.reciprocal(TMP[:, 3, :], TMP[:, 3, :]))
            for j in range(CK):
                if j >= 2:
                    dve.wait_ge(s_yl, j - 1)
                V_.scalar_tensor_tensor(SC[:, j % 2, :], YC[:, j, :], prm("g_oc", j), TMP[:, 3, :],
                                        ALU.mult, ALU.mult).then_inc(s_yn, 1)
                dve.wait_ge(s_ynh, j + 1)
                dve.wait_ge(s_yn, j + 1)
                V_.tensor_tensor(YL[:, j, :], SC[:, j % 2, :], YH[:, j, :].bitcast(F32), ALU.subtract
                                 ).then_inc(s_yl, 1)
            for b in range(CK):
                dve.wait_ge(s_yh, b + 1)
                V_.scalar_tensor_tensor(YL[:, CK + b, :], pb[4 + b], prm("g_oa", b),
                                        YH[:, CK + b, :].bitcast(F32), ALU.mult, ALU.subtract).then_inc(s_yl, 1)

            for m in range(DK):
                dve.wait_ge(s_used, UNITS["wo"][0] + m + 1)
                V_.tensor_tensor(X[:, m, :], X[:, m, :], pb[m % NS], ALU.add).then_inc(s_x["ffn"].sem, 1)
                if m:
                    low("ffn", "g_ffn", (m - 1) // 2, 2, (m - 1) % 2, AH, AL)
                    add_square("ffn", (m - 1) // 2, 2, (m - 1) % 2)
            add_square("ffn", 3, 2, 1)
            low("ffn", "g_ffn", 3, 2, 1, AH, AL)

            def ffn(f, norm, down):
                S, u0 = FS[f], UNITS[f][0]
                sfx, o = ("", 2) if f == "ffn" else ("2", 1)
                norm_reciprocal(norm)

                def up(i, j):
                    wait(dve, s_used, i, NS, u0 + 2 * j + 2)
                    wait(dve, S["sl"], i, 2, j - 1)
                    V_.tensor_tensor(TMP[:, 2 + j, :], pb[2 * j + 1], RS[:], ALU.mult).then_inc(S["up"].sem, 1)

                def chunk(i, j):
                    wait(dve, s_used, i, NS, u0 + 2 * j + 1)
                    wait(dve, S["t3"], i, 2, j - 1)
                    V_.tensor_tensor(PAD[:, j, o:o + T], pb[2 * j], RS[:], ALU.mult).then_inc(S["pad"].sem, 1)
                    if isinstance(i, int):
                        up(i, j)
                    wait(dve, S["t1"], i, 2, j + 1)
                    wait(dve, S["pad"], i, 2, j + 1)
                    t = TMP[:, j, :]
                    V_.scalar_tensor_tensor(t, PAD[:, j, 1:T + 1], prm_at("fcw" + sfx, FC, i, 2, j), t,
                                            ALU.mult, ALU.add).then_inc(S["ta"].sem, 1)
                    wait(dve, S["ta"], i, 2, j + 1)
                    V_.scalar_tensor_tensor(t, PAD[:, j, 2:T + 2], prm_at("fcw" + sfx, 2 * FC, i, 2, j), t,
                                            ALU.mult, ALU.add).then_inc(S["t3"].sem, 1)
                    if not isinstance(i, int):
                        up(i, j)
                    wait(dve, S["act"], i, 2, j + 1)
                    wait(dve, S["up"], i, 2, j + 1)
                    V_.tensor_tensor(TMP[:, 2 + j, :], TMP[:, j, :], TMP[:, 2 + j, :], ALU.mult
                                     ).then_inc(S["h"].sem, 1)
                    wait(dve, S["sh"], i, 2, j + 1)
                    V_.tensor_tensor(at(SL, i, j, 2), TMP[:, 2 + j, :], at(SH, i, j, 2).bitcast(F32),
                                     ALU.subtract).then_inc(S["sl"].sem, 1)

                for j in range(2):
                    chunk(0, j)
                with dve.Fori(1, FC // 2) as i:
                    for j in range(2):
                        chunk(i, j)

                u0 = UNITS[down][0]
                if f == "ffn":
                    for q in range(2):
                        dve.wait_ge(s_ph, q + 1)
                        V_.tensor_tensor(PL[:, q, :], PIN[:, q, :], PH[:, q, :].bitcast(F32), ALU.subtract
                                         ).then_inc(s_pl, 1)

                def tile(i, j):
                    if f == "ffn":
                        wait(dve, s_used, i, 2 * NS, u0 + NS * (j + 1))
                        V_.tensor_tensor(at(X, i, j, 2), at(X, i, j, 2), pb[4 + j], ALU.add
                                         ).then_inc(s_x["ple"].sem, 1)
                        low("ple", "g_ple", i, 2, j, AH, AL)
                        add_square("ple", i, 2, j)
                    else:
                        add_square("fpost", i, 2, j)

                for j in range(2):
                    tile(0, j)
                with dve.Fori(1, DK // 2) as i:
                    for j in range(2):
                        tile(i, j)

            ffn("ffn", "ffn", "down")

            norm_reciprocal("ple")

            def g4(m):
                low("mix2", "pre2", m // 2, 2, m % 2, GH, GL)
                add_square("mix2", m // 2, 2, m % 2)

            dve.wait_ge(s_pp, DK)
            for m in range(DK + 2):
                if m < DK:
                    dve.wait_ge(s_used, UNITS["pgate"][0] + m + 1)
                    if m >= 2:
                        dve.wait_ge(s_sg, m - 1)
                    V_.tensor_tensor(TMP[:, m % 2, :], pb[m % 2], RS[:], ALU.mult).then_inc(s_pgt, 1)
                if 1 <= m <= DK:
                    n = m - 1
                    dve.wait_ge(s_sg, n + 1)
                    V_.tensor_tensor(SG[:, n, :], SG[:, n, :], PP[:, n, :], ALU.mult).then_inc(s_pm, 1)
                    dve.wait_ge(s_pm, n + 1)
                    V_.tensor_tensor(X[:, n, :], X[:, n, :], SG[:, n, :], ALU.add).then_inc(s_x["mix2"].sem, 1)
                if m >= 2:
                    g4(m - 2)

            link(V_.memset(PAD[:, :, T + 1:T + 2], 0.0))
            norm_reciprocal("mix2", 2)
            rows = slice(0, 8)
            dve.wait_ge(s_used, UNITS["small"][0] + 1)
            V_.tensor_tensor(SQ[:, 0, :], pb[0], RS[:], ALU.mult).then_inc(s_row, 1)
            V_.memset(SA[:, 0, :], 0.0)
            dve.wait_ge(s_rw8, 1)
            LF, IG, B, BRV = ROW[3], ROW[0], SQ[rows, 1, :], ACC[rows, :]
            CF, CB, MF, MB = ROW[2], ROW[1], *MROWS
            link(V_.scalar_tensor_tensor(LF, ROW[1], 0.0, ROW[2], ALU.min, ALU.subtract))
            V_.tensor_tensor_scan(B, LF, LF, 0.0, ALU.add, ALU.min)
            link(V_.tensor_tensor_scan(BRV[:, ::-1], LF[:, ::-1], LF[:, ::-1], 0.0, ALU.add, ALU.min))
            V_.tensor_tensor(CF, IG, B, ALU.subtract)
            link(V_.tensor_tensor(CB, IG, BRV, ALU.subtract))
            V_.tensor_tensor_scan(MF, CF, CF, 0.0, ALU.max, ALU.max)
            link(V_.tensor_tensor_scan(MB[:, ::-1], CB[:, ::-1], CB[:, ::-1], 0.0, ALU.max, ALU.max))
            V_.tensor_tensor(B, B, MF, ALU.add)
            V_.tensor_tensor(BRV, BRV, MB, ALU.add).then_inc(s_gabs, 1)

            def projected(pair, bank):
                for n in range(2):
                    dve.wait_ge(s_used, UNITS[f"kq{pair}"][0] + n + 1)
                    V_.tensor_tensor(KQ[pair][n], pb[bank + n], RS[:], ALU.mult).then_inc(s_dup, 1)

            def cumulated(h):
                dve.wait_ge(s_lax, h + 1)
                gate, L = GATE[h]
                link(V_.scalar_tensor_tensor(L, gate, 0.0, L, ALU.min, ALU.subtract))
                V_.tensor_tensor_scan(CUM[h][0:HD], L[0:HD, :], L[0:HD, :], 0.0, ALU.add, ALU.min)
                V_.memset(CUM[h][HD:P, 0:1], 0.0)
                V_.tensor_tensor_scan(CUM[h][HD:P, 1:T], L[HD:P, 0:T - 1], L[HD:P, 0:T - 1], 0.0,
                                      ALU.add, ALU.min).then_inc(s_xg, 1)

            cumulated(0)
            cumulated(1)
            dve.wait_ge(s_xg, 2)
            projected(0, 0)
            dve.wait_ge(s_lz, 4)
            dve.wait_ge(s_lm, 16)

            def decayed(h, l):
                b = (BIG + SMALL)[l]
                q, k = (QB[:, l, :], KB_[:, l, :]) if l < 2 else (QS[:, l - 2, :], KS[:, l - 2, :])
                g = NL * h + l
                dve.wait_ge(s_ee, g + 1)
                if h and l == 0:
                    dve.wait_ge(s_gb, NT * h)
                v = [t.rearrange("p (n s w) -> p n s w", s=2, w=b) for t in
                     (q, k, Q2[:, h % 2, :], K2[:, h % 2, :], DIST[g % 3])]
                for half, (qs, ks) in enumerate(((1, 0), (0, 1))):
                    r = slice(half * HD, (half + 1) * HD)
                    V_.tensor_tensor(v[0][r, :, qs, :], v[2][r, :, qs, :], v[4][r, :, qs, :], ALU.mult)
                    ins = V_.tensor_tensor(v[1][r, :, ks, :], v[3][r, :, ks, :], v[4][r, :, ks, :], ALU.mult)
                ins.then_inc(s_lv, 1)

            def conv_tile(m):
                dve.wait_ge(s_used, UNITS["aqk"][0] + m + 1)
                if m:
                    dve.wait_ge(s_a3, m)
                V_.tensor_tensor(PAD[:, 0, 1:T + 1], pb[4 + m % 2], RS[:], ALU.mult).then_inc(s_apad, 1)
                dst = (AQ if m < 2 else AK)[:, m % 2, :]
                dve.wait_ge(s_apad, m + 1)
                dve.wait_ge(s_a1, m + 1)
                link(V_.scalar_tensor_tensor(dst, PAD[:, 0, 1:T + 1], prm("mcw", 4 + m), dst,
                                             ALU.mult, ALU.add))
                V_.scalar_tensor_tensor(dst, PAD[:, 0, 2:T + 2], prm("mcw", 8 + m), dst,
                                        ALU.mult, ALU.add).then_inc(s_a3, 1)

            masked = TMP[:, 0:2, :].rearrange("p a (l c) -> p (a l) c", c=P)
            for h in range(H2):
                dve.wait_ge(s_kqf, 2 * (h + 1))
                for l in range(NL):
                    decayed(h, l)
                if h == 1:
                    cumulated(2)
                    cumulated(3)
                    dve.wait_ge(s_xg, H2)
                    projected(1, 4)
                if h >= 2:
                    for m in range(2 * h - 4, 2 * h - 2):
                        conv_tile(m)
                for j in range(NT):
                    n = NT * h + j
                    dve.wait_ge(s_gs, n + 1)
                    if n >= 2:
                        dve.wait_ge(s_go, n - 1)
                    link(V_.tensor_tensor(masked, PS[:, SBANK[n % 2]:SBANK[n % 2] + 2, :].rearrange(
                                              "p a (l c) -> p (a l) c", c=P),
                                          LM.rearrange("p (l c) -> p l c", c=P), ALU.mult))
                    V_.tensor_reduce(SA[:, j % 2, tokens(j)], masked.rearrange("p l c -> p c l"),
                                     mybir.AxisListType.X, ALU.add).then_inc(s_sad, 1)
                    dve.wait_ge(s_sad, n + 1)

            def head_squares(y, h, sums, scratch):
                link(V_.tensor_tensor(scratch, y[:, h, :], y[:, h, :], ALU.mult))
                return V_.tensor_reduce(sums[:, NT * h:NT * h + NT], scratch.rearrange("p (i c) -> p i c", i=NT),
                                        mybir.AxisListType.X, ALU.add)

            def gated(h):
                for i in range(NT):
                    ins = V_.scalar_tensor_tensor(YM[:, h, tokens(i)], YM[:, h, tokens(i)],
                                                  MSS[:, NT * h + i:NT * h + i + 1], AO[:, i, tokens(h)],
                                                  ALU.mult, ALU.mult)
                ins.then_inc(s_ym, 1)

            dve.wait_ge(s_oc, H2)
            for h in range(H2):
                ins = head_squares(YB, h, BSS, TMP[:, 2, :])
                if h < H2 - 1:
                    link(ins)
            ins.then_inc(s_ybq, 1)
            dve.wait_ge(s_gs, 4 * NT)
            V_.memset(VA[:, :, :, DV:DV + 1], 1.0).then_inc(s_va, 1)
            dve.wait_ge(s_gn, 1)
            V_.reciprocal(BSS, BSS).then_inc(s_bsr, 1)

            dve.wait_ge(s_zero, 32)
            dve.wait_ge(s_go, 4 * NT)

            def exponents(n):
                h, j = divmod(n, NT)
                if j == 0:
                    dve.wait_ge(s_bcc, 2 * h + 2)
                if n >= 2:
                    dve.wait_ge(s_mo, n - 1)
                for d in range(2):
                    c = CG[:, j, d, h + H2 * d:h + H2 * d + 1]
                    V_.scalar_tensor_tensor(WT[:, n % 2, d, tokens(j)], STAB[h % 2][:, d, tokens(j)], c, NEG[:, d, :],
                                            ALU.add, ALU.add).then_inc(s_ad, 1)

            def weighted(n):
                j = n % NT
                dve.wait_ge(s_ms2, n + 1)
                for d in range(2):
                    dve.wait_ge(s_w, 2 * n + d + 1)
                    c = slice(j * P, T) if d == 0 else slice(0, (j + 1) * P)
                    w = WT[:, n % 2, d, c]
                    V_.scalar_tensor_tensor(w, pb[2 + n % 2][:, c], 0.125, w, ALU.mult, ALU.mult
                                            ).then_inc(s_sw, 1)

            def state_out(h):
                dve.wait_ge(s_num, h + 1)
                den = NUM[:, :, DV]
                link(V_.scalar_tensor_tensor(DN, den, -1.0, den, ALU.mult, ALU.max))
                for d in range(2):
                    m = DN[:, NT * d:NT * d + NT]
                    ins = V_.tensor_tensor(m, m, CG[:, :, 2 + d, h + H2 * d], ALU.max)
                link(ins)
                V_.reciprocal(DN, DN).then_inc(s_hb, 1)

            def state_sum(h):
                dve.wait_ge(s_hst, h + 1)
                for i in range(NT):
                    ins = V_.scalar_tensor_tensor(YM[:, h, tokens(i)], NUM[:, i, 0:DV], DN[:, i:i + 1],
                                                  TMP[:, h % 2, tokens(i)], ALU.mult, ALU.add)
                ins.then_inc(s_hf, 1)
                dve.wait_ge(s_hf, h + 1)
                ins = head_squares(YM, h, MSS, TMP[:, h % 2, :])
                if h >= 2:
                    ins.then_inc(s_ybq, 1)

            def gate_read(m):
                dve.wait_ge(s_used, UNITS["br"][0] + m + 1)
                V_.tensor_tensor(BR[:, m, :], pb[7], RS[:], ALU.mult).then_inc(s_brr, 1)

            def yb_gated(heads):
                for m in heads:
                    dve.wait_ge(s_y2t, m + 1)
                    dve.wait_ge(s_br, H2)
                    V_.scalar_tensor_tensor(BR[:, m, :], pb[TBANK[m]], prm("gnorm", m), BR[:, m, :],
                                            ALU.mult, ALU.mult).then_inc(s_yg, 1)

            def low_turned(heads):
                for m in heads:
                    dve.wait_ge(s_y2h, H2 + m + 1)
                    V_.scalar_tensor_tensor(YL[:, m, :], pb[TBANK[H2 + m]], prm("mnorm", m),
                                            YH[:, m, :].bitcast(F32), ALU.mult, ALU.subtract).then_inc(s_y2l, 1)

            for n in range(NT * H2 + 1):
                if n and n % 3 == 0 and n <= 3 * H2:
                    gate_read(n // 3 - 1)
                if n < NT * H2:
                    exponents(n)
                if n:
                    weighted(n - 1)
                    if n % NT == 0:
                        state_out(n // NT - 1)
                    if n % NT == 1 and n > 1:
                        state_sum(n // NT - 1)
                if n == 3 * H2 + 1:
                    yb_gated(range(0, 3))
                if n == 3 * H2 + 2:
                    yb_gated(range(3, 4))
                    dve.wait_ge(s_gn, 2)
                    link(V_.reciprocal(MSS[:, 0:3 * NT], MSS[:, 0:3 * NT]))
                    for h in range(3):
                        gated(h)
                if n == 3 * H2 + 3:
                    low_turned(range(0, 3))
            state_sum(H2 - 1)
            V_.memset(PAD[:, 1, 0:1], 0.0)
            dve.wait_ge(s_gn, 3)
            link(V_.reciprocal(MSS[:, 3 * NT:], MSS[:, 3 * NT:]))
            gated(3)
            low_turned(range(3, 4))
            for m in range(DK):
                add_square("post", m // 2, 2, m % 2)

            norm_reciprocal("post")
            for m in range(DK):
                dve.wait_ge(s_mn, m + 1)
                V_.tensor_tensor(X[:, m, :], X[:, m, :], MIX[:, m, :], ALU.add).then_inc(s_x["ffn2"].sem, 1)
                if m:
                    low("ffn2", "fpre2", (m - 1) // 2, 2, (m - 1) % 2, AH, AL)
                    add_square("ffn2", (m - 1) // 2, 2, (m - 1) % 2)
            add_square("ffn2", 3, 2, 1)
            low("ffn2", "fpre2", 3, 2, 1, AH, AL)
            ffn("ffn2", "ffn2", "down2")
            norm_reciprocal("fpost")
            dve.wait_ge(s_mix2, DK)
            for m in range(DK):
                if m < OWN:
                    link(V_.tensor_tensor(MIX2[:, m, :], MIX2[:, m, :], RS[:], ALU.mult))
                else:
                    dve.wait_ge(s_mn, DK + m - OWN + 1)
                V_.tensor_tensor(X[:, m, :], X[:, m, :], MIX2[:, m, :], ALU.add).then_inc(s_x["fpost"].sem, 1)


def _masks(np):
    r = np.arange(P)
    consts = np.zeros((P, 3, P), np.float32)
    consts[:, 0] = np.eye(P)
    consts[:, 1] = 1.0 / D
    consts[:, 2] = r[:, None] // HD == r[None] // HD
    dist = r[:, None] - np.arange(T)[None] + (T - P)
    seen = ((dist <= 128).astype(int) + (dist % 4 == 0) + (dist % 16 == 0)) * (dist >= 0)
    log = np.where(seen > 0, np.log(np.maximum(seen, 1)), -1e30)
    slopes = 2.0 ** -(8.0 * np.arange(1, H1 + 1) / H1)
    bias = (log[:, None] - slopes[None, :, None] * np.maximum(dist, 0)[:, None]).astype(np.float32)
    masks = np.zeros((P, 8, P), np.float32)
    for l, b in enumerate(SMALL):
        masks[:, l] = r[:, None] // (2 * b) == r[None] // (2 * b)
    masks[:, 7] = np.eye(P)
    sel = np.zeros((P, 8, P), np.float32)
    for i in range(8):
        sel[i, i] = -1.0
    neg = np.zeros((P, 2, P), np.float32)
    neg[:, 0] = np.where(r[:, None] <= r[None], 0.0, -1e30)
    neg[:, 1] = np.where(r[:, None] >= r[None], 0.0, -1e30)
    return consts, bias, masks.reshape(P, 8 * P), sel.reshape(P, 8 * P), neg


def _column_units(np, w):
    k, c = w.shape
    return w.reshape(k // P, P, c // P, P).transpose(2, 1, 0, 3).reshape(c // P, P, k)


def _row_units(np, w):
    return w.reshape(4, 2, P, T).transpose(0, 2, 1, 3).reshape(4, P, 2 * T)


def _down_units(np, w):
    k, c = w.shape
    v = w.reshape(k // P, P, c // P, P).transpose(2, 1, 0, 3)
    out = np.zeros((c // P * NS, P, UW), w.dtype)
    a = 0
    for q, n in enumerate(DOWN_TILES):
        out[q::NS, :, 0:n * P] = v[:, :, a:a + n].reshape(c // P, P, n * P)
        a += n
    return out


def _layout(np, a):
    g = lambda n: a[n][0]
    w_in, w2 = g("w_in"), g("w_in_2")
    cb, cc, cx, wq, wk, wv = np.split(w_in, 6, axis=1)
    conv = np.stack([_column_units(np, x) for x in (cc, cx, cb)], axis=1).reshape(12, P, UW)
    gate_up = lambda x, y: np.stack([_column_units(np, x), _column_units(np, y)], axis=1).reshape(2 * FC, P, UW)
    proj = _column_units(np, g("w_ple_proj")).reshape(2, 4, P, 2 * P).transpose(0, 2, 1, 3).reshape(2, P, UW)
    o = np.cumsum([0, 512, 512, 512, 16, 256, 256, 512, 512, 32])
    aqk, av, ao, ag, bq, bk, bv, br, blr = (w2[:, o[i]:o[i + 1]] for i in range(9))
    small = np.zeros((D, P), w2.dtype)
    small[:, 0:4], small[:, 4:8] = ag[:, 0:4], ag[:, 8:12]
    small[:, 32:36], small[:, 36:40] = ag[:, 4:8], ag[:, 12:16]
    small[:, 64:96] = blr
    ubk, ubq, ubv = _column_units(np, bk), _column_units(np, bq), _row_units(np, bv)
    w = np.concatenate([
        _column_units(np, wq), _column_units(np, wk), _row_units(np, wv), conv, _column_units(np, g("w_out")),
        gate_up(g("w_gate"), g("w_up")), _down_units(np, g("w_down")), proj, _column_units(np, g("w_ple_gate")),
        ubv[0:2], _column_units(np, small), ubv[2:4], ubk[0:1], ubq[0:1], _row_units(np, ao), ubk[1:2], ubq[1:2],
        _column_units(np, aqk), _row_units(np, av), _column_units(np, br), _column_units(np, g("w_out_2")),
        gate_up(g("ffn_w_gate_2"), g("ffn_w_up_2")), _down_units(np, g("ffn_w_down_2"))], axis=0)
    gw = np.zeros((32, H2, 2, HD), w2.dtype)
    for d in range(2):
        gw[16 * d:16 * d + 16, :, d] = g("gla_w2_2")[d].reshape(16, H2, HD)

    prm = np.zeros((P, NPRM), np.float32)

    def put(name, v, rows=slice(0, P)):
        prm[rows, PCOLS[name]:PCOLS[name] + v.shape[1]] = v

    cols = lambda v: v.reshape(-1, P).T
    taps = lambda v: np.concatenate([cols(x) for x in v], axis=1)
    put("eps", np.repeat(np.array([[EPS, HD * EPS, 1.0, 0.0]], np.float32), P, axis=0))
    for name, src in (("g_mix", "g_mix"), ("g_ffn", "g_ffn"), ("g_ple", "g_ple"), ("pre2", "norm_mix_pre_2"),
                      ("post2", "norm_mix_post_2"), ("fpre2", "norm_ffn_pre_2"), ("fpost2", "norm_ffn_post_2"),
                      ("g_oc", "g_out_conv"), ("g_oa", "g_out_attn"), ("cb", "conv_b"), ("mcb", "mlstm_conv_b_2"),
                      ("fcb", "ffn_conv_b"), ("fcb2", "ffn_conv_b_2"), ("mnorm", "mlstm_norm_2"),
                      ("gnorm", "gla_norm_2")):
        put(name, cols(g(src).reshape(-1)))
    for name, src in (("cw", "conv_w"), ("mcw", "mlstm_conv_w_2"), ("fcw", "ffn_conv_w"), ("fcw2", "ffn_conv_w_2")):
        put(name, taps(g(src)))
    put("qg", np.tile(g("q_norm_g"), 2)[:, None])
    put("kg", np.tile(g("k_norm_g"), 2)[:, None])
    put("glab", g("gla_b_2").reshape(2, H2, HD).transpose(0, 2, 1).reshape(P, H2))
    gb = g("mlstm_gate_b_2")
    put("gib", np.concatenate([gb[0:4], gb[8:12]])[:, None], slice(0, 8))
    put("gfb", np.concatenate([gb[4:8], gb[12:16]])[:, None], slice(32, 40))
    return w, gw.reshape(32, H2 * P), prm


def kernel(**inputs):
    import numpy as np
    import concourse.bacc as bacc
    from concourse.bass_utils import run_bass_kernel_spmd

    a = {k: np.asarray(v) for k, v in inputs.items()}
    w, gw, prm = _layout(np, a)
    consts, bias, masks, sel, neg = _masks(np)
    tiles = lambda v: np.ascontiguousarray(v.T.reshape(-1, P, T).transpose(1, 0, 2))
    arrays = {"x": tiles(a["x"][0]), "p": tiles(a["p"][0, 0]), "w": w, "gla_w": gw, "params": prm,
              "consts": consts, "bias": bias, "masks": masks, "selectors": sel, "negmask": neg}
    arrays = {k: np.ascontiguousarray(v) for k, v in arrays.items()}
    nc = bacc.Bacc("TRN2", target_bir_lowering=False, num_devices=1)
    dram = {k: nc.dram_tensor(f"in_{k}", v.shape, F32, kind="ExternalInput").ap() for k, v in arrays.items()}
    out = nc.dram_tensor("out", (P, DK, T), F32, kind="ExternalOutput").ap()
    build(nc, dram, out)
    r = run_bass_kernel_spmd(nc, [{f"in_{k}": v for k, v in arrays.items()}], core_ids=[0])
    y = r.results[0]["out"]
    return y.transpose(1, 0, 2).reshape(D, T).T.reshape(1, T, D)
```
